# Optimizing a Trainium2 kernel written in Bass

```python
import math
import jax, jax.numpy as jnp
from jax import lax
import numpy as np

D_MODEL = 1024
BATCH = 1
SEQ = 2048
DEPTH = 1

D_MIX = D_MODEL
POOL_WINDOWS = (2, 4, 8, 16)
N_POOL_GROUPS = len(POOL_WINDOWS)
POOL_WIDTH = D_MIX // 4
POOL_GROUP = POOL_WIDTH // N_POOL_GROUPS
DIFF_WIDTH = D_MIX // 2
DIFF_HEAD_DIM = 64
DIFF_HEADS = DIFF_WIDTH // (2 * DIFF_HEAD_DIM)
SB_WIDTH = D_MIX - POOL_WIDTH - DIFF_WIDTH
SB_HEAD_DIM = 64
SB_HEADS = SB_WIDTH // SB_HEAD_DIM
D_IN = POOL_WIDTH + 3 * DIFF_WIDTH + 3 * SB_WIDTH
D_FF = -(-(8 * D_MODEL) // (3 * 256)) * 256
Q_BLOCK = 128
EPS = 1e-6


def rmsnorm(x, g):
    x32 = x.astype(jnp.float32)
    y = x32 * lax.rsqrt(jnp.mean(x32 * x32, axis=-1, keepdims=True) + EPS)
    return y.astype(x.dtype) * g

def pool_mixer(u, pool_w, pool_scale):
    B_, S, _ = u.shape
    ug = u.reshape(B_, S, N_POOL_GROUPS, POOL_GROUP)
    cs = jnp.cumsum(ug.astype(jnp.float32), axis=1)
    cs = jnp.concatenate([jnp.zeros_like(cs[:, :1]), cs], axis=1)
    t = jnp.arange(S)[:, None]
    w = jnp.array(POOL_WINDOWS, dtype=jnp.int32)[None, :]
    lo = jnp.maximum(t + 1 - w, 0)
    cnt = jnp.minimum(t + 1, w).astype(jnp.float32)[..., None]
    gidx = jnp.arange(N_POOL_GROUPS)[None, :]
    win_sum = cs[:, 1:] - cs[:, lo, gidx]
    pooled = (win_sum / cnt - ug.astype(jnp.float32)).astype(u.dtype)
    mixed = jnp.einsum('bsgc,gcd->bsgd', pooled, pool_w)
    return mixed.reshape(B_, S, POOL_WIDTH) * pool_scale

def diff_attention(q, k, v, lam, lam_init, g):
    B_, S = q.shape[0], q.shape[1]
    scale = DIFF_HEAD_DIM ** -0.5
    outs = []
    for start in range(0, S, Q_BLOCK):
        end = start + Q_BLOCK
        qb, kb, vb = q[:, start:end], k[:, :end], v[:, :end]
        s = jnp.einsum('bqhrd,bkhrd->bhrqk', qb, kb).astype(jnp.float32) * scale
        mask = jnp.arange(end)[None, :] <= (start + jnp.arange(Q_BLOCK))[:, None]
        p = jax.nn.softmax(jnp.where(mask, s, -jnp.inf), axis=-1)
        attn = p[:, :, 0] - lam * p[:, :, 1]
        outs.append(jnp.einsum('bhqk,bkhe->bqhe', attn.astype(vb.dtype), vb))
    o = jnp.concatenate(outs, axis=1)
    o = rmsnorm(o, g) * (1.0 - lam_init)
    return o.reshape(B_, S, DIFF_WIDTH)

def stick_breaking_attention(q, k, v, g):
    B_, S = q.shape[0], q.shape[1]
    scale = SB_HEAD_DIM ** -0.5
    outs = []
    for start in range(0, S, Q_BLOCK):
        end = start + Q_BLOCK
        qb, kb, vb = q[:, start:end], k[:, :end], v[:, :end]
        z = jnp.einsum('bqhd,bkhd->bhqk', qb, kb).astype(jnp.float32) * scale
        mask = jnp.arange(end)[None, :] < (start + jnp.arange(Q_BLOCK))[:, None]
        log_1mb = jnp.where(mask, jax.nn.log_sigmoid(-z), 0.0)
        suffix = lax.cumsum(log_1mb, axis=3, reverse=True) - log_1mb
        a = jnp.where(mask, jnp.exp(jax.nn.log_sigmoid(z) + suffix), 0.0)
        outs.append(jnp.einsum('bhqk,bkhd->bqhd', a.astype(vb.dtype), vb))
    o = jnp.concatenate(outs, axis=1)
    return rmsnorm(o, g).reshape(B_, S, SB_WIDTH)

def first_inputs(seed: int = 0) -> dict:
    key = jax.random.key(seed)
    ks = jax.random.split(key, 18)
    f32 = jnp.float32
    nrm = lambda k, shape, s: (jax.random.normal(k, shape, f32) * s).astype(f32)
    return {
        "x": nrm(ks[0], (BATCH, SEQ, D_MODEL), 1.0),
        "norm1_g": 1.0 + nrm(ks[1], (DEPTH, D_MODEL), 0.02),
        "w_in": nrm(ks[2], (DEPTH, D_MODEL, D_IN), D_MODEL ** -0.5),
        "pool_w": nrm(ks[3], (DEPTH, N_POOL_GROUPS, POOL_GROUP, POOL_GROUP), POOL_GROUP ** -0.5),
        "pool_scale": 1.0 + nrm(ks[4], (DEPTH, POOL_WIDTH), 0.02),
        "lam_q1": nrm(ks[5], (DEPTH, DIFF_HEAD_DIM), 0.1),
        "lam_k1": nrm(ks[6], (DEPTH, DIFF_HEAD_DIM), 0.1),
        "lam_q2": nrm(ks[7], (DEPTH, DIFF_HEAD_DIM), 0.1),
        "lam_k2": nrm(ks[8], (DEPTH, DIFF_HEAD_DIM), 0.1),
        "diff_norm_g": 1.0 + nrm(ks[9], (DEPTH, 2 * DIFF_HEAD_DIM), 0.02),
        "sb_norm_g": 1.0 + nrm(ks[10], (DEPTH, SB_HEAD_DIM), 0.02),
        "w_out": nrm(ks[11], (DEPTH, D_MIX, D_MODEL), D_MIX ** -0.5),
        "norm2_g": 1.0 + nrm(ks[12], (DEPTH, D_MODEL), 0.02),
        "w_gate": nrm(ks[13], (DEPTH, D_MODEL, D_FF), D_MODEL ** -0.5),
        "w_up": nrm(ks[14], (DEPTH, D_MODEL, D_FF), D_MODEL ** -0.5),
        "w_down": nrm(ks[15], (DEPTH, D_FF, D_MODEL), D_FF ** -0.5),
        "final_norm_g": 1.0 + nrm(ks[16], (D_MODEL,), 0.02),
    }

def first_block(x, norm1_g, w_in, pool_w, pool_scale, lam_q1, lam_k1, lam_q2, lam_k2,
              diff_norm_g, sb_norm_g, w_out, norm2_g, w_gate, w_up, w_down, final_norm_g):
    B_, S, _ = x.shape
    c0 = POOL_WIDTH
    c1 = c0 + 3 * DIFF_WIDTH
    for l in range(DEPTH):
        h = rmsnorm(x, norm1_g[l])
        p = jnp.einsum('bsd,de->bse', h, w_in[l])
        u = p[..., :c0]
        dq, dk, dv = jnp.split(p[..., c0:c1], 3, axis=-1)
        sq, sk, sv = jnp.split(p[..., c1:], 3, axis=-1)

        a_out = pool_mixer(u, pool_w[l], pool_scale[l])

        lam_init = 0.8 - 0.6 * math.exp(-0.3 * l)
        lam = (jnp.exp(jnp.sum(lam_q1[l] * lam_k1[l]).astype(jnp.float32))
               - jnp.exp(jnp.sum(lam_q2[l] * lam_k2[l]).astype(jnp.float32)) + lam_init)
        b_out = diff_attention(dq.reshape(B_, S, DIFF_HEADS, 2, DIFF_HEAD_DIM),
                               dk.reshape(B_, S, DIFF_HEADS, 2, DIFF_HEAD_DIM),
                               dv.reshape(B_, S, DIFF_HEADS, 2 * DIFF_HEAD_DIM),
                               lam, lam_init, diff_norm_g[l])

        c_out = stick_breaking_attention(sq.reshape(B_, S, SB_HEADS, SB_HEAD_DIM),
                                         sk.reshape(B_, S, SB_HEADS, SB_HEAD_DIM),
                                         sv.reshape(B_, S, SB_HEADS, SB_HEAD_DIM),
                                         sb_norm_g[l])

        mix = jnp.concatenate([a_out, b_out, c_out], axis=-1)
        x = x + jnp.einsum('bse,ed->bsd', mix, w_out[l])

        h2 = rmsnorm(x, norm2_g[l])
        gate = jnp.einsum('bsd,df->bsf', h2, w_gate[l])
        up = jnp.einsum('bsd,df->bsf', h2, w_up[l])
        x = x + jnp.einsum('bsf,fd->bsd', jax.nn.silu(gate) * up, w_down[l])
    return rmsnorm(x, final_norm_g)


_first_inputs = first_inputs


def first_inputs(seed=0):
    import zlib

    import numpy as np

    out = dict(_first_inputs(seed))
    spreads = {}
    factors = {'pool_scale': 8.0,
     'lam_q1': 8.0,
     'lam_k2': 3.182,
     'diff_norm_g': 5.44,
     'sb_norm_g': 6.239,
     'norm2_g': 4.877,
     'final_norm_g': 2.86}
    for name, (base, spread) in spreads.items():
        noise = np.random.default_rng([zlib.crc32(name.encode()), seed]).standard_normal(out[name].shape)
        drawn = base * np.exp(spread * noise) if base else spread * noise
        out[name] = __import__('jax').numpy.asarray(drawn.astype(out[name].dtype))
    for name, factor in factors.items():
        out[name] = (out[name] * factor).astype(out[name].dtype)
    return out


_narrow_inputs = first_inputs


def first_inputs(seed=0):
    out = dict(_narrow_inputs(seed))
    wider = {'pool_scale': 3.86,
     'lam_q1': 12.0,
     'diff_norm_g': 3.77,
     'sb_norm_g': 3.79,
     'final_norm_g': 3.22}
    for name, times in wider.items():
        mean = out[name].mean()
        out[name] = (mean + times * (out[name] - mean)).astype(out[name].dtype)
    return out


CHUNK = 128
MIX_WIDTH = D_MODEL
GMLP_WIDTH = MIX_WIDTH // 2
GMLP_GROUP_DIM = 128
N_GMLP_GROUPS = GMLP_WIDTH // GMLP_GROUP_DIM
RET_WIDTH = MIX_WIDTH - GMLP_WIDTH
RET_HEAD_DIM = 128
N_RET_HEADS = RET_WIDTH // RET_HEAD_DIM
ROPE_THETA = 10000.0
PROJ_SIZES = [GMLP_WIDTH, GMLP_WIDTH, GMLP_WIDTH, RET_WIDTH, RET_WIDTH, RET_WIDTH, RET_WIDTH]
PROJ_WIDTH = sum(PROJ_SIZES)
PROJ_SPLITS = [int(i) for i in np.cumsum(PROJ_SIZES)[:-1]]


def rmsnorm_2(x, g):
    xf = x.astype(jnp.float32)
    y = xf * lax.rsqrt(jnp.mean(xf * xf, axis=-1, keepdims=True) + EPS)
    return (y * g.astype(jnp.float32)).astype(x.dtype)

def group_layernorm(x, g):
    xf = x.astype(jnp.float32)
    mu = jnp.mean(xf, axis=-1, keepdims=True)
    var = jnp.mean(jnp.square(xf - mu), axis=-1, keepdims=True)
    return ((xf - mu) * lax.rsqrt(var + EPS) * g.astype(jnp.float32)).astype(x.dtype)

def rotary(x, positions):
    half = x.shape[-1] // 2
    inv_freq = 1.0 / (ROPE_THETA ** (jnp.arange(half, dtype=jnp.float32) / half))
    ang = positions.astype(jnp.float32)[..., None] * inv_freq
    cos = jnp.cos(ang)[:, :, None, :].astype(x.dtype)
    sin = jnp.sin(ang)[:, :, None, :].astype(x.dtype)
    x1, x2 = x[..., :half], x[..., half:]
    return jnp.concatenate([x1 * cos - x2 * sin, x2 * cos + x1 * sin], axis=-1)

def gmlp_branch(u, v, gate, ln_g, w_s, b_s):
    B, S, _ = u.shape
    nc = S // CHUNK
    v = v.reshape(B, nc, CHUNK, N_GMLP_GROUPS, GMLP_GROUP_DIM)
    v = group_layernorm(v, ln_g.reshape(N_GMLP_GROUPS, GMLP_GROUP_DIM))
    causal = jnp.tril(jnp.ones((CHUNK, CHUNK), dtype=w_s.dtype))
    ws = w_s * causal[None]
    mixed = jnp.einsum('gts,bnsgd->bntgd', ws, v) + b_s.T[None, None, :, :, None]
    out = u.reshape(B, nc, CHUNK, N_GMLP_GROUPS, GMLP_GROUP_DIM) * mixed
    return out.reshape(B, S, GMLP_WIDTH) * jax.nn.silu(gate)

def retention_branch(q, k, v, gate, positions, gn_g):
    B, S, _ = q.shape
    nc = S // CHUNK
    H, Dh = N_RET_HEADS, RET_HEAD_DIM
    q = rotary(q.reshape(B, S, H, Dh), positions)
    k = rotary(k.reshape(B, S, H, Dh), positions) * (Dh ** -0.5)
    v = v.reshape(B, S, H, Dh)
    q = q.reshape(B, nc, CHUNK, H, Dh)
    k = k.reshape(B, nc, CHUNK, H, Dh)
    v = v.reshape(B, nc, CHUNK, H, Dh)

    log_gamma = jnp.log(1.0 - 2.0 ** (-5.0 - jnp.arange(H, dtype=jnp.float32)))
    idx = jnp.arange(CHUNK, dtype=jnp.float32)
    diff = idx[:, None] - idx[None, :]
    decay_mask = jnp.where(diff[None] >= 0,
                           jnp.exp(jnp.maximum(diff, 0.0)[None] * log_gamma[:, None, None]),
                           0.0)

    scores = jnp.einsum('bnqhd,bnkhd->bnhqk', q, k) * decay_mask[None, None]
    intra = jnp.einsum('bnhqk,bnkhe->bnqhe', scores, v)

    k_decay = jnp.exp((CHUNK - 1.0 - idx)[:, None] * log_gamma[None, :])
    kv_chunk = jnp.einsum('bnkhd,bnkhe,kh->bnhde', k, v, k_decay)
    chunk_decay = jnp.exp(CHUNK * log_gamma)[None, :, None, None]

    def step(state, kv):
        return state * chunk_decay + kv, state

    init = jnp.zeros_like(kv_chunk[:, 0])
    _, states = lax.scan(step, init, jnp.moveaxis(kv_chunk, 1, 0))
    states = jnp.moveaxis(states, 0, 1)

    q_decay = jnp.exp((idx + 1.0)[:, None] * log_gamma[None, :])
    cross = jnp.einsum('bnqhd,bnhde,qh->bnqhe', q, states, q_decay)

    o = (intra + cross).reshape(B, S, H, Dh)
    o = group_layernorm(o, gn_g.reshape(H, Dh)).astype(gate.dtype)
    return o.reshape(B, S, RET_WIDTH) * jax.nn.silu(gate)

def hybrid_layer(x, c, positions, w_ada, b_ada, g_pre, w_in, gmlp_ln_g, gmlp_ws, gmlp_bs,
                 ret_gn_g, w_out, g_post):
    mod = jnp.einsum('bd,de->be', jax.nn.silu(c), w_ada) + b_ada
    shift, scale, gate = jnp.split(mod, 3, axis=-1)
    h = rmsnorm_2(x, g_pre) * (1.0 + scale[:, None, :]) + shift[:, None, :]
    proj = jnp.einsum('bsd,de->bse', h, w_in)
    gu, gv, gg, rq, rk, rv, rg = jnp.split(proj, PROJ_SPLITS, axis=-1)
    y_gmlp = gmlp_branch(gu, gv, gg, gmlp_ln_g, gmlp_ws, gmlp_bs)
    y_ret = retention_branch(rq, rk, rv, rg, positions, ret_gn_g)
    y = jnp.concatenate([y_gmlp, y_ret], axis=-1)
    y = rmsnorm_2(jnp.einsum('bsm,md->bsd', y, w_out), g_post)
    return x + gate[:, None, :] * y

def second_inputs(seed: int = 0) -> dict:
    key = jax.random.key(seed)
    ks = jax.random.split(key, 14)
    f32 = jnp.float32
    x = jax.random.normal(ks[0], (BATCH, SEQ, D_MODEL), f32)
    c = jax.random.normal(ks[1], (BATCH, D_MODEL), f32)
    positions = jnp.broadcast_to(jnp.arange(SEQ, dtype=jnp.int32)[None, :], (BATCH, SEQ))
    w_ada = jax.random.normal(ks[2], (DEPTH, D_MODEL, 3 * D_MODEL), f32) * (0.5 * D_MODEL ** -0.5)
    b_ada = jax.random.normal(ks[3], (DEPTH, 3 * D_MODEL), f32) * 0.02
    g_pre = 1.0 + 0.02 * jax.random.normal(ks[4], (DEPTH, D_MODEL), f32)
    w_in = jax.random.normal(ks[5], (DEPTH, D_MODEL, PROJ_WIDTH), f32) * (D_MODEL ** -0.5)
    gmlp_ln_g = 1.0 + 0.02 * jax.random.normal(ks[6], (DEPTH, GMLP_WIDTH), f32)
    gmlp_ws = jax.random.normal(ks[7], (DEPTH, N_GMLP_GROUPS, CHUNK, CHUNK), f32) * (CHUNK ** -0.5)
    gmlp_bs = 1.0 + 0.02 * jax.random.normal(ks[8], (DEPTH, N_GMLP_GROUPS, CHUNK), f32)
    ret_gn_g = 1.0 + 0.02 * jax.random.normal(ks[9], (DEPTH, RET_WIDTH), f32)
    w_out = jax.random.normal(ks[10], (DEPTH, MIX_WIDTH, D_MODEL), f32) * (MIX_WIDTH ** -0.5)
    g_post = 1.0 + 0.02 * jax.random.normal(ks[11], (DEPTH, D_MODEL), f32)
    return {"x": x, "c": c, "positions": positions, "w_ada": w_ada, "b_ada": b_ada,
            "g_pre": g_pre, "w_in": w_in, "gmlp_ln_g": gmlp_ln_g, "gmlp_ws": gmlp_ws,
            "gmlp_bs": gmlp_bs, "ret_gn_g": ret_gn_g, "w_out": w_out, "g_post": g_post}

def second_block(x, c, positions, w_ada, b_ada, g_pre, w_in, gmlp_ln_g, gmlp_ws, gmlp_bs,
              ret_gn_g, w_out, g_post):
    for layer in range(DEPTH):
        x = hybrid_layer(x, c, positions, w_ada[layer], b_ada[layer], g_pre[layer], w_in[layer],
                         gmlp_ln_g[layer], gmlp_ws[layer], gmlp_bs[layer], ret_gn_g[layer],
                         w_out[layer], g_post[layer])
    return x


_first_inputs_2 = second_inputs


def second_inputs(seed=0):
    import zlib

    import numpy as np

    out = dict(_first_inputs_2(seed))
    spreads = {}
    factors = {'g_pre': 5.906, 'gmlp_ln_g': 8.0, 'gmlp_bs': 8.0, 'ret_gn_g': 8.0, 'g_post': 8.0}
    for name, (base, spread) in spreads.items():
        noise = np.random.default_rng([zlib.crc32(name.encode()), seed]).standard_normal(out[name].shape)
        drawn = base * np.exp(spread * noise) if base else spread * noise
        out[name] = __import__('jax').numpy.asarray(drawn.astype(out[name].dtype))
    for name, factor in factors.items():
        out[name] = (out[name] * factor).astype(out[name].dtype)
    return out


_narrow_inputs_2 = second_inputs


def second_inputs(seed=0):

    out = dict(_narrow_inputs_2(seed))
    wider = {'gmlp_ln_g': 6.14, 'gmlp_bs': 4.86, 'ret_gn_g': 12.0, 'g_post': 3.34}
    for name, times in wider.items():
        mean = out[name].mean()
        out[name] = (mean + times * (out[name] - mean)).astype(out[name].dtype)
    return out


def setup_inputs(seed=0):
    out = dict(first_inputs(seed))
    for name, value in second_inputs(seed + 1).items():
        if name != "x":
            out[name + "_2"] = value
    return out


def reference(
    x, norm1_g, w_in, pool_w, pool_scale, lam_q1, lam_k1, lam_q2, lam_k2, diff_norm_g,
    sb_norm_g, w_out, norm2_g, w_gate, w_up, w_down, final_norm_g, c_2, positions_2, w_ada_2,
    b_ada_2, g_pre_2, w_in_2, gmlp_ln_g_2, gmlp_ws_2, gmlp_bs_2, ret_gn_g_2, w_out_2, g_post_2,
):
    x = first_block(
        x, norm1_g, w_in, pool_w, pool_scale, lam_q1, lam_k1, lam_q2, lam_k2, diff_norm_g,
        sb_norm_g, w_out, norm2_g, w_gate, w_up, w_down, final_norm_g,
    )
    return second_block(
        x, c_2, positions_2, w_ada_2, b_ada_2, g_pre_2, w_in_2, gmlp_ln_g_2, gmlp_ws_2,
        gmlp_bs_2, ret_gn_g_2, w_out_2, g_post_2,
    )


_drawn_inputs = setup_inputs


def setup_inputs(seed=0):
    import zlib

    import numpy as np

    out = dict(_drawn_inputs(seed))
    spreads = {}
    factors = {'lam_q1': 8.0, 'g_pre_2': 2.8, 'ret_gn_g_2': 2.67}
    for name, (base, spread) in spreads.items():
        noise = np.random.default_rng([zlib.crc32(name.encode()), seed]).standard_normal(out[name].shape)
        drawn = base * np.exp(spread * noise) if base else spread * noise
        out[name] = __import__('jax').numpy.asarray(drawn.astype(out[name].dtype))
    for name, factor in factors.items():
        out[name] = (out[name] * factor).astype(out[name].dtype)
    return out
```

```python
import math
from contextlib import ExitStack

import numpy as np

import concourse.bass as bass
from concourse import mybir

F32 = mybir.dt.float32
FR = mybir.dt.float32r
I32 = mybir.dt.int32
ACT = mybir.ActivationFunctionType
ALU = mybir.AluOpType
AX = mybir.AxisListType.X

S = 2048
HT = 1024
D = 1024
NKT = 8
EPS = 1e-6
BIGV = 3.0e38
NEGV = -1.0e30
C_IDENT, C_DMASK, C_SBMIN, C_SBMUL, C_CAUS = 0, 128, 256, 384, 512
C_RMASK, C_QDEC, C_KDEC, C_INVF, C_ICNT, C_IW = 640, 1152, 1664, 1668, 1732, 1764
C_END = 1766


def shape_constants():
    c = np.zeros((128, C_END), np.float32)
    i = np.arange(128)
    q, k = i[:, None], i[None, :]
    c[:, C_IDENT:C_IDENT + 128] = np.eye(128)
    c[:, C_DMASK:C_DMASK + 128] = np.where(k <= q, BIGV, NEGV)
    c[:, C_SBMIN:C_SBMIN + 128] = np.where(k < q, BIGV, NEGV)
    c[:, C_SBMUL:C_SBMUL + 128] = np.where(k < q, 1.0, 0.0)
    c[:, C_CAUS:C_CAUS + 128] = np.where(q <= k, 1.0, 0.0)
    for h in range(4):
        lg = math.log(1.0 - 2.0 ** (-5.0 - h))
        diff = k - q
        sc = 128.0 ** -0.5
        c[:, C_RMASK + 128 * h:C_RMASK + 128 * h + 128] = np.where(diff >= 0, np.exp(np.maximum(diff, 0) * lg), 0.0) * sc
        c[:, C_QDEC + 128 * h:C_QDEC + 128 * h + 128] = np.exp((k + 1.0) * lg)
        c[:, C_KDEC + h] = np.exp((127.0 - i) * lg) * sc
    e = (np.arange(64, dtype=np.float32) / np.float32(64)).astype(np.float32)
    c[:, C_INVF:C_INVF + 64] = (np.float32(1.0) / np.power(np.float32(10000.0), e).astype(np.float32))[None, :]
    for t in range(2):
        for part in range(2):
            w = (2, 4, 8, 16)[2 * t + part]
            rows = slice(64 * part, 64 * part + 64)
            c[rows, C_ICNT + 16 * t:C_ICNT + 16 * t + 16] = (1.0 / np.minimum(np.arange(16) + 1, w))[None, :]
            c[rows, C_IW + t] = 1.0 / w
    return c


def two_pi_parts():
    left, parts = 2 * math.pi, []
    for _ in range(3):
        e = math.floor(math.log2(left)) - 7
        p = math.floor(left / 2.0 ** e) * 2.0 ** e
        parts.append(p)
        left -= p
    return parts + [left]


class Slot:

    def __init__(self, ap):
        self.ap = ap
        self.free = []


class Ring:
    def __init__(self, slots):
        self.slots = slots
        self.n = 0

    def take(self):
        s = self.slots[self.n % len(self.slots)]
        self.n += 1
        return s


def build(nc, I, const, out, scr):
    queues = {k: [] for k in ("pe", "act", "dve", "pool", "sp")}
    count = {}

    with ExitStack() as ctx:
        def sem(name):
            s = ctx.enter_context(nc.semaphore(name))
            count[name] = 0
            return (name, s)

        esem = {k: sem("done_" + k) for k in ("pe", "act", "dve", "pool")}

        def op(e, f, *waits, inc=True):
            flat = []
            for w in waits:
                flat += w if isinstance(w, list) else [w]
            queues[e].append((flat, f, (esem[e][1], 1) if inc else None))
            if inc:
                count[esem[e][0]] += 1
                return (esem[e], count[esem[e][0]])
            return None

        def dma(e, s, o, i, *waits, slow=False):
            flat = []
            for w in waits:
                flat += w if isinstance(w, list) else [w]
            queues[e].append((flat, lambda g: g.dma_start(o, i, allow_slow_non_contiguous=slow), (s[1], 16)))
            count[s[0]] += 16
            return (s, count[s[0]])

        def sbt(name, n, dt=F32, stack=ctx):
            return stack.enter_context(nc.sbuf_tensor(name, [128, n], dt))

        BIG = sbt("BIG", 16384, FR)
        XH = sbt("XH", 8192)
        XS = sbt("XS", 8192)
        WF = sbt("WF", 8192, FR)
        RAW = sbt("RAW", 3072)
        EV = sbt("EV", 2048)
        CB = sbt("CB", 640)
        ST = sbt("ST", 512)
        GROW = sbt("GROW", 256)
        GPROW = sbt("GPROW", 1024)
        SM = sbt("SM", 512)
        with ExitStack() as lay:
            AT = sbt("AT", 4096, FR, lay)
        with ExitStack() as lay:
            R2 = sbt("R2", 4096, F32, lay)
        PS = [ctx.enter_context(nc.psum_tensor(f"PS{i}", [128, 512], F32)) for i in range(8)]
        bank = [Slot(p) for p in PS]

        def smc(a, n):
            return SM[:, a:a + n]
        G1C, G2C, GPC = smc(0, 8), smc(8, 8), smc(16, 8)
        SHC, SCC = smc(24, 8), smc(32, 8)
        PSC, DGC, SGC = smc(40, 2), smc(42, 1), smc(43, 1)
        BSC, CC = smc(44, 4), smc(48, 8)
        NLAM, LT = smc(56, 1), smc(57, 4)
        SS, RV, RT = smc(64, 16), smc(80, 16), smc(96, 16)
        RSTD = smc(112, 16)
        MX, NM, SUMS, SC2 = smc(128, 16), smc(144, 4), smc(160, 16), smc(176, 8)
        POSF, ONE = smc(192, 8), smc(200, 1)
        BN, MV = smc(208, 48), smc(256, 16)
        IWC = smc(272, 2)
        ICN = smc(280, 32)
        KDC = smc(312, 4)
        MODC = smc(320, 16)
        LAMV = smc(336, 128)
        LAMD = smc(464, 1)
        LAME = smc(468, 4)
        ident = CB[:, C_IDENT:C_IDENT + 128]
        dmask = CB[:, C_DMASK:C_DMASK + 128]
        sbmin = CB[:, C_SBMIN:C_SBMIN + 128]
        sbmul = CB[:, C_SBMUL:C_SBMUL + 128]
        caus = CB[:, C_CAUS:C_CAUS + 128]

        s_c = sem("s_const")
        s_raw = [sem(f"s_raw{i}") for i in range(3)]
        s_kv = [sem(f"s_kv{i}") for i in range(2)]
        s_q = [sem(f"s_q{i}") for i in range(2)]
        s_x = [sem(f"s_x{i}") for i in range(2)]
        s_y = sem("s_y")
        s_u = sem("s_u")
        s_m = sem("s_m")
        s_r2 = sem("s_r2")
        s_gw = [sem(f"s_gw{i}") for i in range(4)]
        s_gr = [sem(f"s_gr{i}") for i in range(2)]
        s_ada = [sem(f"s_ada{i}") for i in range(2)]
        s_ev = [sem(f"s_ev{i}") for i in range(4)]
        s_o = [sem(f"s_o{i}") for i in range(2)]
        s_us = sem("s_us")
        s_yu = [sem(f"s_yu{i}") for i in range(2)]
        s_out = sem("s_out")

        def col(v, k):
            return v.rearrange("(k p) -> p k", p=128)

        dma("sp", s_c, CB[:, :], const[:, 0:640])
        dma("sp", s_c, KDC, const[:, C_KDEC:C_KDEC + 4])
        dma("sp", s_c, ICN, const[:, C_ICNT:C_ICNT + 32])
        dma("sp", s_c, IWC, const[:, C_IW:C_IW + 2])
        dma("sp", s_c, G1C, col(I["norm1_g"][0, :], 8), slow=True)
        dma("sp", s_c, G2C, col(I["norm2_g"][0, :], 8), slow=True)
        dma("sp", s_c, GPC, col(I["g_pre_2"][0, :], 8), slow=True)
        dma("sp", s_c, SHC, col(I["b_ada_2"][0, 0:1024], 8), slow=True)
        dma("sp", s_c, SCC, col(I["b_ada_2"][0, 1024:2048], 8), slow=True)
        dma("sp", s_c, CC, col(I["c_2"][0, :], 8), slow=True)
        dma("sp", s_c, PSC, col(I["pool_scale"][0, :], 2), slow=True)
        dma("sp", s_c, DGC, col(I["diff_norm_g"][0, :], 1), slow=True)
        sg = I["sb_norm_g"].rearrange("a d -> d a")
        dma("sp", s_c, SGC[0:64, :], sg, slow=True)
        dma("sp", s_c, SGC[64:128, :], sg, slow=True)
        dma("sp", s_c, BSC, I["gmlp_bs_2"][0, :, :].rearrange("g t -> t g"), slow=True)
        for i, n in enumerate(("lam_q1", "lam_k1")):
            dma("sp", s_c, LAMV[:, 64 * i:64 * i + 64], I[n][0:1, :].broadcast_to([128, 64]))
        consts = (s_c, count["s_const"])

        t_one = op("dve", lambda e: e.memset(ONE, 1.0))
        t_l = op("dve", lambda e: e.tensor_tensor(LAMV[:, 0:64], LAMV[:, 0:64], LAMV[:, 64:128], ALU.mult), consts)
        t_l1 = op("dve", lambda e: e.reduce_sum(LAME[:, 0:1], LAMV[:, 0:64], AX), t_l)
        for i, n in enumerate(("lam_q2", "lam_k2")):
            t_lm = dma("sp", s_m, LAMV[:, 64 * i:64 * i + 64], I[n][0:1, :].broadcast_to([128, 64]), t_l1)
        t_l = op("dve", lambda e: e.tensor_tensor(LAMV[:, 0:64], LAMV[:, 0:64], LAMV[:, 64:128], ALU.mult), t_lm, t_l1)
        t_l2 = op("dve", lambda e: e.reduce_sum(LAME[:, 1:2], LAMV[:, 0:64], AX), t_l)
        t_e = op("act", lambda e: e.activation(LAME[:, 2:4], LAME[:, 0:2], ACT.Exp), t_l1, t_l2)
        t_d = op("dve", lambda e: e.tensor_tensor(LAMD, LAME[:, 3:4], LAME[:, 2:3], ALU.subtract), t_e)
        lam_init = 0.8 - 0.6 * math.exp(-0.3 * 0)
        t_nlam = op("dve", lambda e: e.tensor_scalar_add(NLAM, LAMD, -lam_init), t_d)
        t_dg = op("dve", lambda e: e.tensor_scalar_mul(DGC, DGC, 1.0 - lam_init), consts)

        raw = [Slot(RAW[:, 1024 * i:1024 * i + 1024]) for i in range(3)]
        wslot = [Slot((WF[:, 4096 * i:4096 * i + 2048], WF[:, 4096 * i + 2048:4096 * i + 4096])) for i in range(2)]
        wr = {"raw": 0, "slot": 0}

        def wprep(pieces):
            s = wslot[wr["slot"] % 2]
            wr["slot"] += 1
            hi, lo = s.ap
            toks = []
            for i in range(2):
                n = wr["raw"] % 3
                wr["raw"] += 1
                r = raw[n]
                for d, src in pieces(i, r.ap):
                    t_in = dma("sp", s_raw[n], d, src, r.free)
                h = hi[:, 1024 * i:1024 * i + 1024]
                l = lo[:, 1024 * i:1024 * i + 1024]
                t_hi = op("act", lambda e, h=h, r=r: e.activation(h, r.ap, ACT.Copy), t_in, s.free)
                t_lo = op("pool", lambda e, h=h, r=r, l=l: e.tensor_tensor(l, r.ap, h.bitcast(F32), ALU.subtract),
                          t_hi, t_in, s.free)
                r.free = [t_lo, t_hi]
                toks.append(t_lo)
            s.free = []
            return s, toks[1:] + [t_hi]

        def cols_of(W, segs):
            Wv = W.rearrange("(k p) n -> p k n", p=128)

            def pieces(i, r):
                rv = r.rearrange("p (k n) -> p k n", k=4)
                at, res = 0, []
                for c0, n in segs:
                    res.append((rv[:, :, at:at + n], Wv[:, 4 * i:4 * i + 4, c0:c0 + n]))
                    at += n
                return res
            return pieces

        def rows_of(W, r0):
            def pieces(i, r):
                return [(r, W[r0 + 128 * i:r0 + 128 * i + 128, :])]
            return pieces

        class Stream:
            def __init__(self, reqs):
                self.reqs = list(reqs)
                self.ready = []

            def ahead(self):
                if self.reqs and len(self.ready) < 2:
                    self.ready.append(wprep(self.reqs.pop(0)))

            def next(self):
                if not self.ready:
                    self.ahead()
                return self.ready.pop(0)

        bigh = BIG[:, 0:8192].rearrange("p (k t) -> p k t", k=8)
        bigl = BIG[:, 8192:16384].rearrange("p (k t) -> p k t", k=8)
        xh = XH[:, :].rearrange("p (t d) -> p t d", t=8)
        xs = XS[:, :].rearrange("p (t d) -> p t d", t=8)
        ev = [Slot(EV[:, 512 * i:512 * i + 512]) for i in range(4)]
        ring_ev = Ring(ev)
        pring = Ring(bank)

        def split_psum(b, t_mm, hi, lo, scale=None, bias=None, waits=[], w=512):
            v = ring_ev.take()
            src = b.ap[:, 0:w]
            tmp = v.ap[:, 0:w]
            if scale is None:
                t = op("dve", lambda e: e.tensor_copy(tmp, src), t_mm, v.free)
            elif bias is None:
                t = op("dve", lambda e: e.tensor_scalar(tmp, src, scale, None, ALU.mult), t_mm, v.free, waits)
            else:
                t = op("dve", lambda e: e.tensor_scalar(tmp, src, scale, bias, ALU.mult, ALU.add), t_mm, v.free, waits)
            b.free = [t]
            t_hi = op("act", lambda e: e.activation(hi, tmp, ACT.Copy), t, waits)
            t_lo = op("pool", lambda e: e.tensor_tensor(lo, tmp, hi.bitcast(F32), ALU.subtract), t_hi, waits)
            v.free = [t_hi, t_lo]
            return t_hi, t_lo

        def rstd_from(n, width, t_ss, src=SS, eps_scale=None):
            v, r, t, = RV[:, 0:n], RSTD[:, 0:n], RT[:, 0:n]
            a = op("dve", lambda e: e.tensor_scalar(v, src[:, 0:n] if src is SS else src, 1.0 / width, EPS, ALU.mult, ALU.add), t_ss)
            b = op("act", lambda e: e.activation(r, v, ACT.Ln), a)
            b = op("act", lambda e: e.activation(r, r, ACT.Exp, scale=-0.5), b)
            c = op("dve", lambda e: e.tensor_tensor(t, r, r, ALU.mult), b)
            c = op("dve", lambda e: e.tensor_tensor(t, t, v, ALU.mult), c)
            c = op("dve", lambda e: e.tensor_scalar(t, t, -0.5, 1.5, ALU.mult, ALU.add), c)
            return op("dve", lambda e: e.tensor_tensor(r, r, t, ALU.mult), c)

        st = {"big": [], "xs": [], "big_r": [], "rstd_r": []}

        def sumsq(src8, rdy):
            toks = []
            for t in range(8):
                toks.append(op("act", lambda e, t=t: e.activation(xs[:, t, :], src8[:, t, :], ACT.Square,
                                                                 accum_out=SS[:, t:t + 1]), rdy, st["xs"], st["rstd_r"]))
            return toks

        def transpose_in(src8, t_src, scale_col, bias_col=None, waits=[]):
            toks = []
            last_pe = None
            for j in range(2):
                for k in range(8):
                    b = pring.take()
                    for t in range(4):
                        last_pe = op("pe", lambda e, b=b, t=t, k=k, j=j: e.transpose(
                            b.ap[:, 128 * t:128 * t + 128], src8[:, 4 * j + t, 128 * k:128 * k + 128], ident),
                            t_src[4 * j + t], b.free, inc=t == 3)
                    hi = bigh[:, k, 512 * j:512 * j + 512]
                    lo = bigl[:, k, 512 * j:512 * j + 512]
                    toks += list(split_psum(b, last_pe, hi, lo, scale_col(k), bias_col and bias_col(k),
                                            waits=st["big_r"] + waits))
            st["big_r"] = []
            return toks[-2:], last_pe

        def norm_in(rdy, scale_col, bias_col=None, waits=[]):
            t_ss = sumsq(xh, rdy)
            t_r = rstd_from(8, 1024, t_ss)
            toks = []
            for t in range(8):
                toks.append(op("dve", lambda e, t=t: e.tensor_scalar(xs[:, t, :], xh[:, t, :], RSTD[:, t:t + 1], None,
                                                                      ALU.mult), t_r, t_ss, rdy))
            st["rstd_r"] = [toks[-1]]
            st["big"], t_pe = transpose_in(xs, toks, scale_col, bias_col, waits)
            st["xs"] = [t_pe]

        def three(e_list, o, Ah, Al, Bh, Bl, start, stop, waits, last):
            op("pe", lambda e: e.matmul(o, Ah, Bh, start=start, stop=False), waits, inc=False)
            op("pe", lambda e: e.matmul(o, Ah, Bl, start=False, stop=False), inc=False)
            return op("pe", lambda e: e.matmul(o, Al, Bh, start=False, stop=stop), inc=last)

        def gemm_f(slot, f, j, b, waits):
            wh = slot.ap[0].rearrange("p (k n) -> p k n", k=8)
            wl = slot.ap[1].rearrange("p (k n) -> p k n", k=8)
            for k in range(8):
                fs = slice(128 * f, 128 * f + 128)
                ts = slice(512 * j, 512 * j + 512)
                t = three(None, b.ap[:, :], wh[:, k, fs], wl[:, k, fs], bigh[:, k, ts], bigl[:, k, ts],
                          k == 0, k == 7, (waits + b.free) if k == 0 else [], k == 7)
            return t

        def gemm_t(slot, t, b, waits, n=256):
            wh = slot.ap[0].rearrange("p (k n) -> p k n", k=8)
            wl = slot.ap[1].rearrange("p (k n) -> p k n", k=8)
            ts = slice(128 * t, 128 * t + 128)
            for k in range(8):
                r = three(None, b.ap[:, 0:n], bigh[:, k, ts], bigl[:, k, ts], wh[:, k, 0:n], wl[:, k, 0:n],
                          k == 0, k == 7, (waits + b.free) if k == 0 else [], k == 7)
            return r

        QS, KS, VS, US, YS = scr["QS"], scr["KS"], scr["VS"], scr["US"], scr["YS"]
        w_in = I["w_in"][0, :, :]
        x_v = I["x"][0, :, :].rearrange("(t p) d -> p t d", p=128)
        o_v = out[0, :, :].rearrange("(t p) d -> p t d", p=128)
        ys_v = YS.rearrange("(t p) d -> p t d", p=128)
        t_xfree = []
        uhist = {"done": []}
        yst = {"r": []}
        state_tok = {}

        staged = Ring([Slot((AT[:, 1024 * i:1024 * i + 512], AT[:, 1024 * i + 512:1024 * i + 1024])) for i in range(4)])
        s_st = [sem(f"s_st{i}") for i in range(4)]

        def store_parts(n, s, t_hi, t_lo, dh, dl, view=lambda a: a):
            a = dma("sp", s_st[n], dh, view(s.ap[0]).bitcast(F32), t_hi)
            b = dma("sp", s_st[n], dl, view(s.ap[1]).bitcast(F32), t_lo)
            s.free = [b]
            return b

        at_free = {"t": []}

        def all_of(toks):
            best = {}
            for s, v in toks:
                if s[0] not in best or best[s[0]][1] < v:
                    best[s[0]] = (s, v)
            return list(best.values())

        for H in range(2):
            tok0 = H * HT
            for i in range(2):
                t_x = dma("sp", s_x[i], xh[:, 4 * i:4 * i + 4, :], x_v[:, 8 * H + 4 * i:8 * H + 4 * i + 4, :], t_xfree)
            rdy = [(s_x[0], count["s_x0"]), (s_x[1], count["s_x1"])]
            blocks = [("u", 0, 0)] + [("q", 256 + 256 * i, i) for i in range(2)] + [("k", 768 + 256 * i, i) for i in range(2)] \
                + [("v", 1280 + 256 * i, i) for i in range(2)] + [("q", 1792, 2), ("k", 2048, 2), ("v", 2304, 2)]
            ws = Stream([cols_of(w_in, [(c, 256)]) for _, c, _ in blocks])
            ws.ahead()
            norm_in(rdy, lambda k: G1C[:, k:k + 1], waits=[consts])
            for s in staged.slots:
                s.free = list(at_free["t"])
            stores = []
            for kind, c0, idx in blocks:
                slot, t_w = ws.next()
                ws.ahead()
                last = []
                if kind in "uqk":
                    for f in range(2):
                        for j in range(2):
                            b = pring.take()
                            t_mm = gemm_f(slot, f, j, b, t_w + st["big"])
                            last = [t_mm]
                            sl = slice(tok0 + 512 * j, tok0 + 512 * j + 512)
                            if kind == "u":
                                v = ring_ev.take()
                                n = ev.index(v)
                                t = op("dve", lambda e, v=v, b=b: e.tensor_copy(v.ap, b.ap[:, :]), t_mm, v.free)
                                b.free = [t]
                                v.free = [dma("sp", s_ev[n], US[f, :, 16 + sl.start:16 + sl.stop], v.ap, t)]
                                stores.append(v.free[0])
                            else:
                                n = staged.n % 4
                                s = staged.take()
                                ft = 2 * idx + f
                                t_hi, t_lo = split_psum(b, t_mm, s.ap[0], s.ap[1], 0.125 if kind == "q" else None,
                                                        waits=list(s.free))
                                Z = QS if kind == "q" else KS
                                stores.append(store_parts(n, s, t_hi, t_lo, Z[0, ft, :, sl], Z[1, ft, :, sl]))
                else:
                    for t2 in range(4):
                        b = pring.take()
                        n = staged.n % 4
                        s = staged.take()
                        for u in range(2):
                            wh = slot.ap[0].rearrange("p (k n) -> p k n", k=8)
                            wl = slot.ap[1].rearrange("p (k n) -> p k n", k=8)
                            ts = slice(128 * (2 * t2 + u), 128 * (2 * t2 + u) + 128)
                            for k in range(8):
                                t_mm = three(None, b.ap[:, 256 * u:256 * u + 256], bigh[:, k, ts], bigl[:, k, ts],
                                             wh[:, k, :], wl[:, k, :], k == 0, k == 7,
                                             (t_w + st["big"] + b.free) if k == 0 and u == 0 else [], k == 7 and u == 1)
                        last = [t_mm]
                        t_hi, t_lo = split_psum(b, t_mm, s.ap[0], s.ap[1], waits=list(s.free))
                        r0 = tok0 + 256 * t2
                        for f in range(2):
                            dst = [VS[p, 2 * idx + f, r0:r0 + 256, :].rearrange("(u p) e -> p u e", p=128) for p in range(2)]
                            view = lambda a, f=f: a.rearrange("p (u n) -> p u n", u=2)[:, :, 128 * f:128 * f + 128]
                            stores.append(store_parts(n, s, t_hi, t_lo, dst[0], dst[1], view))
                slot.free = last
            st["big_r"] = last
            stores = all_of(stores)
            if H == 0:
                zt = op("dve", lambda e: e.memset(EV[:, 0:16], 0.0), ev[0].free)
                for f in range(2):
                    zd = dma("sp", s_us, US[f, :, 0:16], EV[:, 0:16], zt)
                ev[0].free = [zd]
                uhist["done"] = [zd]

            nk0 = 8 * H
            kvs = [Slot(BIG[:, 8192 * i:8192 * i + 8192]) for i in range(2)]
            for s in kvs:
                s.free = list(st["big_r"])
            qsl = [Slot(AT[:, 2048 * i:2048 * i + 2048]) for i in range(2)]
            for s in qsl:
                s.free = list(stores)
            tr = Ring([Slot(WF[:, 1024 * i:1024 * i + 1024]) for i in range(8)])
            for s in tr.slots:
                s.free = list(st["big_r"])
            ob = [Slot(EV[:, 1024 * i:1024 * i + 1024]) for i in range(2)]
            ob[0].free = ev[0].free + ev[1].free
            ob[1].free = ev[2].free + ev[3].free
            sring = Ring(bank[0:4])
            tring = Ring(bank[4:6])
            oring = Ring(bank[6:8])
            L = tok0 + HT
            pa = [Slot(XS[:, 2048 * i:2048 * i + 2048]) for i in range(4)]
            for s in pa:
                s.free = list(st["xs"])
            ystores = []

            def load_head(j):
                kv, q = kvs[j % 2], qsl[j % 2]
                kk = kv.ap[:, 0:4096].rearrange("p (a t) -> p a t", a=2)
                vv = kv.ap[:, 4096:8192].rearrange("p (t a e) -> p t a e", a=2, e=128)
                qq = q.ap.rearrange("p (a t) -> p a t", a=2)
                for a in range(2):
                    t1 = dma("sp", s_q[j % 2], qq[:, a, :].bitcast(F32), QS[a, j, :, tok0:tok0 + HT], stores, q.free)
                    dma("sp", s_kv[j % 2], kk[:, a, 0:L].bitcast(F32), KS[a, j, :, 0:L], stores, kv.free)
                    t2 = dma("sp", s_kv[j % 2], vv[:, 0:L // 128, a, :].bitcast(F32),
                             VS[a, j, 0:L, :].rearrange("(t p) e -> p t e", p=128), stores, kv.free)
                kv.free, q.free = [], []
                return qq, kk, vv, [t1, t2], kv, q

            def qk(hd, r, qt, c, w):
                qq, kk, vv, t_ld, _, _ = hd
                b = sring.take()
                rs = slice(64 * r, 64 * r + 64)
                qs = slice(128 * qt, 128 * qt + 128)
                ks = slice(512 * c, 512 * c + w)
                t = three(None, b.ap[:, 0:w], qq[rs, 0, qs], qq[rs, 1, qs], kk[rs, 0, ks], kk[rs, 1, ks],
                          True, True, t_ld + b.free, True)
                return b, t

            def turn(src, w, t_src):
                b, s = tring.take(), tr.take()
                for i in range(w // 128):
                    t = op("pe", lambda e, i=i: e.transpose(b.ap[:, 128 * i:128 * i + 128],
                                                            src[:, 128 * i:128 * i + 128], ident),
                           t_src, b.free, inc=i == w // 128 - 1)
                hi, lo = s.ap[:, 0:w], s.ap[:, 512:512 + w]
                t_hi = op("act", lambda e: e.activation(hi, b.ap[:, 0:w], ACT.Copy), t, s.free)
                t_lo = op("dve", lambda e: e.tensor_tensor(lo, b.ap[:, 0:w], hi.bitcast(F32), ALU.subtract), t_hi, s.free)
                b.free = [t_lo]
                s.free = []
                return s, t_lo, t

            def pv(hd, s, t_s, c, w, o, e0, en, first, last):
                vv = hd[2]
                for i in range(w // 128):
                    kt = 4 * c + i
                    hi, lo = s.ap[:, 128 * i:128 * i + 128], s.ap[:, 512 + 128 * i:512 + 128 * i + 128]
                    fst, lst = first and i == 0, last and i == w // 128 - 1
                    op("pe", lambda e, hi=hi, kt=kt, fst=fst: e.matmul(o.ap[:, 0:2 * en], hi, vv[:, kt, :, e0:e0 + en],
                                                                      start=fst, stop=False, skip_group_check=True),
                       t_s, o.free if fst else [], inc=False)
                    t = op("pe", lambda e, lo=lo, kt=kt, lst=lst: e.matmul(o.ap[:, 0:en], lo, vv[:, kt, 0, e0:e0 + en],
                                                                          start=False, stop=lst, skip_group_check=True),
                           inc=i == w // 128 - 1)
                s.free = [t]
                return t

            def chunks(n):
                return [(c, min(512, 128 * n - 512 * c)) for c in range((n + 3) // 4)]

            heads = {0: load_head(0)}

            def finish_tile(j, O, t_o):
                o = O.ap.rearrange("p (t e) -> p t e", t=8)
                parts = 1 if j < 4 else 2
                en = 128 // parts
                tq = []
                for t in range(8):
                    for r in range(parts):
                        a = op("act", lambda e, t=t, r=r: e.activation(LAMV[:, 0:en], o[:, t, en * r:en * r + en], ACT.Square,
                                                                      accum_out=SS[:, parts * t + r:parts * t + r + 1]),
                               t_o, st["rstd_r"], tq[-1:])
                        tq.append(a)
                t_r = rstd_from(8 * parts, en, tq)
                ts = []
                for t in range(8):
                    for r in range(parts):
                        ts.append(op("dve", lambda e, t=t, r=r: e.tensor_scalar(
                            o[:, t, en * r:en * r + en], o[:, t, en * r:en * r + en],
                            RSTD[:, parts * t + r:parts * t + r + 1], None, ALU.mult), t_r, t_o))
                st["rstd_r"] = [ts[-1]]
                c0 = 256 + 128 * j
                d = dma("pool", s_o[j % 2], ys_v[:, 8 * H:8 * H + 8, c0:c0 + 128], o, ts[-1], yst["r"])
                O.free = [d]
                ystores.append(d)

            prev = None

            def diff_scores(it, r):
                hd, qt, n, p, m = it["hd"], it["qt"], it["n"], it["p"][r], it["m"]
                bs = []
                for c, w in chunks(n):
                    b, t = qk(hd, r, qt, c, w)
                    if c == (n - 1) // 4:
                        dg = b.ap[:, w - 128:w]
                        t = op("dve", lambda e, dg=dg: e.tensor_tensor(dg, dg, dmask, ALU.min), t)
                    t = op("dve", lambda e, b=b, w=w, c=c: e.reduce_max(MX[:, 8 * m + 4 * r + c:8 * m + 4 * r + c + 1], b.ap[:, 0:w], AX),
                           t, it["mfree"])
                    bs.append((c, w, b, t))
                k = len(bs)
                t_nm = op("dve", lambda e: e.tensor_reduce(NM[:, 2 * m + r:2 * m + r + 1], MX[:, 8 * m + 4 * r:8 * m + 4 * r + k],
                                                           AX, ALU.max, negate=True), t, it["mfree"])
                for c, w, b, t in bs:
                    tt = op("act", lambda e, b=b, w=w, c=c: e.activation(
                        p.ap[:, 512 * c:512 * c + w], b.ap[:, 0:w], ACT.Exp, bias=NM[:, 2 * m + r:2 * m + r + 1],
                        accum_out=SUMS[:, 8 * m + 4 * r + c:8 * m + 4 * r + c + 1]), t_nm, p.free, it["mfree"])
                    b.free = [tt]
                p.free = []
                it["t"][r] = tt
                it["nm"] = tt
                it["k"] = k

            def diff_out(it):
                m, k, n, hd = it["m"], it["k"], it["n"], it["hd"]
                p1, p2 = it["p"]
                sc = SC2[:, 4 * m:4 * m + 4]
                sums = SUMS[:, 8 * m:8 * m + 8].rearrange("p (r c) -> p r c", r=2)
                a = op("dve", lambda e: e.reduce_sum(sc[:, 0:2], sums[:, :, 0:k], AX), it["t"][0], it["t"][1])
                a = op("dve", lambda e: e.reciprocal(sc[:, 2:4], sc[:, 0:2]), a)
                a = op("dve", lambda e: e.tensor_scalar(sc[:, 1:2], sc[:, 3:4], sc[:, 0:1], NLAM, ALU.mult, ALU.mult), a, t_nlam)
                full = 128 * n
                a = op("dve", lambda e: e.scalar_tensor_tensor(p1.ap[:, 0:full], p2.ap[:, 0:full], sc[:, 1:2], p1.ap[:, 0:full],
                                                               ALU.mult, ALU.add), a)
                p2.free = [a]
                o = oring.take()
                pend = None
                cs = chunks(n)
                for i, (c, w) in enumerate(cs + [(None, None)]):
                    cur = None
                    if c is not None:
                        s, t_s, t_pe = turn(p1.ap[:, 512 * c:512 * c + w], w, [a])
                        cur = (s, t_s, c, w)
                        p1.free = [t_pe]
                    if pend is not None:
                        s0, ts0, c0, w0 = pend
                        t_pv = pv(hd, s0, [ts0], c0, w0, o, 0, 128, c0 == 0, c0 == len(cs) - 1)
                    pend = cur
                dst = it["O"].ap[:, 128 * it["qt"]:128 * it["qt"] + 128]
                x = op("dve", lambda e: e.tensor_scalar(dst, o.ap[:, 0:128], sc[:, 2:3], None, ALU.mult), t_pv, it["O"].free)
                x = op("dve", lambda e: e.scalar_tensor_tensor(dst, o.ap[:, 128:256], sc[:, 2:3], dst, ALU.mult, ALU.add), x)
                o.free = [x]
                it["done"] = x
                hd[4].free, hd[5].free = [t_pv], [t_pv]

            items = []
            for j in range(4):
                for qt in range(8):
                    items.append((j, qt))
            mfree = {0: [], 1: []}
            its = []
            for i, (j, qt) in enumerate(items + [(None, None)]):
                it = None
                if j is not None:
                    if qt == 0:
                        if j not in heads:
                            heads[j] = load_head(j)
                    if qt == 2 and j + 1 < 6:
                        heads[j + 1] = load_head(j + 1)
                    it = {"hd": heads[j], "qt": qt, "n": nk0 + qt + 1, "m": i % 2, "p": (pa[2 * (i % 2)], pa[2 * (i % 2) + 1]),
                          "t": {}, "O": ob[j % 2], "mfree": mfree[i % 2], "j": j}
                    diff_scores(it, 0)
                if prev is not None:
                    diff_out(prev)
                    mfree[prev["m"]] = [prev["done"]]
                    if prev["qt"] == 7:
                        finish_tile(prev["j"], prev["O"], prev["done"])
                if it is not None:
                    diff_scores(it, 1)
                prev = it

            aslot = Ring([Slot(XS[:, 512 * i:512 * i + 512]) for i in range(8)])
            cslot = Ring([Slot(XS[:, 4096 + 512 * i:4096 + 512 * i + 512]) for i in range(6)])
            for i, s in enumerate(aslot.slots):
                s.free = pa[i // 4].free
            for i, s in enumerate(cslot.slots):
                s.free = pa[2 + i // 4].free
            work = []
            for j in (4, 5):
                for qt in range(8):
                    for r in range(2):
                        cs = chunks(nk0 + qt + 1)[::-1]
                        g = {"j": j, "r": r, "qt": qt, "carry": None}
                        for i, (c, w) in enumerate(cs):
                            work.append({"g": g, "c": c, "w": w, "first": i == 0, "last": i == len(cs) - 1})

            def sb_a(x):
                g = x["g"]
                if g["j"] not in heads:
                    heads[g["j"]] = load_head(g["j"])
                if g["j"] == 4 and g["qt"] == 2 and 5 not in heads:
                    heads[5] = load_head(5)
                x["b"], t = qk(heads[g["j"]], g["r"], g["qt"], x["c"], x["w"])
                x["a"] = aslot.take()
                b, a, w = x["b"], x["a"].ap[:, 0:x["w"]], x["w"]
                t = op("act", lambda e: e.activation(a, b.ap[:, 0:w], ACT.Abs), t, x["a"].free)
                t = op("act", lambda e: e.activation(a, a, ACT.Exp, scale=-1.0), t)
                x["t"] = op("act", lambda e: e.activation(a, a, ACT.Ln, bias=1.0), t)

            def sb_b(x):
                g, b, a, w = x["g"], x["b"], x["a"].ap[:, 0:x["w"]], x["w"]
                x["cs"] = cslot.take()
                cc = x["cs"].ap[:, 0:w]
                t = op("dve", lambda e: e.scalar_tensor_tensor(a, b.ap[:, 0:w], 0.0, a, ALU.max, ALU.add), x["t"])
                if x["first"]:
                    t = op("dve", lambda e: e.tensor_tensor(a[:, w - 128:w], a[:, w - 128:w], sbmul, ALU.mult), t)
                init = 0.0 if g["carry"] is None else g["carry"][0]
                wt = [] if g["carry"] is None else [g["carry"][1]]
                t = op("dve", lambda e: e.tensor_tensor_scan(cc[:, ::-1], ONE.broadcast_to([128, w]), a[:, ::-1], init,
                                                             ALU.mult, ALU.add), t, wt, x["cs"].free, t_one)
                g["carry"] = (cc[:, 0:1], t)
                t = op("dve", lambda e: e.tensor_tensor(a, b.ap[:, 0:w], cc, ALU.subtract), t)
                b.free = [t]
                x["cs"].free = [t]
                if x["first"]:
                    t = op("dve", lambda e: e.tensor_tensor(a[:, w - 128:w], a[:, w - 128:w], sbmin, ALU.min), t)
                x["t"] = t

            def sb_c(x):
                a = x["a"].ap[:, 0:x["w"]]
                t = op("act", lambda e: e.activation(a, a, ACT.Exp), x["t"])
                x["s"], x["ts"], t_pe = turn(a, x["w"], [t])
                x["a"].free = [t_pe]

            def sb_d(x):
                g = x["g"]
                if x["first"]:
                    g["o"] = oring.take()
                o = g["o"]
                t = pv(heads[g["j"]], x["s"], [x["ts"]], x["c"], x["w"], o, 64 * g["r"], 64, x["first"], x["last"])
                heads[g["j"]][4].free = [t]
                heads[g["j"]][5].free = [t]
                if x["last"]:
                    O = ob[g["j"] % 2]
                    dst = O.ap[:, 128 * g["qt"] + 64 * g["r"]:128 * g["qt"] + 64 * g["r"] + 64]
                    y = op("dve", lambda e: e.tensor_copy(dst, o.ap[:, 0:64]), t, O.free)
                    y = op("dve", lambda e: e.tensor_tensor(dst, o.ap[:, 64:128], dst, ALU.add), y)
                    o.free = [y]
                    if g["qt"] == 7 and g["r"] == 1:
                        finish_tile(g["j"], O, y)

            nwork = len(work)
            for i in range(nwork + 3):
                if i < nwork:
                    sb_a(work[i])
                if 0 <= i - 1 < nwork:
                    sb_b(work[i - 1])
                if 0 <= i - 3 < nwork:
                    sb_d(work[i - 3])
                if 0 <= i - 2 < nwork:
                    sb_c(work[i - 2])

            att_pe = [(esem["pe"], count["done_pe"])]
            st["xs"] = att_pe + all_of([t for s in aslot.slots + cslot.slots for t in s.free])
            st["big_r"] = list(att_pe)
            for s in wslot:
                s.free = list(att_pe)
            ev_free = ob[0].free + ob[1].free
            for v in ev:
                v.free = list(ev_free)
            pring = Ring(bank)

            ws = Stream([cols_of(I["w_out"][0, :, :], [(256 * i, 256)]) for i in range(4)])
            ws.ahead()
            pw = XS[:, 8192 - 256:8192]
            t_z = op("dve", lambda e: e.memset(pw, 0.0), st["xs"])
            for f in range(2):
                for g in range(2):
                    t_pw = dma("sp", s_u, pw[64 * g:64 * g + 64, 128 * f + 64 * g:128 * f + 64 * g + 64],
                               I["pool_w"][0, 2 * f + g, :, :], t_z, st["xs"])
            NU = 1040
            t_us = []
            ua, ub = XS[:, 0:NU], XS[:, NU:2 * NU]
            pooled = [XS[:, 2 * NU:2 * NU + 1024], XS[:, 2 * NU + 1024:2 * NU + 2048]]
            free_u = list(st["xs"])
            mixed = []
            for f in range(2):
                t_in = dma("sp", s_u, ua, US[f, :, tok0:tok0 + NU], stores, uhist["done"], free_u, [t_pw])
                lo_w, hi_w = ((2, 4), (8, 16))[f]
                cur, nxt, sh, t = ua, ub, 1, t_in
                pl = pooled[f]
                orig_free = t_in

                bufs = [XS[:, 4 * NU:5 * NU], XS[:, 5 * NU:6 * NU]]
                src = ua
                steps = 0
                w = 1
                t_seg = {}
                while w < hi_w:
                    dst = bufs[steps % 2]
                    w0 = w
                    s0 = 2 * w - 1
                    t = op("dve", lambda e, dst=dst, src=src, w0=w0, s0=s0: e.tensor_tensor(
                        dst[:, s0:NU], src[:, s0:NU], src[:, s0 - w0:NU - w0], ALU.add), t, t_in, free_u)
                    w *= 2
                    steps += 1
                    src = dst
                    if w == lo_w:
                        t = op("dve", lambda e, dst=dst, pl=pl: e.tensor_copy(pl[0:64, :], dst[0:64, 16:NU]), t, free_u)
                    if w == hi_w:
                        t = op("dve", lambda e, dst=dst, pl=pl: e.tensor_copy(pl[64:128, :], dst[64:128, 16:NU]), t, free_u)
                if H == 0:
                    t = op("dve", lambda e, pl=pl, f=f: e.tensor_tensor(pl[:, 0:16], pl[:, 0:16], ICN[:, 16 * f:16 * f + 16], ALU.mult), t)
                    t = op("dve", lambda e, pl=pl, f=f: e.tensor_scalar(pl[:, 16:1024], pl[:, 16:1024], IWC[:, f:f + 1], None, ALU.mult), t)
                else:
                    t = op("dve", lambda e, pl=pl, f=f: e.tensor_scalar(pl, pl, IWC[:, f:f + 1], None, ALU.mult), t)
                t = op("dve", lambda e, pl=pl: e.tensor_tensor(pl, pl, ua[:, 16:NU], ALU.subtract), t)
                free_u = [t]
                for j in range(2):
                    b = pring.take()
                    t_mm = op("pe", lambda e, b=b, j=j, f=f, pl=pl: e.matmul(b.ap[:, :], pw[:, 128 * f:128 * f + 128],
                                                                      pl[:, 512 * j:512 * j + 512], start=True, stop=True),
                              t, t_pw, b.free)
                    mixed += list(split_psum(b, t_mm, bigh[:, f, 512 * j:512 * j + 512], bigl[:, f, 512 * j:512 * j + 512],
                                             PSC[:, f:f + 1], waits=st["big_r"]))
            st["xs"] = [t_mm] + free_u
            t_y = []
            for i in range(2):
                t_y.append(dma("sp", s_y, xs[:, 4 * i:4 * i + 4, 256:1024], ys_v[:, 8 * H + 4 * i:8 * H + 4 * i + 4, 256:1024],
                               ystores, st["xs"]))
            yst["r"] = [t_y[1]]
            for j in range(2):
                for k in range(2, 8):
                    b = pring.take()
                    for t in range(4):
                        t_pe = op("pe", lambda e, b=b, t=t, k=k, j=j: e.transpose(
                            b.ap[:, 128 * t:128 * t + 128], xs[:, 4 * j + t, 128 * k:128 * k + 128], ident),
                            t_y[1], b.free, inc=t == 3)
                    mixed += list(split_psum(b, t_pe, bigh[:, k, 512 * j:512 * j + 512], bigl[:, k, 512 * j:512 * j + 512],
                                             DGC if k < 6 else SGC, waits=st["big_r"] + [t_dg]))
            st["xs"] = [t_pe]
            st["big"] = all_of(mixed)

            def residual_gemm(ws, nblk, res):
                for i in range(nblk):
                    slot, t_w = ws.next()
                    ws.ahead()
                    for t in range(8):
                        b = pring.take()
                        t_mm = gemm_t(slot, t, b, t_w + st["big"])
                        res.append(sink(i, t, b, t_mm))
                    slot.free = [t_mm]
                return t_mm

            def sink(i, t, b, t_mm):
                dst = xh[:, t, 256 * i:256 * i + 256]
                x = op("dve", lambda e: e.tensor_tensor(dst, b.ap[:, 0:256], dst, ALU.add), t_mm)
                b.free = [x]
                return x
            res = []
            st["big_r"] = [residual_gemm(ws, 4, res)]
            wg, wu, wd = I["w_gate"][0, :, :], I["w_up"][0, :, :], I["w_down"][0, :, :]
            NG = 11
            order = [("g", 0), ("u", 0)]
            for g in range(1, NG):
                order += [("g", g), ("d", g - 1), ("u", g)]
            order.append(("d", NG - 1))
            reqs = []
            for kind, g in order:
                reqs.append(rows_of(wd, 256 * g) if kind == "d" else cols_of(wg if kind == "g" else wu, [(256 * g, 256)]))
            ws = Stream(reqs)
            ws.ahead()
            norm_in(res[-1:], lambda k: G2C[:, k:k + 1])
            at = AT[:, :].rearrange("p (a f t) -> p a f t", a=2, f=2)
            at_r = all_of(stores + [(esem["pe"], count["done_pe"])])
            sgs = [Slot(XS[:, 512 * i:512 * i + 512]) for i in range(4)]
            for s in sgs:
                s.free = list(st["xs"])
            ACC = XS[:, 2048:5120]
            ada = [Slot(XS[:, 5120:6144]), Slot(XS[:, 6144:7168])]
            t_acc = None
            ada_free = list(st["xs"])
            if H == 0:
                t_sc = op("act", lambda e: e.activation(CC, CC, ACT.Silu), consts)
                for s in ada:
                    s.free = list(st["xs"])
            acc_t = [None] * 3
            na = 0
            for kind, g in order:
                slot, t_w = ws.next()
                ws.ahead()
                if kind in "gu":
                    for f in range(2):
                        for j in range(2):
                            b = pring.take()
                            t_mm = gemm_f(slot, f, j, b, t_w + st["big"])
                            s = sgs[2 * f + j]
                            if kind == "g":
                                s.t = op("act", lambda e, s=s, b=b: e.activation(s.ap, b.ap[:, :], ACT.Silu), t_mm, s.free)
                                b.free = [s.t]
                            else:
                                x = op("dve", lambda e, s=s, b=b: e.tensor_tensor(s.ap, b.ap[:, :], s.ap, ALU.mult), t_mm, s.t)
                                b.free = [x]
                                hi, lo = at[:, 0, f, 512 * j:512 * j + 512], at[:, 1, f, 512 * j:512 * j + 512]
                                t_hi = op("act", lambda e, s=s, hi=hi: e.activation(hi, s.ap, ACT.Copy), x, at_r)
                                t_lo = op("pool", lambda e, s=s, hi=hi, lo=lo: e.tensor_tensor(lo, s.ap, hi.bitcast(F32), ALU.subtract),
                                          t_hi, x, at_r)
                                s.free = [t_hi, t_lo]
                                t_at = [t_hi, t_lo]
                    if H == 0 and kind == "g" and g < 8:
                        for n in range(3):
                            a = ada[na % 2]
                            t_a = dma("sp", s_ada[na % 2], a.ap, I["w_ada_2"][0, 128 * g:128 * g + 128, 1024 * n:1024 * n + 1024], a.free)
                            na += 1
                            acc = ACC[:, 1024 * n:1024 * n + 1024]
                            if g == 0:
                                acc_t[n] = op("dve", lambda e, a=a, acc=acc: e.tensor_scalar(acc, a.ap, CC[:, 0:1], None, ALU.mult),
                                              t_a, t_sc, ada_free)
                            else:
                                acc_t[n] = op("dve", lambda e, a=a, acc=acc, g=g: e.scalar_tensor_tensor(
                                    acc, a.ap, CC[:, g:g + 1], acc, ALU.mult, ALU.add), t_a, acc_t[n])
                            a.free = [acc_t[n]]
                else:
                    dh = slot.ap[0].rearrange("p (f n) -> p f n", f=2)
                    dl = slot.ap[1].rearrange("p (f n) -> p f n", f=2)
                    for t in range(8):
                        for n in range(2):
                            b = pring.take()
                            ts, ns = slice(128 * t, 128 * t + 128), slice(512 * n, 512 * n + 512)
                            for f in range(2):
                                t_mm = three(None, b.ap[:, :], at[:, 0, f, ts], at[:, 1, f, ts], dh[:, f, ns], dl[:, f, ns],
                                             f == 0, f == 1, (t_w + t_at + b.free) if f == 0 else [], f == 1)
                            dst = xh[:, t, ns]
                            x = op("dve", lambda e, b=b, dst=dst: e.tensor_tensor(dst, b.ap[:, :], dst, ALU.add), t_mm,
                                   *( [] if g else [st["xs"]]))
                            b.free = [x]
                    at_r = [t_mm]
                slot.free = [t_mm]
            st["big_r"] = [t_mm]
            t_res = x
            t_gate_end = [t_mm]
            if H == 0:
                b = pring.take()
                for k in range(16):
                    t_m = op("pe", lambda e, k=k, b=b: e.matmul(b.ap[:, k:k + 1], ACC[:, 128 * k:128 * k + 128], ONE,
                                                               start=True, stop=True, skip_group_check=True), acc_t, t_one, b.free, inc=k == 15)
                x = op("dve", lambda e, b=b: e.tensor_copy(MODC, b.ap[:, 0:16]), t_m)
                b.free = [x]
                x1 = op("dve", lambda e: e.tensor_tensor(SHC, SHC, MODC[:, 0:8], ALU.add), x, consts)
                x2 = op("dve", lambda e: e.tensor_tensor(SCC, SCC, MODC[:, 8:16], ALU.add), x)
                x2 = op("dve", lambda e: e.tensor_scalar_add(SCC, SCC, 1.0), x2)
                t_mod = op("dve", lambda e: e.tensor_tensor(GPC, GPC, SCC, ALU.mult), x2, x1)
                rb = XS[:, 5120:6144]
                rg = XS[:, 6144:7168]
                t_rb = dma("sp", s_ada[0], rb, I["b_ada_2"][0:1, 2048:3072].broadcast_to([128, 1024]), ada[0].free)
                t_rg = dma("sp", s_ada[1], rg, I["g_post_2"][0:1, :].broadcast_to([128, 1024]), ada[1].free)
                ONEM = XS[:, 7168:7296]
                t_om = op("dve", lambda e: e.memset(ONEM, 1.0), ada_free)
                for n in range(2):
                    b = pring.take()
                    ns = slice(512 * n, 512 * n + 512)
                    t_m = op("pe", lambda e, n=n, b=b: e.matmul(b.ap[:, :], ONEM, ACC[:, 2048 + 512 * n:2560 + 512 * n],
                                                               start=True, stop=True), acc_t, t_om, b.free)
                    x = op("dve", lambda e, b=b, ns=ns: e.tensor_tensor(GPROW[:, ns], b.ap[:, :], rb[:, ns], ALU.add), t_m, t_rb)
                    b.free = [x]
                    t_gp = op("dve", lambda e, ns=ns: e.tensor_tensor(GPROW[:, ns], GPROW[:, ns], rg[:, ns], ALU.mult), x, t_rg)
                st["xs"] = [t_gp, t_m]
            st["xs"] = st["xs"] + all_of([t for s in sgs for t in s.free])

            t_ss = sumsq(xh, [t_res])
            t_r = rstd_from(8, 1024, t_ss)
            gf = XS[:, 0:1024]
            t_gf = dma("sp", s_m, gf, I["final_norm_g"].rearrange("(a d) -> a d", a=1).broadcast_to([128, 1024]), t_ss)
            for t in range(8):
                x = op("dve", lambda e, t=t: e.scalar_tensor_tensor(xh[:, t, :], xh[:, t, :], RSTD[:, t:t + 1], gf, ALU.mult, ALU.mult),
                       t_r, t_gf, t_ss)
            st["rstd_r"] = [x]
            st["xs"] = [x]
            wi = I["w_in_2"][0, :, :]
            units = []
            for p in range(2):
                a, c = 2 * p, 2 * p + 1
                units.append(("g", p, [cols_of(wi, [(128 * a, 128), (512 + 128 * a, 128)]),
                                       cols_of(wi, [(128 * c, 128), (512 + 128 * c, 128)]),
                                       cols_of(wi, [(1024 + 256 * p, 256)])]))
            for h in range(4):
                o = 1536 + 128 * h
                units.append(("r", h, [cols_of(wi, [(o, 128), (o + 512, 128)]), cols_of(wi, [(o + 1024, 128), (o + 1536, 128)])]))
            units = [units[0], units[2], units[1], units[3], units[4], units[5]]
            ws = Stream([r for u in units for r in u[2]])
            ws.ahead()
            norm_in([x], lambda k: GPC[:, k:k + 1], lambda k: SHC[:, k:k + 1], waits=[t_mod])

            r2w = all_of(at_r + [(esem["pe"], count["done_pe"])])
            cos = R2[:, 0:512].rearrange("p (t i) -> p t i", t=8)
            sin = R2[:, 512:1024].rearrange("p (t i) -> p t i", t=8)
            rmk = R2[:, 1024:1536]
            qdc = R2[:, 1536:2048]
            tmpa = R2[:, 2048:2560]
            tmpb = R2[:, 2560:3072]
            YB = R2[:, 3072:4096]
            t_r2 = dma("sp", s_r2, rmk, const[:, C_RMASK:C_RMASK + 512], r2w)
            t_r2 = dma("sp", s_r2, qdc, const[:, C_QDEC:C_QDEC + 512], r2w)
            invf = tmpb[:, 0:64]
            t_r2 = dma("sp", s_r2, invf, const[:, C_INVF:C_INVF + 64], r2w)
            posi = tmpb[:, 64:72].bitcast(I32)
            t_r2 = dma("sp", s_r2, posi, I["positions_2"][0, tok0:tok0 + HT].rearrange("(t p) -> p t", p=128), r2w, slow=True)
            x = op("dve", lambda e: e.tensor_copy(POSF, posi), t_r2)
            for t in range(8):
                x = op("dve", lambda e, t=t: e.tensor_scalar(cos[:, t, :], invf, POSF[:, t:t + 1], None, ALU.mult), x, r2w)
            cf, sf = R2[:, 0:512], R2[:, 512:1024]
            magic = 12582912.0
            x = op("dve", lambda e: e.tensor_scalar(sf, cf, 1.0 / (2 * math.pi), magic, ALU.mult, ALU.add), x)
            x = op("dve", lambda e: e.tensor_scalar_add(sf, sf, -magic), x)
            for part in two_pi_parts():
                x = op("dve", lambda e, part=part: e.scalar_tensor_tensor(cf, sf, -part, cf, ALU.mult, ALU.add), x)
            lim = float(np.nextafter(np.float32(math.pi), np.float32(0)))
            x = op("dve", lambda e: e.tensor_scalar(cf, cf, lim, -lim, ALU.min, ALU.max), x)
            y = op("act", lambda e: e.activation(sf, cf, ACT.Sin), x)
            y = op("act", lambda e: e.activation(cf, cf, ACT.Sin, scale=0.5), y)
            y = op("dve", lambda e: e.tensor_tensor(cf, cf, cf, ALU.mult), y)
            t_cs = op("dve", lambda e: e.tensor_scalar(cf, cf, -2.0, 1.0, ALU.mult, ALU.add), y)

            pb = Ring([Slot(XS[:, 2048 * i:2048 * i + 2048]) for i in range(4)])
            for s in pb.slots:
                s.free = list(st["xs"])
            small = Ring([Slot(EV[:, 128 * i:128 * i + 128]) for i in range(16)])
            evf = all_of([t for v in ev for t in v.free])
            for s in small.slots:
                s.free = list(evf)
            pring = Ring(bank[0:4])
            mring = Ring(bank[4:8])
            yb = Slot(YB)
            yb.free = list(r2w)
            ystores = []
            grs = [Slot(GROW[:, 128 * i:128 * i + 128]) for i in range(2)]
            t_tmp = [t_cs]
            nun = 0

            def store_y(c0, t_y):
                d = dma("pool", s_yu[0], ys_v[:, 8 * H:8 * H + 8, c0:c0 + 128], yb.ap.rearrange("p (t e) -> p t e", t=8), t_y, yst["r"])
                yb.free = [d]
                ystores.append(d)

            def layer_norm8(src, t_src, en=128):
                ts = []
                for c in range(8):
                    y = op("dve", lambda e, c=c: e.bn_stats(BN[:, 6 * c:6 * c + 6], src(c)), t_src, st["rstd_r"])
                    ts.append(y)
                for c in range(8):
                    y = op("dve", lambda e, c=c: e.bn_aggr(MV[:, 2 * c:2 * c + 2], BN[:, 6 * c:6 * c + 6]), ts[c], st["rstd_r"])
                mv = MV.rearrange("p (c a) -> p c a", a=2)
                return rstd_from(8, 1.0, [y], src=mv[:, :, 1])

            def load_row(src, n):
                g = grs[n % 2]
                t = dma("sp", s_gr[n % 2], g.ap, src.broadcast_to([128, 128]), g.free)
                return g, t

            def gmlp_steps(p, bufs, toks, n0):
                steps = []
                Gb = bufs[2].ap.rearrange("p (t n) -> p t n", t=8)
                for gi in range(2):
                    g = 2 * p + gi
                    B = bufs[gi].ap.rearrange("p (t n) -> p t n", t=8)
                    loc = {}

                    def s_norm(g=g, B=B, loc=loc, n=n0 + gi, gi=gi):
                        wt = small.take()
                        t_w = dma("sp", s_gw[g], wt.ap, I["gmlp_ws_2"][0, g, :, :], wt.free)
                        wt2 = small.take()
                        b = mring.take()
                        t = op("pe", lambda e: e.transpose(b.ap[:, 0:128], wt.ap, ident), t_w, b.free)
                        t = op("dve", lambda e: e.tensor_tensor(wt2.ap, b.ap[:, 0:128], caus, ALU.mult), t, wt2.free)
                        b.free = [t]
                        wt.free = [t]
                        loc["w"], loc["tw"] = wt2, t
                        row, t_row = load_row(I["gmlp_ln_g_2"][0:1, 128 * g:128 * g + 128], n)
                        t_r = layer_norm8(lambda c: B[:, c, 128:256], toks[gi] + toks[2])
                        for c in range(8):
                            t = op("dve", lambda e, c=c: e.tensor_scalar(B[:, c, 128:256], B[:, c, 128:256], MV[:, 2 * c:2 * c + 1],
                                                                          RSTD[:, c:c + 1], ALU.subtract, ALU.mult), t_r)
                            t = op("dve", lambda e, c=c: e.tensor_tensor(B[:, c, 128:256], B[:, c, 128:256], row.ap, ALU.mult), t, t_row)
                        row.free = [t]
                        st["rstd_r"] = [t]
                        loc["v"] = t
                        gs = Gb[:, :, 128 * gi:128 * gi + 128]
                        loc["g"] = op("act", lambda e: e.activation(gs, gs, ACT.Silu), toks[2])

                    def s_mix(q, g=g, B=B, loc=loc, gi=gi):
                        b = mring.take()
                        w = loc["w"]
                        t = op("pe", lambda e: e.matmul(b.ap[:, :].rearrange("p (t n) -> p t n", t=4), w.ap,
                                                        B[:, 4 * q:4 * q + 4, 128:256], start=True, stop=True),
                               loc["tw"], loc["v"], b.free)
                        us = B[:, 4 * q:4 * q + 4, 0:128]
                        t = op("dve", lambda e: e.scalar_tensor_tensor(us, b.ap[:, :].rearrange("p (t n) -> p t n", t=4),
                                                                       BSC[:, g:g + 1], us, ALU.add, ALU.mult), t)
                        b.free = [t]
                        dst = yb.ap.rearrange("p (t e) -> p t e", t=8)[:, 4 * q:4 * q + 4, :]
                        loc["y"] = op("dve", lambda e: e.tensor_tensor(dst, us, Gb[:, 4 * q:4 * q + 4, 128 * gi:128 * gi + 128],
                                                                       ALU.mult), t, loc["g"], yb.free)
                        if q == 1:
                            loc["w"].free = [loc["y"]]
                            store_y(128 * g, loc["y"])
                            bufs[gi].free = [loc["y"]]
                            if gi == 1:
                                bufs[2].free = [loc["y"]]
                    steps += [s_norm, lambda f=s_mix: f(0), lambda f=s_mix: f(1)]
                return steps

            def ret_steps(h, bufs, toks, n0):
                A = bufs[0].ap.rearrange("p (t n) -> p t n", t=8)
                B = bufs[1].ap.rearrange("p (t n) -> p t n", t=8)
                ta = tmpa.rearrange("p (t i) -> p t i", t=8)
                tb = tmpb.rearrange("p (t i) -> p t i", t=8)
                loc = {}
                cd = (1.0 - 2.0 ** (-5.0 - h)) ** 128
                S_ = ST[:, 128 * h:128 * h + 128]
                ctx_ = [dict() for _ in range(8)]

                def rot():
                    for half in range(2):
                        x1 = A[:, :, 128 * half:128 * half + 64]
                        x2 = A[:, :, 128 * half + 64:128 * half + 128]
                        t1 = op("dve", lambda e, x1=x1: e.tensor_tensor(ta, x1, sin, ALU.mult), toks[0] + t_tmp)
                        t2 = op("dve", lambda e, x2=x2: e.tensor_tensor(tb, x2, sin, ALU.mult), t_tmp)
                        t3 = op("dve", lambda e, x1=x1: e.tensor_tensor(x1, x1, cos, ALU.mult), t1)
                        t4 = op("dve", lambda e, x2=x2: e.tensor_tensor(x2, x2, cos, ALU.mult), t2)
                        t5 = op("dve", lambda e, x1=x1: e.tensor_tensor(x1, x1, tb, ALU.subtract), t3)
                        t6 = op("dve", lambda e, x2=x2: e.tensor_tensor(x2, x2, ta, ALU.add), t4)
                        t_tmp[:] = [t6]
                        loc[half] = [t5, t6]
                    loc["rot"] = [t6]
                    if H == 0:
                        state_tok[h] = [op("dve", lambda e: e.memset(S_, 0.0))]
                    loc["g"] = op("act", lambda e: e.activation(B[:, :, 128:256], B[:, :, 128:256], ACT.Silu), toks[1])

                def s_a(c):
                    x = ctx_[c]
                    b = mring.take()
                    op("pe", lambda e: e.transpose(b.ap[:, 0:128], A[:, c, 0:128], ident), loc["rot"], b.free, inc=False)
                    t = op("pe", lambda e: e.transpose(b.ap[:, 128:256], A[:, c, 128:256], ident))
                    x["qT"], x["kT"], x["qd"], x["kd"] = [small.take() for _ in range(4)]
                    t1 = op("act", lambda e: e.activation(x["qT"].ap, b.ap[:, 0:128], ACT.Copy), t, x["qT"].free)
                    t2 = op("act", lambda e: e.activation(x["kT"].ap, b.ap[:, 128:256], ACT.Copy), t1, x["kT"].free)
                    t3 = op("pool", lambda e: e.tensor_tensor(x["qd"].ap, x["qT"].ap, qdc[:, 128 * h:128 * h + 128], ALU.mult),
                            t1, x["qd"].free, t_r2)
                    t4 = op("pool", lambda e: e.tensor_scalar(x["kd"].ap, A[:, c, 128:256], KDC[:, h:h + 1], None, ALU.mult),
                            loc["rot"], x["kd"].free, consts)
                    b.free = [t2]
                    x["ta"] = [t2, t4]

                def s_b(c):
                    x = ctx_[c]
                    b = mring.take()
                    op("pe", lambda e: e.matmul(b.ap[:, 0:128], x["kT"].ap, x["qT"].ap, start=True, stop=True), x["ta"], b.free, inc=False)
                    t = op("pe", lambda e: e.matmul(b.ap[:, 128:256], x["kd"].ap, B[:, c, 0:128], start=True, stop=True), toks[1])
                    x["kT"].free = [t]
                    x["kd"].free = [t]
                    x["sm"] = small.take()
                    x["tb"] = op("dve", lambda e: e.tensor_tensor(x["sm"].ap, b.ap[:, 0:128], rmk[:, 128 * h:128 * h + 128], ALU.mult),
                                 t, x["sm"].free, t_r2)
                    x["bank"] = b

                def s_c(c):
                    x = ctx_[c]
                    b = mring.take()
                    op("pe", lambda e: e.matmul(b.ap[:, 0:128], x["sm"].ap, B[:, c, 0:128], start=True, stop=False), x["tb"], b.free, inc=False)
                    t = op("pe", lambda e: e.matmul(b.ap[:, 0:128], x["qd"].ap, S_, start=False, stop=True), state_tok[h])
                    x["sm"].free = [t]
                    x["qd"].free = [t]
                    x["qT"].free = [t]
                    kvb = x["bank"]
                    t2 = op("dve", lambda e: e.scalar_tensor_tensor(S_, S_, cd, kvb.ap[:, 128:256], ALU.mult, ALU.add), t, x["tb"])
                    kvb.free = [t2]
                    state_tok[h] = [t2]
                    t3 = op("dve", lambda e: e.tensor_copy(A[:, c, 0:128], b.ap[:, 0:128]), t)
                    b.free = [t3]
                    loc["o"] = t3

                def fin():
                    row, t_row = load_row(I["ret_gn_g_2"][0:1, 128 * h:128 * h + 128], n0)
                    t_r = layer_norm8(lambda c: A[:, c, 0:128], [loc["o"]])
                    y8 = yb.ap.rearrange("p (t e) -> p t e", t=8)
                    for c in range(8):
                        t = op("dve", lambda e, c=c: e.tensor_scalar(A[:, c, 0:128], A[:, c, 0:128], MV[:, 2 * c:2 * c + 1],
                                                                      RSTD[:, c:c + 1], ALU.subtract, ALU.mult), t_r)
                        t = op("dve", lambda e, c=c: e.tensor_tensor(A[:, c, 0:128], A[:, c, 0:128], row.ap, ALU.mult), t, t_row)
                    row.free = [t]
                    st["rstd_r"] = [t]
                    t = op("dve", lambda e: e.tensor_tensor(y8, A[:, :, 0:128], B[:, :, 128:256], ALU.mult), t, loc["g"], yb.free)
                    store_y(512 + 128 * h, t)
                    bufs[0].free = [t]
                    bufs[1].free = [t]

                steps = [rot]
                for i in range(10):
                    def one(i=i):
                        if i < 8:
                            s_a(i)
                        if 0 <= i - 1 < 8:
                            s_b(i - 1)
                        if 0 <= i - 2 < 8:
                            s_c(i - 2)
                    steps.append(one)
                return steps + [fin]

            pending = []
            for kind, idx, req in units:
                bufs, toks = [], []
                total = 8 * len(req)
                done = 0
                nsteps = len(pending)
                for _ in req:
                    slot, t_w = ws.next()
                    ws.ahead()
                    buf = None
                    for t in range(8):
                        b = pring.take()
                        t_mm = gemm_t(slot, t, b, t_w + st["big"])
                        if buf is None:
                            buf = pb.take()
                            while not isinstance(buf.free, list):
                                pending.pop(0)()
                        dst = buf.ap.rearrange("p (t n) -> p t n", t=8)[:, t, :]
                        x = op("act", lambda e, b=b, dst=dst: e.activation(dst, b.ap[:, 0:256], ACT.Copy), t_mm, buf.free)
                        b.free = [x]
                        done += 1
                        want = nsteps * done // total
                        while nsteps - len(pending) < want:
                            pending.pop(0)()
                    slot.free = [t_mm]
                    buf.free = None
                    bufs.append(buf)
                    toks.append([x])
                while pending:
                    pending.pop(0)()
                pending = gmlp_steps(idx, bufs, toks, nun) if kind == "g" else ret_steps(idx, bufs, toks, nun)
                nun += 2 if kind == "g" else 1
            ws = Stream([cols_of(I["w_out_2"][0, :, :], [(256 * i, 256)]) for i in range(4)])
            ws.ahead()
            while pending:
                pending.pop(0)()
            st["big_r"] = [t_mm]
            st["xs"] = all_of([t for s in pb.slots for t in s.free])
            for v in ev:
                v.free = all_of([t for s in small.slots for t in s.free])
            mfr = [b.free for b in bank]
            pring = Ring(bank)
            t_y = []
            for i in range(2):
                t_y.append(dma("sp", s_y, xs[:, 4 * i:4 * i + 4, :], ys_v[:, 8 * H + 4 * i:8 * H + 4 * i + 4, :],
                               ystores, st["xs"]))
            yst["r"] = [t_y[1]]
            st["big"], t_pe = transpose_in(xs, [t_y[1]] * 8, lambda k: None)
            st["xs"] = [t_pe]
            zs = []

            def sink(i, t, b, t_mm):
                dst = xs[:, t, 256 * i:256 * i + 256]
                x = op("act", lambda e: e.activation(dst, b.ap[:, 0:256], ACT.Copy), t_mm, st["xs"])
                b.free = [x]
                return x
            st["big_r"] = [residual_gemm(ws, 4, zs)]
            junk = R2[:, 2048:3072]
            t_ss = []
            for t in range(8):
                t_ss.append(op("act", lambda e, t=t: e.activation(junk, xs[:, t, :], ACT.Square, accum_out=SS[:, t:t + 1]),
                               zs[-1:], st["rstd_r"], t_tmp, t_ss[-1:]))
            t_r = rstd_from(8, 1024, t_ss)
            outs = []
            for t in range(8):
                x = op("dve", lambda e, t=t: e.scalar_tensor_tensor(xs[:, t, :], xs[:, t, :], RSTD[:, t:t + 1], GPROW[:, :],
                                                                    ALU.mult, ALU.mult), t_r, t_gp, zs[-1:])
                y = op("pool", lambda e, t=t: e.tensor_tensor(xs[:, t, :], xs[:, t, :], xh[:, t, :], ALU.add), x)
                outs.append(dma("sp", s_out, o_v[:, 8 * H + t, :], xs[:, t, :], y))
            st["rstd_r"] = [x]
            st["xs"] = [outs[-1]]
            t_xfree = [y]
            at_free["t"] = all_of([yb.free[0], t_ss[-1], (esem["pe"], count["done_pe"]), (esem["dve"], count["done_dve"]),
                                   (esem["pool"], count["done_pool"]), (esem["act"], count["done_act"])])

        ends = [(s, count[s[0]]) for s in s_st + s_ev + s_o + s_yu + [s_us, s_out] if count[s[0]]]

        block = ctx.enter_context(nc.Block())

        def play(e, name):
            seen = {}
            for waits, f, inc in queues[name]:
                for w in waits:
                    if w is None:
                        continue
                    s, v = w
                    if seen.get(s[0], 0) < v:
                        e.wait_ge(s[1], v)
                        seen[s[0]] = v
                r = f(e)
                if inc:
                    r.then_inc(*inc)

        @block.tensor
        def _(e):
            play(e, "pe")

        @block.scalar
        def _(e):
            play(e, "act")

        @block.vector
        def _(e):
            play(e, "dve")

        @block.gpsimd
        def _(e):
            play(e, "pool")

        @block.sync
        def _(e):
            play(e, "sp")
            for s, v in ends:
                e.wait_ge(s[1], v)


_INS = ["x", "norm1_g", "w_in", "pool_w", "pool_scale", "lam_q1", "lam_k1", "lam_q2", "lam_k2", "diff_norm_g",
        "sb_norm_g", "w_out", "norm2_g", "w_gate", "w_up", "w_down", "final_norm_g", "c_2", "positions_2", "w_ada_2",
        "b_ada_2", "g_pre_2", "w_in_2", "gmlp_ln_g_2", "gmlp_ws_2", "gmlp_bs_2", "ret_gn_g_2", "w_out_2", "g_post_2"]


def kernel(**inputs):
    import concourse.bacc as bacc
    from concourse.bass_utils import run_bass_kernel_spmd

    nc = bacc.Bacc("TRN2", target_bir_lowering=False, num_devices=1)
    arrays, aps = {}, {}
    for name in _INS:
        a = np.ascontiguousarray(inputs[name])
        arrays[f"in_{name}"] = a
        aps[name] = nc.dram_tensor(f"in_{name}", a.shape, mybir.dt.from_np(a.dtype), kind="ExternalInput").ap()
    arrays["shape_constants"] = shape_constants()
    const = nc.dram_tensor("shape_constants", [128, C_END], F32, kind="ExternalInput").ap()
    out = nc.dram_tensor("out_0", [1, S, D], F32, kind="ExternalOutput").ap()
    scr = {}
    for name, shape in (("QS", [2, 6, 128, S]), ("KS", [2, 6, 128, S]), ("VS", [2, 6, S, 128]),
                        ("US", [2, 128, S + 16]), ("YS", [S, D])):
        scr[name] = nc.dram_tensor("scratch_" + name, shape, F32, kind="Internal").ap()
    build(nc, aps, const, out, scr)
    r = run_bass_kernel_spmd(nc, [arrays], core_ids=[0])
    return r.results[0]["out_0"]
```

```python
import math
from contextlib import ExitStack

import numpy as np

import concourse.bass as bass
from concourse import mybir

F32 = mybir.dt.float32
FR = mybir.dt.float32r
I32 = mybir.dt.int32
ACT = mybir.ActivationFunctionType
ALU = mybir.AluOpType
AX = mybir.AxisListType.X

S = 2048
HT = 1024
D = 1024
NKT = 8
EPS = 1e-6
BIGV = 3.0e38
NEGV = -1.0e30
C_IDENT, C_DMASK, C_SBMIN, C_SBMUL, C_CAUS = 0, 128, 256, 384, 512
C_RMASK, C_QDEC, C_KDEC, C_INVF, C_ICNT, C_IW = 640, 1152, 1664, 1668, 1732, 1764
C_END = 1766


def shape_constants():
    c = np.zeros((128, C_END), np.float32)
    i = np.arange(128)
    q, k = i[:, None], i[None, :]
    c[:, C_IDENT:C_IDENT + 128] = np.eye(128)
    c[:, C_DMASK:C_DMASK + 128] = np.where(k <= q, BIGV, NEGV)
    c[:, C_SBMIN:C_SBMIN + 128] = np.where(k < q, BIGV, NEGV)
    c[:, C_SBMUL:C_SBMUL + 128] = np.where(k < q, 1.0, 0.0)
    c[:, C_CAUS:C_CAUS + 128] = np.where(q <= k, 1.0, 0.0)
    for h in range(4):
        lg = math.log(1.0 - 2.0 ** (-5.0 - h))
        diff = k - q
        sc = 128.0 ** -0.5
        c[:, C_RMASK + 128 * h:C_RMASK + 128 * h + 128] = np.where(diff >= 0, np.exp(np.maximum(diff, 0) * lg), 0.0) * sc
        c[:, C_QDEC + 128 * h:C_QDEC + 128 * h + 128] = np.exp((k + 1.0) * lg)
        c[:, C_KDEC + h] = np.exp((127.0 - i) * lg) * sc
    e = (np.arange(64, dtype=np.float32) / np.float32(64)).astype(np.float32)
    c[:, C_INVF:C_INVF + 64] = (np.float32(1.0) / np.power(np.float32(10000.0), e).astype(np.float32))[None, :]
    for t in range(2):
        for part in range(2):
            w = (2, 4, 8, 16)[2 * t + part]
            rows = slice(64 * part, 64 * part + 64)
            c[rows, C_ICNT + 16 * t:C_ICNT + 16 * t + 16] = (1.0 / np.minimum(np.arange(16) + 1, w))[None, :]
            c[rows, C_IW + t] = 1.0 / w
    return c


def two_pi_parts():
    left, parts = 2 * math.pi, []
    for _ in range(3):
        e = math.floor(math.log2(left)) - 7
        p = math.floor(left / 2.0 ** e) * 2.0 ** e
        parts.append(p)
        left -= p
    return parts + [left]


class Slot:

    def __init__(self, ap):
        self.ap = ap
        self.free = []


class Ring:
    def __init__(self, slots):
        self.slots = slots
        self.n = 0

    def take(self):
        s = self.slots[self.n % len(self.slots)]
        self.n += 1
        return s


def build(nc, I, const, out, scr):
    queues = {k: [] for k in ("pe", "act", "dve", "pool", "sp")}
    count = {}

    with ExitStack() as ctx:
        def sem(name):
            s = ctx.enter_context(nc.semaphore(name))
            count[name] = 0
            return (name, s)

        esem = {k: sem("done_" + k) for k in ("pe", "act", "dve", "pool")}

        def op(e, f, *waits, inc=True):
            flat = []
            for w in waits:
                flat += w if isinstance(w, list) else [w]
            queues[e].append((flat, f, (esem[e][1], 1) if inc else None))
            if inc:
                count[esem[e][0]] += 1
                return (esem[e], count[esem[e][0]])
            return None

        def dma(e, s, o, i, *waits, slow=False):
            flat = []
            for w in waits:
                flat += w if isinstance(w, list) else [w]
            queues[e].append((flat, lambda g: g.dma_start(o, i, allow_slow_non_contiguous=slow), (s[1], 16)))
            count[s[0]] += 16
            return (s, count[s[0]])

        def sbt(name, n, dt=F32, stack=ctx):
            return stack.enter_context(nc.sbuf_tensor(name, [128, n], dt))

        BIG = sbt("BIG", 16384, FR)
        XH = sbt("XH", 8192)
        XS = sbt("XS", 8192)
        WF = sbt("WF", 8192, FR)
        RAW = sbt("RAW", 3072)
        EV = sbt("EV", 2048)
        CB = sbt("CB", 640)
        ST = sbt("ST", 512)
        GROW = sbt("GROW", 256)
        GPROW = sbt("GPROW", 1024)
        SM = sbt("SM", 592)
        with ExitStack() as lay:
            AT = sbt("AT", 4096, FR, lay)
        with ExitStack() as lay:
            R2 = sbt("R2", 4096, F32, lay)
        PS = [ctx.enter_context(nc.psum_tensor(f"PS{i}", [128, 512], F32)) for i in range(8)]
        bank = [Slot(p) for p in PS]

        def smc(a, n):
            return SM[:, a:a + n]
        G1C, G2C, GPC = smc(0, 8), smc(8, 8), smc(16, 8)
        SHC, SCC = smc(24, 8), smc(32, 8)
        PSC, DGC, SGC = smc(40, 2), smc(42, 1), smc(43, 1)
        BSC, CC = smc(44, 4), smc(48, 8)
        NLAM, LT = smc(56, 1), smc(57, 4)
        SS, RV, RT = smc(64, 16), smc(80, 16), smc(96, 16)
        RSTD = smc(112, 16)
        MX, NM, SUMS, SC2 = smc(480, 32), smc(512, 32), smc(544, 32), smc(576, 16)
        POSF, ONE = smc(192, 8), smc(200, 1)
        BN, MV = smc(208, 48), smc(256, 16)
        IWC = smc(272, 2)
        ICN = smc(280, 32)
        KDC = smc(312, 4)
        MODC = smc(320, 16)
        LAMV = smc(336, 128)
        LAMD = smc(464, 1)
        LAME = smc(468, 4)
        ident = CB[:, C_IDENT:C_IDENT + 128]
        dmask = CB[:, C_DMASK:C_DMASK + 128]
        sbmin = CB[:, C_SBMIN:C_SBMIN + 128]
        sbmul = CB[:, C_SBMUL:C_SBMUL + 128]
        caus = CB[:, C_CAUS:C_CAUS + 128]

        s_c = sem("s_const")
        s_raw = [sem(f"s_raw{i}") for i in range(3)]
        s_kv = [sem(f"s_kv{i}") for i in range(2)]
        s_q = [sem(f"s_q{i}") for i in range(4)]
        s_x = [sem(f"s_x{i}") for i in range(2)]
        s_y = sem("s_y")
        s_u = sem("s_u")
        s_m = sem("s_m")
        s_r2 = sem("s_r2")
        s_gw = [sem(f"s_gw{i}") for i in range(4)]
        s_gr = [sem(f"s_gr{i}") for i in range(2)]
        s_ada = [sem(f"s_ada{i}") for i in range(2)]
        s_ev = [sem(f"s_ev{i}") for i in range(4)]
        s_o = [sem(f"s_o{i}") for i in range(2)]
        s_us = sem("s_us")
        s_yu = [sem(f"s_yu{i}") for i in range(2)]
        s_out = sem("s_out")

        def col(v, k):
            return v.rearrange("(k p) -> p k", p=128)

        dma("sp", s_c, CB[:, :], const[:, 0:640])
        dma("sp", s_c, KDC, const[:, C_KDEC:C_KDEC + 4])
        dma("sp", s_c, ICN, const[:, C_ICNT:C_ICNT + 32])
        dma("sp", s_c, IWC, const[:, C_IW:C_IW + 2])
        dma("sp", s_c, G1C, col(I["norm1_g"][0, :], 8), slow=True)
        dma("sp", s_c, G2C, col(I["norm2_g"][0, :], 8), slow=True)
        dma("sp", s_c, GPC, col(I["g_pre_2"][0, :], 8), slow=True)
        dma("sp", s_c, SHC, col(I["b_ada_2"][0, 0:1024], 8), slow=True)
        dma("sp", s_c, SCC, col(I["b_ada_2"][0, 1024:2048], 8), slow=True)
        dma("sp", s_c, CC, col(I["c_2"][0, :], 8), slow=True)
        dma("sp", s_c, PSC, col(I["pool_scale"][0, :], 2), slow=True)
        dma("sp", s_c, DGC, col(I["diff_norm_g"][0, :], 1), slow=True)
        sg = I["sb_norm_g"].rearrange("a d -> d a")
        dma("sp", s_c, SGC[0:64, :], sg, slow=True)
        dma("sp", s_c, SGC[64:128, :], sg, slow=True)
        dma("sp", s_c, BSC, I["gmlp_bs_2"][0, :, :].rearrange("g t -> t g"), slow=True)
        for i, n in enumerate(("lam_q1", "lam_k1")):
            dma("sp", s_c, LAMV[:, 64 * i:64 * i + 64], I[n][0:1, :].broadcast_to([128, 64]))
        consts = (s_c, count["s_const"])

        queues["act"].append(([], lambda e: e.preload_act_table_set("natural_log_exp_and_others"), None))
        t_one = op("dve", lambda e: e.memset(ONE, 1.0))
        t_l = op("dve", lambda e: e.tensor_tensor(LAMV[:, 0:64], LAMV[:, 0:64], LAMV[:, 64:128], ALU.mult), consts)
        t_l1 = op("dve", lambda e: e.reduce_sum(LAME[:, 0:1], LAMV[:, 0:64], AX), t_l)
        for i, n in enumerate(("lam_q2", "lam_k2")):
            t_lm = dma("sp", s_m, LAMV[:, 64 * i:64 * i + 64], I[n][0:1, :].broadcast_to([128, 64]), t_l1)
        t_l = op("dve", lambda e: e.tensor_tensor(LAMV[:, 0:64], LAMV[:, 0:64], LAMV[:, 64:128], ALU.mult), t_lm, t_l1)
        t_l2 = op("dve", lambda e: e.reduce_sum(LAME[:, 1:2], LAMV[:, 0:64], AX), t_l)
        t_e = op("act", lambda e: e.activation(LAME[:, 2:4], LAME[:, 0:2], ACT.Exp), t_l1, t_l2)
        t_d = op("dve", lambda e: e.tensor_tensor(LAMD, LAME[:, 3:4], LAME[:, 2:3], ALU.subtract), t_e)
        lam_init = 0.8 - 0.6 * math.exp(-0.3 * 0)
        t_nlam = op("dve", lambda e: e.tensor_scalar_add(NLAM, LAMD, -lam_init), t_d)
        t_dg = op("dve", lambda e: e.tensor_scalar_mul(DGC, DGC, 1.0 - lam_init), consts)

        raw = [Slot(RAW[:, 1024 * i:1024 * i + 1024]) for i in range(3)]
        wslot = [Slot((WF[:, 4096 * i:4096 * i + 2048], WF[:, 4096 * i + 2048:4096 * i + 4096])) for i in range(2)]
        wr = {"raw": 0, "slot": 0}

        def wprep(pieces):
            s = wslot[wr["slot"] % 2]
            wr["slot"] += 1
            hi, lo = s.ap
            toks = []
            for i in range(2):
                n = wr["raw"] % 3
                wr["raw"] += 1
                r = raw[n]
                for d, src in pieces(i, r.ap):
                    t_in = dma("sp", s_raw[n], d, src, r.free)
                h = hi[:, 1024 * i:1024 * i + 1024]
                l = lo[:, 1024 * i:1024 * i + 1024]
                t_hi = op("act", lambda e, h=h, r=r: e.activation(h, r.ap, ACT.Copy), t_in, s.free)
                t_lo = op("pool", lambda e, h=h, r=r, l=l: e.tensor_tensor(l, r.ap, h.bitcast(F32), ALU.subtract),
                          t_hi, t_in, s.free)
                r.free = [t_lo, t_hi]
                toks.append(t_lo)
            s.free = []
            return s, toks[1:] + [t_hi]

        def cols_of(W, segs):
            Wv = W.rearrange("(k p) n -> p k n", p=128)

            def pieces(i, r):
                rv = r.rearrange("p (k n) -> p k n", k=4)
                at, res = 0, []
                for c0, n in segs:
                    res.append((rv[:, :, at:at + n], Wv[:, 4 * i:4 * i + 4, c0:c0 + n]))
                    at += n
                return res
            return pieces

        def rows_of(W, r0):
            def pieces(i, r):
                return [(r, W[r0 + 128 * i:r0 + 128 * i + 128, :])]
            return pieces

        class Stream:
            def __init__(self, reqs):
                self.reqs = list(reqs)
                self.ready = []

            def ahead(self):
                if self.reqs and len(self.ready) < 2:
                    self.ready.append(wprep(self.reqs.pop(0)))

            def next(self):
                if not self.ready:
                    self.ahead()
                return self.ready.pop(0)

        bigh = BIG[:, 0:8192].rearrange("p (k t) -> p k t", k=8)
        bigl = BIG[:, 8192:16384].rearrange("p (k t) -> p k t", k=8)
        xh = XH[:, :].rearrange("p (t d) -> p t d", t=8)
        xs = XS[:, :].rearrange("p (t d) -> p t d", t=8)
        ev = [Slot(EV[:, 512 * i:512 * i + 512]) for i in range(4)]
        ring_ev = Ring(ev)
        pring = Ring(bank)

        def split_psum(b, t_mm, hi, lo, scale=None, bias=None, waits=[], w=512):
            v = ring_ev.take()
            src = b.ap[:, 0:w]
            tmp = v.ap[:, 0:w]
            if scale is None:
                t = op("dve", lambda e: e.tensor_copy(tmp, src), t_mm, v.free)
            elif bias is None:
                t = op("dve", lambda e: e.tensor_scalar(tmp, src, scale, None, ALU.mult), t_mm, v.free, waits)
            else:
                t = op("dve", lambda e: e.tensor_scalar(tmp, src, scale, bias, ALU.mult, ALU.add), t_mm, v.free, waits)
            b.free = [t]
            t_hi = op("act", lambda e: e.activation(hi, tmp, ACT.Copy), t, waits)
            t_lo = op("pool", lambda e: e.tensor_tensor(lo, tmp, hi.bitcast(F32), ALU.subtract), t_hi, waits)
            v.free = [t_hi, t_lo]
            return t_hi, t_lo

        def log_exp_tables():
            queues["act"].append(([], lambda e: e.preload_act_table_set("natural_log_exp_and_others"), None))

        def rstd_from(n, width, t_ss, src=SS, tables=False):
            if tables:
                log_exp_tables()
            v, r, t, = RV[:, 0:n], RSTD[:, 0:n], RT[:, 0:n]
            a = op("dve", lambda e: e.tensor_scalar(v, src[:, 0:n] if src is SS else src, 1.0 / width, EPS, ALU.mult, ALU.add), t_ss)
            b = op("act", lambda e: e.activation(r, v, ACT.Ln), a)
            b = op("act", lambda e: e.activation(r, r, ACT.Exp, scale=-0.5), b)
            c = op("dve", lambda e: e.tensor_tensor(t, r, r, ALU.mult), b)
            c = op("dve", lambda e: e.tensor_tensor(t, t, v, ALU.mult), c)
            c = op("dve", lambda e: e.tensor_scalar(t, t, -0.5, 1.5, ALU.mult, ALU.add), c)
            return op("dve", lambda e: e.tensor_tensor(r, r, t, ALU.mult), c)

        st = {"big": [], "xs": [], "big_r": [], "rstd_r": []}

        def sumsq(src8, rdy):
            toks = []
            for t in range(8):
                toks.append(op("act", lambda e, t=t: e.activation(xs[:, t, :], src8[:, t, :], ACT.Square,
                                                                 accum_out=SS[:, t:t + 1]), rdy, st["xs"], st["rstd_r"]))
            return toks

        def transpose_in(src8, t_src, scale_col, bias_col=None, waits=[]):
            toks = []
            last_pe = None
            for j in range(2):
                for k in range(8):
                    b = pring.take()
                    for t in range(4):
                        last_pe = op("pe", lambda e, b=b, t=t, k=k, j=j: e.transpose(
                            b.ap[:, 128 * t:128 * t + 128], src8[:, 4 * j + t, 128 * k:128 * k + 128], ident),
                            t_src[4 * j + t], b.free, inc=t == 3)
                    hi = bigh[:, k, 512 * j:512 * j + 512]
                    lo = bigl[:, k, 512 * j:512 * j + 512]
                    toks += list(split_psum(b, last_pe, hi, lo, scale_col(k), bias_col and bias_col(k),
                                            waits=st["big_r"] + waits))
            st["big_r"] = []
            return toks[-2:], last_pe

        def norm_in(rdy, scale_col, bias_col=None, waits=[]):
            t_ss = sumsq(xh, rdy)
            t_r = rstd_from(8, 1024, t_ss)
            toks = []
            for t in range(8):
                toks.append(op("dve", lambda e, t=t: e.tensor_scalar(xs[:, t, :], xh[:, t, :], RSTD[:, t:t + 1], None,
                                                                      ALU.mult), t_r, t_ss, rdy))
            st["rstd_r"] = [toks[-1]]
            st["big"], t_pe = transpose_in(xs, toks, scale_col, bias_col, waits)
            st["xs"] = [t_pe]

        def three(e_list, o, Ah, Al, Bh, Bl, start, stop, waits, last):
            op("pe", lambda e: e.matmul(o, Ah, Bh, start=start, stop=False), waits, inc=False)
            op("pe", lambda e: e.matmul(o, Ah, Bl, start=False, stop=False), inc=False)
            return op("pe", lambda e: e.matmul(o, Al, Bh, start=False, stop=stop), inc=last)

        def gemm_f(slot, f, j, b, waits):
            wh = slot.ap[0].rearrange("p (k n) -> p k n", k=8)
            wl = slot.ap[1].rearrange("p (k n) -> p k n", k=8)
            for k in range(8):
                fs = slice(128 * f, 128 * f + 128)
                ts = slice(512 * j, 512 * j + 512)
                t = three(None, b.ap[:, :], wh[:, k, fs], wl[:, k, fs], bigh[:, k, ts], bigl[:, k, ts],
                          k == 0, k == 7, (waits + b.free) if k == 0 else [], k == 7)
            return t

        def gemm_t(slot, t, b, waits, n=256):
            wh = slot.ap[0].rearrange("p (k n) -> p k n", k=8)
            wl = slot.ap[1].rearrange("p (k n) -> p k n", k=8)
            ts = slice(128 * t, 128 * t + 128)
            for k in range(8):
                r = three(None, b.ap[:, 0:n], bigh[:, k, ts], bigl[:, k, ts], wh[:, k, 0:n], wl[:, k, 0:n],
                          k == 0, k == 7, (waits + b.free) if k == 0 else [], k == 7)
            return r

        QS, KS, VS, US, YS = scr["QS"], scr["KS"], scr["VS"], scr["US"], scr["YS"]
        w_in = I["w_in"][0, :, :]
        x_v = I["x"][0, :, :].rearrange("(t p) d -> p t d", p=128)
        o_v = out[0, :, :].rearrange("(t p) d -> p t d", p=128)
        ys_v = YS.rearrange("(t p) d -> p t d", p=128)
        t_xfree = []
        uhist = {"done": []}
        yst = {"r": []}
        state_tok = {}

        staged = Ring([Slot((AT[:, 1024 * i:1024 * i + 512], AT[:, 1024 * i + 512:1024 * i + 1024])) for i in range(4)])
        s_st = [sem(f"s_st{i}") for i in range(4)]

        def store_parts(n, s, t_hi, t_lo, dh, dl, view=lambda a: a):
            a = dma("sp", s_st[n], dh, view(s.ap[0]).bitcast(F32), t_hi)
            b = dma("sp", s_st[n], dl, view(s.ap[1]).bitcast(F32), t_lo)
            s.free = [b]
            return b

        at_free = {"t": []}

        def all_of(toks):
            best = {}
            for s, v in toks:
                if s[0] not in best or best[s[0]][1] < v:
                    best[s[0]] = (s, v)
            return list(best.values())

        for H in range(2):
            tok0 = H * HT
            for i in range(2):
                t_x = dma("sp", s_x[i], xh[:, 4 * i:4 * i + 4, :], x_v[:, 8 * H + 4 * i:8 * H + 4 * i + 4, :], t_xfree)
            rdy = [(s_x[0], count["s_x0"]), (s_x[1], count["s_x1"])]
            blocks = [("u", 0, 0)] + [("q", 256 + 256 * i, i) for i in range(2)] + [("k", 768 + 256 * i, i) for i in range(2)] \
                + [("v", 1280 + 256 * i, i) for i in range(2)] + [("q", 1792, 2), ("k", 2048, 2), ("v", 2304, 2)]
            ws = Stream([cols_of(w_in, [(c, 256)]) for _, c, _ in blocks])
            ws.ahead()
            norm_in(rdy, lambda k: G1C[:, k:k + 1], waits=[consts])
            for s in staged.slots:
                s.free = list(at_free["t"])
            stores = []
            for kind, c0, idx in blocks:
                slot, t_w = ws.next()
                ws.ahead()
                last = []
                if kind in "uqk":
                    for f in range(2):
                        for j in range(2):
                            b = pring.take()
                            t_mm = gemm_f(slot, f, j, b, t_w + st["big"])
                            last = [t_mm]
                            sl = slice(tok0 + 512 * j, tok0 + 512 * j + 512)
                            if kind == "u":
                                v = ring_ev.take()
                                n = ev.index(v)
                                t = op("dve", lambda e, v=v, b=b: e.tensor_copy(v.ap, b.ap[:, :]), t_mm, v.free)
                                b.free = [t]
                                v.free = [dma("sp", s_ev[n], US[f, :, 16 + sl.start:16 + sl.stop], v.ap, t)]
                                stores.append(v.free[0])
                            else:
                                n = staged.n % 4
                                s = staged.take()
                                ft = 2 * idx + f
                                t_hi, t_lo = split_psum(b, t_mm, s.ap[0], s.ap[1], 0.125 if kind == "q" else None,
                                                        waits=list(s.free))
                                Z = QS if kind == "q" else KS
                                stores.append(store_parts(n, s, t_hi, t_lo, Z[0, ft, :, sl], Z[1, ft, :, sl]))
                else:
                    for t2 in range(4):
                        b = pring.take()
                        n = staged.n % 4
                        s = staged.take()
                        for u in range(2):
                            wh = slot.ap[0].rearrange("p (k n) -> p k n", k=8)
                            wl = slot.ap[1].rearrange("p (k n) -> p k n", k=8)
                            ts = slice(128 * (2 * t2 + u), 128 * (2 * t2 + u) + 128)
                            for k in range(8):
                                t_mm = three(None, b.ap[:, 256 * u:256 * u + 256], bigh[:, k, ts], bigl[:, k, ts],
                                             wh[:, k, :], wl[:, k, :], k == 0, k == 7,
                                             (t_w + st["big"] + b.free) if k == 0 and u == 0 else [], k == 7 and u == 1)
                        last = [t_mm]
                        t_hi, t_lo = split_psum(b, t_mm, s.ap[0], s.ap[1], waits=list(s.free))
                        r0 = tok0 + 256 * t2
                        for f in range(2):
                            dst = [VS[p, 2 * idx + f, r0:r0 + 256, :].rearrange("(u p) e -> p u e", p=128) for p in range(2)]
                            view = lambda a, f=f: a.rearrange("p (u n) -> p u n", u=2)[:, :, 128 * f:128 * f + 128]
                            stores.append(store_parts(n, s, t_hi, t_lo, dst[0], dst[1], view))
                slot.free = last
            st["big_r"] = last
            stores = all_of(stores)
            if H == 0:
                zt = op("dve", lambda e: e.memset(EV[:, 0:16], 0.0), ev[0].free)
                for f in range(2):
                    zd = dma("sp", s_us, US[f, :, 0:16], EV[:, 0:16], zt)
                ev[0].free = [zd]
                uhist["done"] = [zd]

            nk0 = 8 * H
            kvs = [Slot(BIG[:, 8192 * i:8192 * i + 8192]) for i in range(2)]
            for s in kvs:
                s.free = list(st["big_r"])
            qsl = [Slot(AT[:, 1024 * i:1024 * i + 1024]) for i in range(4)]
            for s in qsl:
                s.free = list(stores)
            tr = Ring([Slot(WF[:, 1024 * i:1024 * i + 1024]) for i in range(8)])
            for s in tr.slots:
                s.free = list(st["big_r"])
            ob = [Slot(EV[:, 1024 * i:1024 * i + 1024]) for i in range(2)]
            ob[0].free = ev[0].free + ev[1].free
            ob[1].free = ev[2].free + ev[3].free
            traw = Ring([Slot(RAW[:, 512 * i:512 * i + 512]) for i in range(6)])
            for i, v in enumerate(traw.slots):
                v.free = list(raw[i // 2].free)
            sring = Ring(bank[0:5])
            tring = Ring(bank[5:7])
            oring = Ring(bank[7:8])
            L = tok0 + HT
            ystores = []

            def load_head(j):
                kv = kvs[j % 2]
                kk = kv.ap[:, 0:4096].rearrange("p (r t) -> p r t", r=2)
                vv = kv.ap[:, 4096:8192].rearrange("p (t a e) -> p t a e", a=2, e=128)
                for a in range(2):
                    dma("sp", s_kv[j % 2], kk[64 * a:64 * a + 64, :, 0:L].bitcast(F32),
                        KS[a, j, :, 0:L].rearrange("(r d) t -> d r t", r=2), stores, kv.free)
                    t = dma("sp", s_kv[j % 2], vv[:, 0:L // 128, a, :].bitcast(F32),
                            VS[a, j, 0:L, :].rearrange("(t p) e -> p t e", p=128), stores, kv.free)
                kv.free = []
                return kk, vv, [t], kv

            queries = {}

            def load_queries(j, h):
                n = (4 * j + h) % 4
                q = qsl[n]
                qq = q.ap.rearrange("p (a r t) -> p a r t", a=2, r=2)
                t0 = tok0 + 256 * h
                for a in range(2):
                    for d in range(2):
                        t = dma("sp", s_q[n], qq[64 * d:64 * d + 64, a, :, :].bitcast(F32),
                                QS[a, j, :, t0:t0 + 256].rearrange("(r d) t -> d r t", r=2), stores, q.free)
                q.free = []
                queries[j, h] = (qq, t, q)

            def qk(g, c, w):
                j, qt = g["j"], g["qt"]
                kk, vv, t_ld, _ = heads[j]
                qq, t_q, slot = queries[j, qt // 2]
                res = []
                qs = slice(128 * (qt % 2), 128 * (qt % 2) + 128)
                ks = slice(512 * c, 512 * c + w)
                for r in range(2):
                    b = sring.take()
                    for a in range(2):
                        t = op("pe", lambda e, a=a, r=r, b=b: e.matmul(b.ap[:, 0:w], qq[:, a, r, qs], kk[:, r, ks],
                                                                      start=a == 0, stop=a == 1),
                               t_ld, t_q, b.free, inc=a == 1)
                    res.append((b, t))
                slot.free = [t]
                g["nchunk"] = g.get("nchunk", 0) + 1
                if qt % 2 and g["nchunk"] == len(chunks(nk0 + qt + 1)):
                    h = qt // 2
                    nxt = (j + 1, h) if j < 5 else None
                    if nxt:
                        load_queries(*nxt)
                return res

            def turn(src, w, t_src, hi_engine):
                b, s, v = tring.take(), tr.take(), traw.take()
                for i in range(w // 128):
                    t = op("pe", lambda e, i=i: e.transpose(b.ap[:, 128 * i:128 * i + 128],
                                                            src[:, 128 * i:128 * i + 128], ident),
                           t_src, b.free, inc=i == w // 128 - 1)
                hi, lo, tmp = s.ap[:, 0:w], s.ap[:, 512:512 + w], v.ap[:, 0:w]
                t_c = op("act", lambda e: e.activation(tmp, b.ap[:, 0:w], ACT.Copy), t, v.free)
                b.free = [t_c]
                if hi_engine == "act":
                    t_hi = op("act", lambda e: e.activation(hi, tmp, ACT.Copy), t_c, s.free)
                else:
                    t_hi = op("dve", lambda e: e.tensor_copy(hi, tmp), t_c, s.free)
                t_lo = op("pool", lambda e: e.tensor_tensor(lo, tmp, hi.bitcast(F32), ALU.subtract), t_hi, t_c, s.free)
                v.free = [t_lo]
                s.free = []
                return s, [t_hi, t_lo], t

            def pv(hd, s, t_s, c, w, o, e0, en, first, last, clear=True):
                vv = hd[1]
                for i in range(w // 128):
                    kt = 4 * c + i
                    hi, lo = s.ap[:, 128 * i:128 * i + 128], s.ap[:, 512 + 128 * i:512 + 128 * i + 128]
                    fst, lst = first and i == 0, last and i == w // 128 - 1
                    op("pe", lambda e, hi=hi, kt=kt, fst=fst: e.matmul(o.ap[:, 0:2 * en], hi, vv[:, kt, :, e0:e0 + en],
                                                                      start=fst and clear, stop=False, skip_group_check=True),
                       t_s, o.free if fst else [], inc=False)
                    t = op("pe", lambda e, lo=lo, kt=kt, lst=lst: e.matmul(o.ap[:, 0:en], lo, vv[:, kt, 0, e0:e0 + en],
                                                                          start=False, stop=lst, skip_group_check=True),
                           inc=i == w // 128 - 1)
                s.free = [t]
                return t

            def chunks(n):
                return [(c, min(512, 128 * n - 512 * c)) for c in range((n + 3) // 4)]

            heads = {0: load_head(0)}
            for h in range(4):
                load_queries(0, h)
            heads[1] = load_head(1)

            def finish_tile(j, O, t_o):
                o = O.ap.rearrange("p (t e) -> p t e", t=8)
                parts = 1 if j < 4 else 2
                n, en = 8 * parts, 128 // parts
                v = O.ap.rearrange("p (n e) -> p n e", n=n)
                q = SCR.rearrange("p (n e) -> p n e", n=n)
                t = op("pool", lambda e: e.tensor_tensor(SCR, O.ap, O.ap, ALU.mult), t_o, scr_free)
                t = op("dve", lambda e: e.reduce_sum(SS[:, 0:n], q, AX), t, st["rstd_r"])
                scr_free[:] = [t]
                t = rstd_from(n, en, [t])
                t = op("pool", lambda e: e.tensor_tensor(v, v, RSTD[:, 0:n].rearrange("p (n a) -> p n a", a=1).broadcast_to([128, n, en]),
                                                         ALU.mult), t, t_o)
                ts = [t]
                st["rstd_r"] = [t]
                c0 = 256 + 128 * j
                d = dma("pool", s_o[j % 2], ys_v[:, 8 * H:8 * H + 8, c0:c0 + 128], o, ts[-1], yst["r"])
                O.free = [d]
                ystores.append(d)

            pch = Ring([Slot(XS[:, 512 * i:512 * i + 512]) for i in range(14)])
            SCR = XS[:, 7168:8192]
            scr_free = list(st["xs"])
            for s in pch.slots:
                s.free = list(st["xs"])
            work = []
            for j in range(4):
                for qt in range(8):
                    g = {"j": j, "qt": qt, "m": (8 * j + qt) % 4, "nc": len(chunks(nk0 + qt + 1)), "t": []}
                    for c, w in chunks(nk0 + qt + 1):
                        work.append({"g": g, "c": c, "w": w, "first": c == 0, "last": c == g["nc"] - 1})
            mfree = {m: [] for m in range(4)}

            def df_a(x):
                g, c, w = x["g"], x["c"], x["w"]
                j, m = g["j"], g["m"]
                x["p"] = []
                for r, (b, t) in enumerate(qk(g, c, w)):
                    if x["last"]:
                        dg = b.ap[:, w - 128:w]
                        t = op("dve", lambda e, dg=dg: e.tensor_tensor(dg, dg, dmask, ALU.min), t)
                    nm = NM[:, 8 * m + 4 * r + c:8 * m + 4 * r + c + 1]
                    sm = SUMS[:, 8 * m + 4 * r + c:8 * m + 4 * r + c + 1]
                    t = op("dve", lambda e, b=b, nm=nm: e.tensor_reduce(nm, b.ap[:, 0:w], AX, ALU.max, negate=True), t, mfree[m])
                    p = pch.take()
                    t = op("act", lambda e, b=b, nm=nm, sm=sm, p=p: e.activation(p.ap[:, 0:w], b.ap[:, 0:w], ACT.Exp, bias=nm,
                                                                              accum_out=sm), t, p.free, mfree[m])
                    b.free = [t]
                    p.free = []
                    x["p"].append(p)
                    g["t"].append(t)

            def df_e(g):
                m, k = g["m"], g["nc"]
                nm = NM[:, 8 * m:8 * m + 8].rearrange("p (r c) -> p r c", r=2)[:, :, 0:k]
                sm = SUMS[:, 8 * m:8 * m + 8].rearrange("p (r c) -> p r c", r=2)[:, :, 0:k]
                f = MX[:, 8 * m:8 * m + 8].rearrange("p (r c) -> p r c", r=2)[:, :, 0:k]
                sc = SC2[:, 4 * m:4 * m + 4]
                a = op("dve", lambda e: e.tensor_reduce(sc[:, 0:2], nm, AX, ALU.min), g["t"])
                a0 = op("act", lambda e: e.activation(f[:, 0, :], nm[:, 0, :], ACT.Exp, scale=-1.0, bias=sc[:, 0:1]), a)
                a1 = op("act", lambda e: e.activation(f[:, 1, :], nm[:, 1, :], ACT.Exp, scale=-1.0, bias=sc[:, 1:2]), a)
                a = op("dve", lambda e: e.tensor_tensor(sm, sm, f, ALU.mult), a0, a1, g["t"])
                a = op("dve", lambda e: e.reduce_sum(sc[:, 2:4], sm, AX), a)
                a = op("dve", lambda e: e.reciprocal(sc[:, 2:4], sc[:, 2:4]), a)
                b0 = op("dve", lambda e: e.tensor_scalar(f[:, 0, :], f[:, 0, :], sc[:, 2:3], None, ALU.mult), a)
                b1 = op("dve", lambda e: e.tensor_scalar(f[:, 1, :], f[:, 1, :], sc[:, 3:4], NLAM, ALU.mult, ALU.mult), a, t_nlam)
                g["e"] = [b0, b1]

            def df_c(x):
                g, c, w, (p1, p2) = x["g"], x["c"], x["w"], x["p"]
                q1 = 8 * g["m"] + c
                a = op("pool", lambda e: e.tensor_scalar(p1.ap[:, 0:w], p1.ap[:, 0:w], MX[:, q1:q1 + 1], 1.0, ALU.mult, ALU.mult), g["e"], g["t"])
                a = op("dve", lambda e: e.scalar_tensor_tensor(p1.ap[:, 0:w], p2.ap[:, 0:w], MX[:, q1 + 4:q1 + 5], p1.ap[:, 0:w],
                                                               ALU.mult, ALU.add), a, g["e"])
                p2.free = [a]
                x["t"] = a
                if x["last"]:
                    mfree[g["m"]] = [a]

            def df_t(x):
                p1 = x["p"][0]
                x["s"], x["ts"], t_pe = turn(p1.ap[:, 0:x["w"]], x["w"], [x["t"]], "act")
                p1.free = [t_pe]

            def pv_stage(x, e0, en):
                g = x["g"]
                if x["first"]:
                    g["o"] = oring.take()
                o = g["o"]
                hd = heads[g["j"]]
                t = pv(hd, x["s"], x["ts"], x["c"], x["w"], o, e0, en, x["first"], x["last"])
                hd[3].free = [t]
                if x["last"]:
                    O = ob[g["j"] % 2]
                    dst = O.ap[:, 128 * g["qt"] + e0:128 * g["qt"] + e0 + en]
                    y = op("dve", lambda e: e.tensor_copy(dst, o.ap[:, 0:en]), t, O.free)
                    y = op("dve", lambda e: e.tensor_tensor(dst, o.ap[:, en:2 * en], dst, ALU.add), y)
                    o.free = [y]
                    return O, y
                return None, None

            def df_d(x):
                O, y = pv_stage(x, 0, 128)
                j = x["g"]["j"]
                if O and x["g"]["qt"] == 7:
                    heads[j + 2] = load_head(j + 2)
                    finish_tile(j, O, y)

            nwork = len(work)
            for i in range(nwork + 9):
                if i < nwork:
                    df_a(work[i])
                if 0 <= i - 1 < nwork and work[i - 1]["last"]:
                    df_e(work[i - 1]["g"])
                if 0 <= i - 5 < nwork:
                    df_c(work[i - 5])
                if 0 <= i - 8 < nwork:
                    df_d(work[i - 8])
                if 0 <= i - 6 < nwork:
                    df_t(work[i - 6])

            aslot = Ring([Slot(XS[:, 512 * i:512 * i + 512]) for i in range(10)])
            cslot = Ring([Slot(XS[:, 5120 + 512 * i:5120 + 512 * i + 512]) for i in range(4)])
            for s, p in zip(aslot.slots + cslot.slots, pch.slots):
                s.free = list(p.free)
            work = []
            for j in (4, 5):
                for qt in range(8):
                    cs = chunks(nk0 + qt + 1)[::-1]
                    g = {"j": j, "qt": qt, "carry": [None, None]}
                    for i, (c, w) in enumerate(cs):
                        work.append({"g": g, "c": c, "w": w, "first": i == 0, "last": i == len(cs) - 1})

            def sb_a(x):
                g, w = x["g"], x["w"]
                x["b"], x["a"], x["t"] = [], [], [None, None]
                for r, (b, t) in enumerate(qk(g, x["c"], w)):
                    s = aslot.take()
                    a = s.ap[:, 0:w]
                    x["t"][r] = op("act", lambda e, a=a, b=b: e.activation(a, b.ap[:, 0:w], ACT.Abs), t, s.free)
                    x["b"].append(b)
                    x["a"].append(s)
                for r in range(2):
                    a = x["a"][r].ap[:, 0:w]
                    x["t"][r] = op("act", lambda e, a=a: e.activation(a, a, ACT.Exp, scale=-1.0), x["t"][r])
                for r in range(2):
                    a = x["a"][r].ap[:, 0:w]
                    x["t"][r] = op("act", lambda e, a=a: e.activation(a, a, ACT.Ln, bias=1.0), x["t"][r])

            def sb_b(x):
                g, w = x["g"], x["w"]
                aa = [x["a"][r].ap[:, 0:w] for r in range(2)]
                t, cc, cs = [None, None], [None, None], [None, None]
                for r in range(2):
                    a, b = aa[r], x["b"][r]
                    t[r] = op("dve", lambda e, a=a, b=b: e.scalar_tensor_tensor(a, b.ap[:, 0:w], 0.0, a, ALU.max, ALU.add), x["t"][r])
                if x["first"]:
                    for r in range(2):
                        d = aa[r][:, w - 128:w]
                        t[r] = op("dve", lambda e, d=d: e.tensor_tensor(d, d, sbmul, ALU.mult), t[r])
                for r in range(2):
                    cs[r] = cslot.take()
                    cc[r] = cs[r].ap[:, 0:w]
                    first = g["carry"][r] is None
                    init, wt = (0.0, []) if first else (g["carry"][r][0], [g["carry"][r][1]])
                    t[r] = op("dve", lambda e, a=aa[r], o=cc[r], init=init: e.tensor_tensor_scan(
                        o[:, ::-1], ONE.broadcast_to([128, w]), a[:, ::-1], init, ALU.mult, ALU.add), t[r], wt, cs[r].free, t_one)
                    g["carry"][r] = (cc[r][:, 0:1], t[r])
                for r in range(2):
                    b = x["b"][r]
                    t[r] = op("dve", lambda e, a=aa[r], b=b, c=cc[r]: e.tensor_tensor(a, b.ap[:, 0:w], c, ALU.subtract), t[r])
                    b.free = [t[r]]
                    cs[r].free = [t[r]]
                if x["first"]:
                    for r in range(2):
                        d = aa[r][:, w - 128:w]
                        t[r] = op("dve", lambda e, d=d: e.tensor_tensor(d, d, sbmin, ALU.min), t[r])
                x["t"] = t

            def sb_c(x):
                for r in range(2):
                    a = x["a"][r].ap[:, 0:x["w"]]
                    x["t"][r] = op("act", lambda e, a=a: e.activation(a, a, ACT.Exp), x["t"][r])

            def sb_t(x):
                x["s"] = []
                for r in range(2):
                    s, ts, t_pe = turn(x["a"][r].ap[:, 0:x["w"]], x["w"], [x["t"][r]], "dve")
                    x["a"][r].free = [t_pe]
                    x["s"].append((s, ts))

            def sb_d(x):
                g = x["g"]
                hd = heads[g["j"]]
                o = bank[7]
                for r in range(2):
                    s, ts = x["s"][r]
                    view = Slot(o.ap[:, 128 * r:128 * r + 128])
                    view.free = o.free
                    t = pv(hd, s, ts, x["c"], x["w"], view, 64 * r, 64, x["first"], x["last"], clear=r == 0)
                hd[3].free = [t]
                if x["last"]:
                    O = ob[g["j"] % 2]
                    dst = O.ap[:, 128 * g["qt"]:128 * g["qt"] + 128].rearrange("p (r e) -> p r e", r=2)
                    ov = o.ap[:, 0:256].rearrange("p (r a e) -> p r a e", r=2, a=2)
                    y = op("dve", lambda e: e.tensor_copy(dst, ov[:, :, 0, :]), t, O.free)
                    y = op("dve", lambda e: e.tensor_tensor(dst, ov[:, :, 1, :], dst, ALU.add), y)
                    o.free = [y]
                    if g["qt"] == 7:
                        finish_tile(g["j"], O, y)

            nwork = len(work)
            for i in range(nwork + 5):
                if 0 <= i - 2 < nwork:
                    sb_c(work[i - 2])
                if i < nwork:
                    sb_a(work[i])
                if 0 <= i - 1 < nwork:
                    sb_b(work[i - 1])
                if 0 <= i - 5 < nwork:
                    sb_d(work[i - 5])
                if 0 <= i - 3 < nwork:
                    sb_t(work[i - 3])

            att_pe = [(esem["pe"], count["done_pe"])]
            st["xs"] = att_pe + all_of([t for s in aslot.slots + cslot.slots for t in s.free] + scr_free)
            st["big_r"] = list(att_pe)
            for s in wslot:
                s.free = list(att_pe)
            for r in raw:
                r.free = all_of([t for v in traw.slots for t in v.free])
            ev_free = ob[0].free + ob[1].free
            for v in ev:
                v.free = list(ev_free)
            pring = Ring(bank)

            ws = Stream([cols_of(I["w_out"][0, :, :], [(256 * i, 256)]) for i in range(4)])
            ws.ahead()
            pw = XS[:, 8192 - 256:8192]
            t_z = op("dve", lambda e: e.memset(pw, 0.0), st["xs"])
            for f in range(2):
                for g in range(2):
                    t_pw = dma("sp", s_u, pw[64 * g:64 * g + 64, 128 * f + 64 * g:128 * f + 64 * g + 64],
                               I["pool_w"][0, 2 * f + g, :, :], t_z, st["xs"])
            NU = 1040
            t_us = []
            ua, ub = XS[:, 0:NU], XS[:, NU:2 * NU]
            pooled = [XS[:, 2 * NU:2 * NU + 1024], XS[:, 2 * NU + 1024:2 * NU + 2048]]
            free_u = list(st["xs"])
            mixed = []
            for f in range(2):
                t_in = dma("sp", s_u, ua, US[f, :, tok0:tok0 + NU], stores, uhist["done"], free_u, [t_pw])
                lo_w, hi_w = ((2, 4), (8, 16))[f]
                cur, nxt, sh, t = ua, ub, 1, t_in
                pl = pooled[f]
                orig_free = t_in

                bufs = [XS[:, 4 * NU:5 * NU], XS[:, 5 * NU:6 * NU]]
                src = ua
                steps = 0
                w = 1
                t_seg = {}
                while w < hi_w:
                    dst = bufs[steps % 2]
                    w0 = w
                    s0 = 2 * w - 1
                    t = op("dve", lambda e, dst=dst, src=src, w0=w0, s0=s0: e.tensor_tensor(
                        dst[:, s0:NU], src[:, s0:NU], src[:, s0 - w0:NU - w0], ALU.add), t, t_in, free_u)
                    w *= 2
                    steps += 1
                    src = dst
                    if w == lo_w:
                        t = op("dve", lambda e, dst=dst, pl=pl: e.tensor_copy(pl[0:64, :], dst[0:64, 16:NU]), t, free_u)
                    if w == hi_w:
                        t = op("dve", lambda e, dst=dst, pl=pl: e.tensor_copy(pl[64:128, :], dst[64:128, 16:NU]), t, free_u)
                if H == 0:
                    t = op("dve", lambda e, pl=pl, f=f: e.tensor_tensor(pl[:, 0:16], pl[:, 0:16], ICN[:, 16 * f:16 * f + 16], ALU.mult), t)
                    t = op("dve", lambda e, pl=pl, f=f: e.tensor_scalar(pl[:, 16:1024], pl[:, 16:1024], IWC[:, f:f + 1], None, ALU.mult), t)
                else:
                    t = op("dve", lambda e, pl=pl, f=f: e.tensor_scalar(pl, pl, IWC[:, f:f + 1], None, ALU.mult), t)
                t = op("dve", lambda e, pl=pl: e.tensor_tensor(pl, pl, ua[:, 16:NU], ALU.subtract), t)
                free_u = [t]
                for j in range(2):
                    b = pring.take()
                    t_mm = op("pe", lambda e, b=b, j=j, f=f, pl=pl: e.matmul(b.ap[:, :], pw[:, 128 * f:128 * f + 128],
                                                                      pl[:, 512 * j:512 * j + 512], start=True, stop=True),
                              t, t_pw, b.free)
                    mixed += list(split_psum(b, t_mm, bigh[:, f, 512 * j:512 * j + 512], bigl[:, f, 512 * j:512 * j + 512],
                                             PSC[:, f:f + 1], waits=st["big_r"]))
            st["xs"] = [t_mm] + free_u
            t_y = []
            for i in range(2):
                t_y.append(dma("sp", s_y, xs[:, 4 * i:4 * i + 4, 256:1024], ys_v[:, 8 * H + 4 * i:8 * H + 4 * i + 4, 256:1024],
                               ystores, st["xs"]))
            yst["r"] = [t_y[1]]
            for j in range(2):
                for k in range(2, 8):
                    b = pring.take()
                    for t in range(4):
                        t_pe = op("pe", lambda e, b=b, t=t, k=k, j=j: e.transpose(
                            b.ap[:, 128 * t:128 * t + 128], xs[:, 4 * j + t, 128 * k:128 * k + 128], ident),
                            t_y[1], b.free, inc=t == 3)
                    mixed += list(split_psum(b, t_pe, bigh[:, k, 512 * j:512 * j + 512], bigl[:, k, 512 * j:512 * j + 512],
                                             DGC if k < 6 else SGC, waits=st["big_r"] + [t_dg]))
            st["xs"] = [t_pe]
            st["big"] = all_of(mixed)

            def residual_gemm(ws, nblk, res):
                for i in range(nblk):
                    slot, t_w = ws.next()
                    ws.ahead()
                    for t in range(8):
                        b = pring.take()
                        t_mm = gemm_t(slot, t, b, t_w + st["big"])
                        res.append(sink(i, t, b, t_mm))
                    slot.free = [t_mm]
                return t_mm

            def sink(i, t, b, t_mm):
                dst = xh[:, t, 256 * i:256 * i + 256]
                x = op("dve", lambda e: e.tensor_tensor(dst, b.ap[:, 0:256], dst, ALU.add), t_mm)
                b.free = [x]
                return x
            res = []
            st["big_r"] = [residual_gemm(ws, 4, res)]
            wg, wu, wd = I["w_gate"][0, :, :], I["w_up"][0, :, :], I["w_down"][0, :, :]
            NG = 11
            order = [("g", 0), ("u", 0)]
            for g in range(1, NG):
                order += [("g", g), ("d", g - 1), ("u", g)]
            order.append(("d", NG - 1))
            reqs = []
            for kind, g in order:
                reqs.append(rows_of(wd, 256 * g) if kind == "d" else cols_of(wg if kind == "g" else wu, [(256 * g, 256)]))
            ws = Stream(reqs)
            ws.ahead()
            norm_in(res[-1:], lambda k: G2C[:, k:k + 1])
            at = AT[:, :].rearrange("p (a f t) -> p a f t", a=2, f=2)
            at_r = all_of(stores + [(esem["pe"], count["done_pe"])])
            sgs = [Slot(XS[:, 512 * i:512 * i + 512]) for i in range(4)]
            for s in sgs:
                s.free = list(st["xs"])
            ACC = XS[:, 2048:5120]
            ada = [Slot(XS[:, 5120:6144]), Slot(XS[:, 6144:7168])]
            t_acc = None
            ada_free = list(st["xs"])
            if H == 0:
                t_sc = op("act", lambda e: e.activation(CC, CC, ACT.Silu), consts)
                for s in ada:
                    s.free = list(st["xs"])
            acc_t = [None] * 3
            na = 0
            for kind, g in order:
                slot, t_w = ws.next()
                ws.ahead()
                if kind in "gu":
                    for f in range(2):
                        for j in range(2):
                            b = pring.take()
                            t_mm = gemm_f(slot, f, j, b, t_w + st["big"])
                            s = sgs[2 * f + j]
                            if kind == "g":
                                s.t = op("act", lambda e, s=s, b=b: e.activation(s.ap, b.ap[:, :], ACT.Silu), t_mm, s.free)
                                b.free = [s.t]
                            else:
                                x = op("dve", lambda e, s=s, b=b: e.tensor_tensor(s.ap, b.ap[:, :], s.ap, ALU.mult), t_mm, s.t)
                                b.free = [x]
                                hi, lo = at[:, 0, f, 512 * j:512 * j + 512], at[:, 1, f, 512 * j:512 * j + 512]
                                t_hi = op("act", lambda e, s=s, hi=hi: e.activation(hi, s.ap, ACT.Copy), x, at_r)
                                t_lo = op("pool", lambda e, s=s, hi=hi, lo=lo: e.tensor_tensor(lo, s.ap, hi.bitcast(F32), ALU.subtract),
                                          t_hi, x, at_r)
                                s.free = [t_hi, t_lo]
                                t_at = [t_hi, t_lo]
                    if H == 0 and kind == "g" and g < 8:
                        for n in range(3):
                            a = ada[na % 2]
                            t_a = dma("sp", s_ada[na % 2], a.ap, I["w_ada_2"][0, 128 * g:128 * g + 128, 1024 * n:1024 * n + 1024], a.free)
                            na += 1
                            acc = ACC[:, 1024 * n:1024 * n + 1024]
                            if g == 0:
                                acc_t[n] = op("dve", lambda e, a=a, acc=acc: e.tensor_scalar(acc, a.ap, CC[:, 0:1], None, ALU.mult),
                                              t_a, t_sc, ada_free)
                            else:
                                acc_t[n] = op("dve", lambda e, a=a, acc=acc, g=g: e.scalar_tensor_tensor(
                                    acc, a.ap, CC[:, g:g + 1], acc, ALU.mult, ALU.add), t_a, acc_t[n])
                            a.free = [acc_t[n]]
                else:
                    dh = slot.ap[0].rearrange("p (f n) -> p f n", f=2)
                    dl = slot.ap[1].rearrange("p (f n) -> p f n", f=2)
                    for t in range(8):
                        for n in range(2):
                            b = pring.take()
                            ts, ns = slice(128 * t, 128 * t + 128), slice(512 * n, 512 * n + 512)
                            for f in range(2):
                                t_mm = three(None, b.ap[:, :], at[:, 0, f, ts], at[:, 1, f, ts], dh[:, f, ns], dl[:, f, ns],
                                             f == 0, f == 1, (t_w + t_at + b.free) if f == 0 else [], f == 1)
                            dst = xh[:, t, ns]
                            x = op("dve", lambda e, b=b, dst=dst: e.tensor_tensor(dst, b.ap[:, :], dst, ALU.add), t_mm,
                                   *( [] if g else [st["xs"]]))
                            b.free = [x]
                    at_r = [t_mm]
                slot.free = [t_mm]
            st["big_r"] = [t_mm]
            t_res = x
            t_gate_end = [t_mm]
            if H == 0:
                b = pring.take()
                for k in range(16):
                    t_m = op("pe", lambda e, k=k, b=b: e.matmul(b.ap[:, k:k + 1], ACC[:, 128 * k:128 * k + 128], ONE,
                                                               start=True, stop=True, skip_group_check=True), acc_t, t_one, b.free, inc=k == 15)
                x = op("dve", lambda e, b=b: e.tensor_copy(MODC, b.ap[:, 0:16]), t_m)
                b.free = [x]
                x1 = op("dve", lambda e: e.tensor_tensor(SHC, SHC, MODC[:, 0:8], ALU.add), x, consts)
                x2 = op("dve", lambda e: e.tensor_tensor(SCC, SCC, MODC[:, 8:16], ALU.add), x)
                x2 = op("dve", lambda e: e.tensor_scalar_add(SCC, SCC, 1.0), x2)
                t_mod = op("dve", lambda e: e.tensor_tensor(GPC, GPC, SCC, ALU.mult), x2, x1)
                rb = XS[:, 5120:6144]
                rg = XS[:, 6144:7168]
                t_rb = dma("sp", s_ada[0], rb, I["b_ada_2"][0:1, 2048:3072].broadcast_to([128, 1024]), ada[0].free)
                t_rg = dma("sp", s_ada[1], rg, I["g_post_2"][0:1, :].broadcast_to([128, 1024]), ada[1].free)
                ONEM = XS[:, 7168:7296]
                t_om = op("dve", lambda e: e.memset(ONEM, 1.0), ada_free)
                for n in range(2):
                    b = pring.take()
                    ns = slice(512 * n, 512 * n + 512)
                    t_m = op("pe", lambda e, n=n, b=b: e.matmul(b.ap[:, :], ONEM, ACC[:, 2048 + 512 * n:2560 + 512 * n],
                                                               start=True, stop=True), acc_t, t_om, b.free)
                    x = op("dve", lambda e, b=b, ns=ns: e.tensor_tensor(GPROW[:, ns], b.ap[:, :], rb[:, ns], ALU.add), t_m, t_rb)
                    b.free = [x]
                    t_gp = op("dve", lambda e, ns=ns: e.tensor_tensor(GPROW[:, ns], GPROW[:, ns], rg[:, ns], ALU.mult), x, t_rg)
                st["xs"] = [t_gp, t_m]
            st["xs"] = st["xs"] + all_of([t for s in sgs for t in s.free])

            log_exp_tables()
            t_ss = sumsq(xh, [t_res])
            t_r = rstd_from(8, 1024, t_ss)
            gf = XS[:, 0:1024]
            t_gf = dma("sp", s_m, gf, I["final_norm_g"].rearrange("(a d) -> a d", a=1).broadcast_to([128, 1024]), t_ss)
            for t in range(8):
                x = op("dve", lambda e, t=t: e.scalar_tensor_tensor(xh[:, t, :], xh[:, t, :], RSTD[:, t:t + 1], gf, ALU.mult, ALU.mult),
                       t_r, t_gf, t_ss)
            st["rstd_r"] = [x]
            st["xs"] = [x]
            wi = I["w_in_2"][0, :, :]
            units = []
            for p in range(2):
                a, c = 2 * p, 2 * p + 1
                units.append(("g", p, [cols_of(wi, [(128 * a, 128), (512 + 128 * a, 128)]),
                                       cols_of(wi, [(128 * c, 128), (512 + 128 * c, 128)]),
                                       cols_of(wi, [(1024 + 256 * p, 256)])]))
            for h in range(4):
                o = 1536 + 128 * h
                units.append(("r", h, [cols_of(wi, [(o, 128), (o + 512, 128)]), cols_of(wi, [(o + 1024, 128), (o + 1536, 128)])]))
            units = [units[0], units[2], units[1], units[3], units[4], units[5]]
            ws = Stream([r for u in units for r in u[2]])
            ws.ahead()
            norm_in([x], lambda k: GPC[:, k:k + 1], lambda k: SHC[:, k:k + 1], waits=[t_mod])

            r2w = all_of(at_r + [(esem["pe"], count["done_pe"])])
            cos = R2[:, 0:512].rearrange("p (t i) -> p t i", t=8)
            sin = R2[:, 512:1024].rearrange("p (t i) -> p t i", t=8)
            rmk = R2[:, 1024:1536]
            qdc = R2[:, 1536:2048]
            tmpa = R2[:, 2048:2560]
            tmpb = R2[:, 2560:3072]
            YB = R2[:, 3072:4096]
            t_r2 = dma("sp", s_r2, rmk, const[:, C_RMASK:C_RMASK + 512], r2w)
            t_r2 = dma("sp", s_r2, qdc, const[:, C_QDEC:C_QDEC + 512], r2w)
            invf = tmpb[:, 0:64]
            t_r2 = dma("sp", s_r2, invf, const[:, C_INVF:C_INVF + 64], r2w)
            posi = tmpb[:, 64:72].bitcast(I32)
            t_r2 = dma("sp", s_r2, posi, I["positions_2"][0, tok0:tok0 + HT].rearrange("(t p) -> p t", p=128), r2w, slow=True)
            x = op("dve", lambda e: e.tensor_copy(POSF, posi), t_r2)
            for t in range(8):
                x = op("dve", lambda e, t=t: e.tensor_scalar(cos[:, t, :], invf, POSF[:, t:t + 1], None, ALU.mult), x, r2w)
            cf, sf = R2[:, 0:512], R2[:, 512:1024]
            magic = 12582912.0
            x = op("dve", lambda e: e.tensor_scalar(sf, cf, 1.0 / (2 * math.pi), magic, ALU.mult, ALU.add), x)
            x = op("dve", lambda e: e.tensor_scalar_add(sf, sf, -magic), x)
            for part in two_pi_parts():
                x = op("dve", lambda e, part=part: e.scalar_tensor_tensor(cf, sf, -part, cf, ALU.mult, ALU.add), x)
            lim = float(np.nextafter(np.float32(math.pi), np.float32(0)))
            x = op("dve", lambda e: e.tensor_scalar(cf, cf, lim, -lim, ALU.min, ALU.max), x)
            y = op("act", lambda e: e.activation(sf, cf, ACT.Sin), x)
            y = op("act", lambda e: e.activation(cf, cf, ACT.Sin, scale=0.5), y)
            y = op("dve", lambda e: e.tensor_tensor(cf, cf, cf, ALU.mult), y)
            t_cs = op("dve", lambda e: e.tensor_scalar(cf, cf, -2.0, 1.0, ALU.mult, ALU.add), y)

            pb = Ring([Slot(XS[:, 2048 * i:2048 * i + 2048]) for i in range(4)])
            for s in pb.slots:
                s.free = list(st["xs"])
            small = Ring([Slot(EV[:, 128 * i:128 * i + 128]) for i in range(16)])
            evf = all_of([t for v in ev for t in v.free])
            for s in small.slots:
                s.free = list(evf)
            pring = Ring(bank[0:4])
            mring = Ring(bank[4:8])
            yb = Slot(YB)
            yb.free = list(r2w)
            ystores = []
            grs = [Slot(GROW[:, 128 * i:128 * i + 128]) for i in range(2)]
            t_tmp = [t_cs]
            nun = 0

            def store_y(c0, t_y):
                d = dma("pool", s_yu[0], ys_v[:, 8 * H:8 * H + 8, c0:c0 + 128], yb.ap.rearrange("p (t e) -> p t e", t=8), t_y, yst["r"])
                yb.free = [d]
                ystores.append(d)

            def layer_norm8(src, t_src, en=128):
                ts = []
                for c in range(8):
                    y = op("dve", lambda e, c=c: e.bn_stats(BN[:, 6 * c:6 * c + 6], src(c)), t_src, st["rstd_r"])
                    ts.append(y)
                for c in range(8):
                    y = op("dve", lambda e, c=c: e.bn_aggr(MV[:, 2 * c:2 * c + 2], BN[:, 6 * c:6 * c + 6]), ts[c], st["rstd_r"])
                mv = MV.rearrange("p (c a) -> p c a", a=2)
                return rstd_from(8, 1.0, [y], src=mv[:, :, 1], tables=True)

            def load_row(src, n):
                g = grs[n % 2]
                t = dma("sp", s_gr[n % 2], g.ap, src.broadcast_to([128, 128]), g.free)
                return g, t

            def gmlp_steps(p, bufs, toks, n0):
                steps = []
                Gb = bufs[2].ap.rearrange("p (t n) -> p t n", t=8)
                for gi in range(2):
                    g = 2 * p + gi
                    B = bufs[gi].ap.rearrange("p (t n) -> p t n", t=8)
                    loc = {}

                    def s_norm(g=g, B=B, loc=loc, n=n0 + gi, gi=gi):
                        wt = small.take()
                        t_w = dma("sp", s_gw[g], wt.ap, I["gmlp_ws_2"][0, g, :, :], wt.free)
                        wt2 = small.take()
                        b = mring.take()
                        t = op("pe", lambda e: e.transpose(b.ap[:, 0:128], wt.ap, ident), t_w, b.free)
                        t = op("dve", lambda e: e.tensor_tensor(wt2.ap, b.ap[:, 0:128], caus, ALU.mult), t, wt2.free)
                        b.free = [t]
                        wt.free = [t]
                        loc["w"], loc["tw"] = wt2, t
                        row, t_row = load_row(I["gmlp_ln_g_2"][0:1, 128 * g:128 * g + 128], n)
                        t_r = layer_norm8(lambda c: B[:, c, 128:256], toks[gi] + toks[2])
                        for c in range(8):
                            t = op("dve", lambda e, c=c: e.tensor_scalar(B[:, c, 128:256], B[:, c, 128:256], MV[:, 2 * c:2 * c + 1],
                                                                          RSTD[:, c:c + 1], ALU.subtract, ALU.mult), t_r)
                            t = op("dve", lambda e, c=c: e.tensor_tensor(B[:, c, 128:256], B[:, c, 128:256], row.ap, ALU.mult), t, t_row)
                        row.free = [t]
                        st["rstd_r"] = [t]
                        loc["v"] = t
                        gs = Gb[:, :, 128 * gi:128 * gi + 128]
                        loc["g"] = op("act", lambda e: e.activation(gs, gs, ACT.Silu), toks[2])

                    def s_mix(q, g=g, B=B, loc=loc, gi=gi):
                        b = mring.take()
                        w = loc["w"]
                        t = op("pe", lambda e: e.matmul(b.ap[:, :].rearrange("p (t n) -> p t n", t=4), w.ap,
                                                        B[:, 4 * q:4 * q + 4, 128:256], start=True, stop=True),
                               loc["tw"], loc["v"], b.free)
                        us = B[:, 4 * q:4 * q + 4, 0:128]
                        t = op("dve", lambda e: e.scalar_tensor_tensor(us, b.ap[:, :].rearrange("p (t n) -> p t n", t=4),
                                                                       BSC[:, g:g + 1], us, ALU.add, ALU.mult), t)
                        b.free = [t]
                        dst = yb.ap.rearrange("p (t e) -> p t e", t=8)[:, 4 * q:4 * q + 4, :]
                        loc["y"] = op("dve", lambda e: e.tensor_tensor(dst, us, Gb[:, 4 * q:4 * q + 4, 128 * gi:128 * gi + 128],
                                                                       ALU.mult), t, loc["g"], yb.free)
                        if q == 1:
                            loc["w"].free = [loc["y"]]
                            store_y(128 * g, loc["y"])
                            bufs[gi].free = [loc["y"]]
                            if gi == 1:
                                bufs[2].free = [loc["y"]]
                    steps += [s_norm, lambda f=s_mix: f(0), lambda f=s_mix: f(1)]
                return steps

            def ret_steps(h, bufs, toks, n0):
                A = bufs[0].ap.rearrange("p (t n) -> p t n", t=8)
                B = bufs[1].ap.rearrange("p (t n) -> p t n", t=8)
                ta = tmpa.rearrange("p (t i) -> p t i", t=8)
                tb = tmpb.rearrange("p (t i) -> p t i", t=8)
                loc = {}
                cd = (1.0 - 2.0 ** (-5.0 - h)) ** 128
                S_ = ST[:, 128 * h:128 * h + 128]
                ctx_ = [dict() for _ in range(8)]

                def rot():
                    for half in range(2):
                        x1 = A[:, :, 128 * half:128 * half + 64]
                        x2 = A[:, :, 128 * half + 64:128 * half + 128]
                        t1 = op("dve", lambda e, x1=x1: e.tensor_tensor(ta, x1, sin, ALU.mult), toks[0] + t_tmp)
                        t2 = op("dve", lambda e, x2=x2: e.tensor_tensor(tb, x2, sin, ALU.mult), t_tmp)
                        t3 = op("dve", lambda e, x1=x1: e.tensor_tensor(x1, x1, cos, ALU.mult), t1)
                        t4 = op("dve", lambda e, x2=x2: e.tensor_tensor(x2, x2, cos, ALU.mult), t2)
                        t5 = op("dve", lambda e, x1=x1: e.tensor_tensor(x1, x1, tb, ALU.subtract), t3)
                        t6 = op("dve", lambda e, x2=x2: e.tensor_tensor(x2, x2, ta, ALU.add), t4)
                        t_tmp[:] = [t6]
                        loc[half] = [t5, t6]
                    loc["rot"] = [t6]
                    if H == 0:
                        state_tok[h] = [op("dve", lambda e: e.memset(S_, 0.0))]
                    loc["g"] = op("act", lambda e: e.activation(B[:, :, 128:256], B[:, :, 128:256], ACT.Silu), toks[1])

                def s_a(c):
                    x = ctx_[c]
                    b = mring.take()
                    op("pe", lambda e: e.transpose(b.ap[:, 0:128], A[:, c, 0:128], ident), loc["rot"], b.free, inc=False)
                    t = op("pe", lambda e: e.transpose(b.ap[:, 128:256], A[:, c, 128:256], ident))
                    x["qT"], x["kT"], x["qd"], x["kd"] = [small.take() for _ in range(4)]
                    t1 = op("act", lambda e: e.activation(x["qT"].ap, b.ap[:, 0:128], ACT.Copy), t, x["qT"].free)
                    t2 = op("act", lambda e: e.activation(x["kT"].ap, b.ap[:, 128:256], ACT.Copy), t1, x["kT"].free)
                    t3 = op("pool", lambda e: e.tensor_tensor(x["qd"].ap, x["qT"].ap, qdc[:, 128 * h:128 * h + 128], ALU.mult),
                            t1, x["qd"].free, t_r2)
                    t4 = op("pool", lambda e: e.tensor_scalar(x["kd"].ap, A[:, c, 128:256], KDC[:, h:h + 1], None, ALU.mult),
                            loc["rot"], x["kd"].free, consts)
                    b.free = [t2]
                    x["ta"] = [t2, t4]

                def s_b(c):
                    x = ctx_[c]
                    b = mring.take()
                    op("pe", lambda e: e.matmul(b.ap[:, 0:128], x["kT"].ap, x["qT"].ap, start=True, stop=True), x["ta"], b.free, inc=False)
                    t = op("pe", lambda e: e.matmul(b.ap[:, 128:256], x["kd"].ap, B[:, c, 0:128], start=True, stop=True), toks[1])
                    x["kT"].free = [t]
                    x["kd"].free = [t]
                    x["sm"] = small.take()
                    x["tb"] = op("dve", lambda e: e.tensor_tensor(x["sm"].ap, b.ap[:, 0:128], rmk[:, 128 * h:128 * h + 128], ALU.mult),
                                 t, x["sm"].free, t_r2)
                    x["bank"] = b

                def s_c(c):
                    x = ctx_[c]
                    b = mring.take()
                    op("pe", lambda e: e.matmul(b.ap[:, 0:128], x["sm"].ap, B[:, c, 0:128], start=True, stop=False), x["tb"], b.free, inc=False)
                    t = op("pe", lambda e: e.matmul(b.ap[:, 0:128], x["qd"].ap, S_, start=False, stop=True), state_tok[h])
                    x["sm"].free = [t]
                    x["qd"].free = [t]
                    x["qT"].free = [t]
                    kvb = x["bank"]
                    t2 = op("dve", lambda e: e.scalar_tensor_tensor(S_, S_, cd, kvb.ap[:, 128:256], ALU.mult, ALU.add), t, x["tb"])
                    kvb.free = [t2]
                    state_tok[h] = [t2]
                    t3 = op("dve", lambda e: e.tensor_copy(A[:, c, 0:128], b.ap[:, 0:128]), t)
                    b.free = [t3]
                    loc["o"] = t3

                def fin():
                    row, t_row = load_row(I["ret_gn_g_2"][0:1, 128 * h:128 * h + 128], n0)
                    t_r = layer_norm8(lambda c: A[:, c, 0:128], [loc["o"]])
                    y8 = yb.ap.rearrange("p (t e) -> p t e", t=8)
                    for c in range(8):
                        t = op("dve", lambda e, c=c: e.tensor_scalar(A[:, c, 0:128], A[:, c, 0:128], MV[:, 2 * c:2 * c + 1],
                                                                      RSTD[:, c:c + 1], ALU.subtract, ALU.mult), t_r)
                        t = op("dve", lambda e, c=c: e.tensor_tensor(A[:, c, 0:128], A[:, c, 0:128], row.ap, ALU.mult), t, t_row)
                    row.free = [t]
                    st["rstd_r"] = [t]
                    t = op("dve", lambda e: e.tensor_tensor(y8, A[:, :, 0:128], B[:, :, 128:256], ALU.mult), t, loc["g"], yb.free)
                    store_y(512 + 128 * h, t)
                    bufs[0].free = [t]
                    bufs[1].free = [t]

                steps = [rot]
                for i in range(10):
                    def one(i=i):
                        if i < 8:
                            s_a(i)
                        if 0 <= i - 1 < 8:
                            s_b(i - 1)
                        if 0 <= i - 2 < 8:
                            s_c(i - 2)
                    steps.append(one)
                return steps + [fin]

            pending = []
            for kind, idx, req in units:
                bufs, toks = [], []
                total = 8 * len(req)
                done = 0
                nsteps = len(pending)
                for _ in req:
                    slot, t_w = ws.next()
                    ws.ahead()
                    buf = None
                    for t in range(8):
                        b = pring.take()
                        t_mm = gemm_t(slot, t, b, t_w + st["big"])
                        if buf is None:
                            buf = pb.take()
                            while not isinstance(buf.free, list):
                                pending.pop(0)()
                        dst = buf.ap.rearrange("p (t n) -> p t n", t=8)[:, t, :]
                        x = op("act", lambda e, b=b, dst=dst: e.activation(dst, b.ap[:, 0:256], ACT.Copy), t_mm, buf.free)
                        b.free = [x]
                        done += 1
                        want = nsteps * done // total
                        while nsteps - len(pending) < want:
                            pending.pop(0)()
                    slot.free = [t_mm]
                    buf.free = None
                    bufs.append(buf)
                    toks.append([x])
                while pending:
                    pending.pop(0)()
                pending = gmlp_steps(idx, bufs, toks, nun) if kind == "g" else ret_steps(idx, bufs, toks, nun)
                nun += 2 if kind == "g" else 1
            ws = Stream([cols_of(I["w_out_2"][0, :, :], [(256 * i, 256)]) for i in range(4)])
            ws.ahead()
            while pending:
                pending.pop(0)()
            st["big_r"] = [t_mm]
            st["xs"] = all_of([t for s in pb.slots for t in s.free])
            for v in ev:
                v.free = all_of([t for s in small.slots for t in s.free])
            mfr = [b.free for b in bank]
            pring = Ring(bank)
            t_y = []
            for i in range(2):
                t_y.append(dma("sp", s_y, xs[:, 4 * i:4 * i + 4, :], ys_v[:, 8 * H + 4 * i:8 * H + 4 * i + 4, :],
                               ystores, st["xs"]))
            yst["r"] = [t_y[1]]
            st["big"], t_pe = transpose_in(xs, [t_y[1]] * 8, lambda k: None)
            st["xs"] = [t_pe]
            zs = []

            def sink(i, t, b, t_mm):
                dst = xs[:, t, 256 * i:256 * i + 256]
                x = op("act", lambda e: e.activation(dst, b.ap[:, 0:256], ACT.Copy), t_mm, st["xs"])
                b.free = [x]
                return x
            st["big_r"] = [residual_gemm(ws, 4, zs)]
            junk = R2[:, 2048:3072]
            t_ss = []
            for t in range(8):
                t_ss.append(op("act", lambda e, t=t: e.activation(junk, xs[:, t, :], ACT.Square, accum_out=SS[:, t:t + 1]),
                               zs[-1:], st["rstd_r"], t_tmp, t_ss[-1:]))
            t_r = rstd_from(8, 1024, t_ss, tables=True)
            outs = []
            for t in range(8):
                x = op("dve", lambda e, t=t: e.scalar_tensor_tensor(xs[:, t, :], xs[:, t, :], RSTD[:, t:t + 1], GPROW[:, :],
                                                                    ALU.mult, ALU.mult), t_r, t_gp, zs[-1:])
                y = op("pool", lambda e, t=t: e.tensor_tensor(xs[:, t, :], xs[:, t, :], xh[:, t, :], ALU.add), x)
                outs.append(dma("sp", s_out, o_v[:, 8 * H + t, :], xs[:, t, :], y))
            st["rstd_r"] = [x]
            st["xs"] = [outs[-1]]
            t_xfree = [y]
            at_free["t"] = all_of([yb.free[0], t_ss[-1], (esem["pe"], count["done_pe"]), (esem["dve"], count["done_dve"]),
                                   (esem["pool"], count["done_pool"]), (esem["act"], count["done_act"])])

        ends = [(s, count[s[0]]) for s in s_st + s_ev + s_o + s_yu + [s_us, s_out] if count[s[0]]]

        block = ctx.enter_context(nc.Block())

        def play(e, name):
            seen = {}
            for waits, f, inc in queues[name]:
                for w in waits:
                    if w is None:
                        continue
                    s, v = w
                    if seen.get(s[0], 0) < v:
                        e.wait_ge(s[1], v)
                        seen[s[0]] = v
                r = f(e)
                if inc:
                    r.then_inc(*inc)

        @block.tensor
        def _(e):
            play(e, "pe")

        @block.scalar
        def _(e):
            play(e, "act")

        @block.vector
        def _(e):
            play(e, "dve")

        @block.gpsimd
        def _(e):
            play(e, "pool")

        @block.sync
        def _(e):
            play(e, "sp")
            for s, v in ends:
                e.wait_ge(s[1], v)


_INS = ["x", "norm1_g", "w_in", "pool_w", "pool_scale", "lam_q1", "lam_k1", "lam_q2", "lam_k2", "diff_norm_g",
        "sb_norm_g", "w_out", "norm2_g", "w_gate", "w_up", "w_down", "final_norm_g", "c_2", "positions_2", "w_ada_2",
        "b_ada_2", "g_pre_2", "w_in_2", "gmlp_ln_g_2", "gmlp_ws_2", "gmlp_bs_2", "ret_gn_g_2", "w_out_2", "g_post_2"]


def kernel(**inputs):
    import concourse.bacc as bacc
    from concourse.bass_utils import run_bass_kernel_spmd

    nc = bacc.Bacc("TRN2", target_bir_lowering=False, num_devices=1)
    arrays, aps = {}, {}
    for name in _INS:
        a = np.ascontiguousarray(inputs[name])
        arrays[f"in_{name}"] = a
        aps[name] = nc.dram_tensor(f"in_{name}", a.shape, mybir.dt.from_np(a.dtype), kind="ExternalInput").ap()
    arrays["shape_constants"] = shape_constants()
    const = nc.dram_tensor("shape_constants", [128, C_END], F32, kind="ExternalInput").ap()
    out = nc.dram_tensor("out_0", [1, S, D], F32, kind="ExternalOutput").ap()
    scr = {}
    for name, shape in (("QS", [2, 6, 128, S]), ("KS", [2, 6, 128, S]), ("VS", [2, 6, S, 128]),
                        ("US", [2, 128, S + 16]), ("YS", [S, D])):
        scr[name] = nc.dram_tensor("scratch_" + name, shape, F32, kind="Internal").ap()
    build(nc, aps, const, out, scr)
    r = run_bass_kernel_spmd(nc, [arrays], core_ids=[0])
    return r.results[0]["out_0"]
```

```python
import math
from contextlib import ExitStack

import numpy as np

import concourse.bass as bass
from concourse import mybir

F32 = mybir.dt.float32
FR = mybir.dt.float32r
I32 = mybir.dt.int32
ACT = mybir.ActivationFunctionType
ALU = mybir.AluOpType
AX = mybir.AxisListType.X

S = 2048
HT = 1024
D = 1024
NKT = 8
EPS = 1e-6
BIGV = 3.0e38
NEGV = -1.0e30
C_IDENT, C_DMASK, C_SBMIN, C_SBMUL, C_CAUS = 0, 128, 256, 384, 512
C_RMASK, C_QDEC, C_KDEC, C_INVF, C_ICNT, C_IW = 640, 1152, 1664, 1668, 1732, 1764
C_END = 1766


def shape_constants():
    c = np.zeros((128, C_END), np.float32)
    i = np.arange(128)
    q, k = i[:, None], i[None, :]
    c[:, C_IDENT:C_IDENT + 128] = np.eye(128)
    c[:, C_DMASK:C_DMASK + 128] = np.where(k <= q, BIGV, NEGV)
    c[:, C_SBMIN:C_SBMIN + 128] = np.where(k < q, BIGV, NEGV)
    c[:, C_SBMUL:C_SBMUL + 128] = np.where(k < q, 1.0, 0.0)
    c[:, C_CAUS:C_CAUS + 128] = np.where(q <= k, 1.0, 0.0)
    for h in range(4):
        lg = math.log(1.0 - 2.0 ** (-5.0 - h))
        diff = k - q
        sc = 128.0 ** -0.5
        c[:, C_RMASK + 128 * h:C_RMASK + 128 * h + 128] = np.where(diff >= 0, np.exp(np.maximum(diff, 0) * lg), 0.0) * sc
        c[:, C_QDEC + 128 * h:C_QDEC + 128 * h + 128] = np.exp((k + 1.0) * lg)
        c[:, C_KDEC + h] = np.exp((127.0 - i) * lg) * sc
    e = (np.arange(64, dtype=np.float32) / np.float32(64)).astype(np.float32)
    c[:, C_INVF:C_INVF + 64] = (np.float32(1.0) / np.power(np.float32(10000.0), e).astype(np.float32))[None, :]
    for t in range(2):
        for part in range(2):
            w = (2, 4, 8, 16)[2 * t + part]
            rows = slice(64 * part, 64 * part + 64)
            c[rows, C_ICNT + 16 * t:C_ICNT + 16 * t + 16] = (1.0 / np.minimum(np.arange(16) + 1, w))[None, :]
            c[rows, C_IW + t] = 1.0 / w
    return c


def two_pi_parts():
    left, parts = 2 * math.pi, []
    for _ in range(3):
        e = math.floor(math.log2(left)) - 7
        p = math.floor(left / 2.0 ** e) * 2.0 ** e
        parts.append(p)
        left -= p
    return parts + [left]


class Slot:

    def __init__(self, ap):
        self.ap = ap
        self.free = []


class Ring:
    def __init__(self, slots):
        self.slots = slots
        self.n = 0

    def take(self):
        s = self.slots[self.n % len(self.slots)]
        self.n += 1
        return s


def build(nc, I, const, out, scr):
    queues = {k: [] for k in ("pe", "act", "dve", "pool", "sp")}
    count = {}

    with ExitStack() as ctx:
        def sem(name):
            s = ctx.enter_context(nc.semaphore(name))
            count[name] = 0
            return (name, s)

        esem = {k: sem("done_" + k) for k in ("pe", "act", "dve", "pool")}

        def op(e, f, *waits, inc=True):
            flat = []
            for w in waits:
                flat += w if isinstance(w, list) else [w]
            queues[e].append((flat, f, (esem[e][1], 1) if inc else None))
            if inc:
                count[esem[e][0]] += 1
                return (esem[e], count[esem[e][0]])
            return None

        def dma(e, s, o, i, *waits, slow=False):
            flat = []
            for w in waits:
                flat += w if isinstance(w, list) else [w]
            queues[e].append((flat, lambda g: g.dma_start(o, i, allow_slow_non_contiguous=slow), (s[1], 16)))
            count[s[0]] += 16
            return (s, count[s[0]])

        def sbt(name, n, dt=F32, stack=ctx):
            return stack.enter_context(nc.sbuf_tensor(name, [128, n], dt))

        BIG = sbt("BIG", 16384, FR)
        XH = sbt("XH", 8192)
        XS = sbt("XS", 8192)
        WF = sbt("WF", 8192, FR)
        RAW = sbt("RAW", 3072)
        EV = sbt("EV", 2048)
        CB = sbt("CB", 640)
        ST = sbt("ST", 512)
        GROW = sbt("GROW", 256)
        GPROW = sbt("GPROW", 1024)
        SM = sbt("SM", 592)
        with ExitStack() as lay:
            AT = sbt("AT", 4096, FR, lay)
        with ExitStack() as lay:
            R2 = sbt("R2", 4096, F32, lay)
        PS = [ctx.enter_context(nc.psum_tensor(f"PS{i}", [128, 512], F32)) for i in range(8)]
        bank = [Slot(p) for p in PS]

        def smc(a, n):
            return SM[:, a:a + n]
        G1C, G2C, GPC = smc(0, 8), smc(8, 8), smc(16, 8)
        SHC, SCC = smc(24, 8), smc(32, 8)
        PSC, DGC, SGC = smc(40, 2), smc(42, 1), smc(43, 1)
        BSC, CC = smc(44, 4), smc(48, 8)
        NLAM, LT = smc(56, 1), smc(57, 4)
        SS, RV, RT = smc(64, 16), smc(80, 16), smc(96, 16)
        RSTD = smc(112, 16)
        MX, NM, SUMS, SC2 = smc(480, 32), smc(512, 32), smc(544, 32), smc(576, 16)
        POSF, ONE = smc(192, 8), smc(200, 1)
        BN, MV = smc(208, 48), smc(256, 16)
        IWC = smc(272, 2)
        ICN = smc(280, 32)
        KDC = smc(312, 4)
        MODC = smc(320, 16)
        LAMV = smc(336, 128)
        LAMD = smc(464, 1)
        LAME = smc(468, 4)
        ident = CB[:, C_IDENT:C_IDENT + 128]
        dmask = CB[:, C_DMASK:C_DMASK + 128]
        sbmin = CB[:, C_SBMIN:C_SBMIN + 128]
        sbmul = CB[:, C_SBMUL:C_SBMUL + 128]
        caus = CB[:, C_CAUS:C_CAUS + 128]

        s_c = sem("s_const")
        s_raw = [sem(f"s_raw{i}") for i in range(3)]
        s_kv = [sem(f"s_kv{i}") for i in range(2)]
        s_q = [sem(f"s_q{i}") for i in range(4)]
        s_x = [sem(f"s_x{i}") for i in range(2)]
        s_y = [sem(f"s_y{i}") for i in range(2)]
        s_yf = sem("s_yf")
        s_u = sem("s_u")
        s_kk = [sem(f"s_kk{i}") for i in range(2)]
        s_m = sem("s_m")
        s_r2 = sem("s_r2")
        s_gw = [sem(f"s_gw{i}") for i in range(4)]
        s_gr = [sem(f"s_gr{i}") for i in range(2)]
        s_ada = [sem(f"s_ada{i}") for i in range(2)]
        s_ev = [sem(f"s_ev{i}") for i in range(4)]
        s_o = [sem(f"s_o{i}") for i in range(2)]
        s_us = sem("s_us")
        s_yu = [sem(f"s_yu{i}") for i in range(2)]
        s_out = [sem(f"s_out{i}") for i in range(2)]

        def col(v, k):
            return v.rearrange("(k p) -> p k", p=128)

        early_x = [dma("sp", s_x[0], XH[:, 1024 * t:1024 * t + 1024], I["x"][0, 128 * t:128 * t + 128, :]) for t in range(4)]
        dma("sp", s_c, CB[:, :], const[:, 0:640])
        dma("sp", s_c, KDC, const[:, C_KDEC:C_KDEC + 4])
        dma("sp", s_c, ICN, const[:, C_ICNT:C_ICNT + 32])
        dma("sp", s_c, IWC, const[:, C_IW:C_IW + 2])
        dma("sp", s_c, G1C, col(I["norm1_g"][0, :], 8), slow=True)
        dma("sp", s_c, G2C, col(I["norm2_g"][0, :], 8), slow=True)
        dma("sp", s_c, GPC, col(I["g_pre_2"][0, :], 8), slow=True)
        dma("sp", s_c, SHC, col(I["b_ada_2"][0, 0:1024], 8), slow=True)
        dma("sp", s_c, SCC, col(I["b_ada_2"][0, 1024:2048], 8), slow=True)
        dma("sp", s_c, CC, col(I["c_2"][0, :], 8), slow=True)
        dma("sp", s_c, PSC, col(I["pool_scale"][0, :], 2), slow=True)
        dma("sp", s_c, DGC, col(I["diff_norm_g"][0, :], 1), slow=True)
        sg = I["sb_norm_g"].rearrange("a d -> d a")
        dma("sp", s_c, SGC[0:64, :], sg, slow=True)
        dma("sp", s_c, SGC[64:128, :], sg, slow=True)
        dma("sp", s_c, BSC, I["gmlp_bs_2"][0, :, :].rearrange("g t -> t g"), slow=True)
        for i, n in enumerate(("lam_q1", "lam_k1")):
            dma("sp", s_c, LAMV[:, 64 * i:64 * i + 64], I[n][0:1, :].broadcast_to([128, 64]))
        consts = (s_c, count["s_const"])

        queues["act"].append(([], lambda e: e.preload_act_table_set("natural_log_exp_and_others"), None))
        t_one = op("dve", lambda e: e.memset(ONE, 1.0))
        t_l = op("dve", lambda e: e.tensor_tensor(LAMV[:, 0:64], LAMV[:, 0:64], LAMV[:, 64:128], ALU.mult), consts)
        t_l1 = op("dve", lambda e: e.reduce_sum(LAME[:, 0:1], LAMV[:, 0:64], AX), t_l)
        for i, n in enumerate(("lam_q2", "lam_k2")):
            t_lm = dma("sp", s_m, LAMV[:, 64 * i:64 * i + 64], I[n][0:1, :].broadcast_to([128, 64]), t_l1)
        t_l = op("dve", lambda e: e.tensor_tensor(LAMV[:, 0:64], LAMV[:, 0:64], LAMV[:, 64:128], ALU.mult), t_lm, t_l1)
        t_l2 = op("dve", lambda e: e.reduce_sum(LAME[:, 1:2], LAMV[:, 0:64], AX), t_l)
        t_e = op("act", lambda e: e.activation(LAME[:, 2:4], LAME[:, 0:2], ACT.Exp), t_l1, t_l2)
        t_d = op("dve", lambda e: e.tensor_tensor(LAMD, LAME[:, 3:4], LAME[:, 2:3], ALU.subtract), t_e)
        lam_init = 0.8 - 0.6 * math.exp(-0.3 * 0)
        t_nlam = op("dve", lambda e: e.tensor_scalar_add(NLAM, LAMD, -lam_init), t_d)
        t_dg = op("dve", lambda e: e.tensor_scalar_mul(DGC, DGC, 1.0 - lam_init), consts)

        raw = [Slot(RAW[:, 1024 * i:1024 * i + 1024]) for i in range(3)]
        wslot = [Slot((WF[:, 4096 * i:4096 * i + 2048], WF[:, 4096 * i + 2048:4096 * i + 4096])) for i in range(2)]
        wr = {"raw": 0, "slot": 0}

        def wprep(pieces):
            s = wslot[wr["slot"] % 2]
            wr["slot"] += 1
            hi, lo = s.ap
            toks = []
            for i in range(2):
                n = wr["raw"] % 3
                wr["raw"] += 1
                r = raw[n]
                for d, src in pieces(i, r.ap):
                    t_in = dma("sp", s_raw[n], d, src, r.free)
                h = hi[:, 1024 * i:1024 * i + 1024]
                l = lo[:, 1024 * i:1024 * i + 1024]
                t_hi = op("act", lambda e, h=h, r=r: e.activation(h, r.ap, ACT.Copy), t_in, s.free)
                t_lo = op("pool", lambda e, h=h, r=r, l=l: e.tensor_tensor(l, r.ap, h.bitcast(F32), ALU.subtract),
                          t_hi, t_in, s.free)
                r.free = [t_lo, t_hi]
                toks.append(t_lo)
            s.free = []
            return s, toks[1:] + [t_hi]

        def cols_of(W, segs):
            Wv = W.rearrange("(k p) n -> p k n", p=128)

            def pieces(i, r):
                rv = r.rearrange("p (k n) -> p k n", k=4)
                at, res = 0, []
                for c0, n in segs:
                    res.append((rv[:, :, at:at + n], Wv[:, 4 * i:4 * i + 4, c0:c0 + n]))
                    at += n
                return res
            return pieces

        def rows_of(W, r0):
            def pieces(i, r):
                return [(r, W[r0 + 128 * i:r0 + 128 * i + 128, :])]
            return pieces

        class Stream:
            def __init__(self, reqs):
                self.reqs = list(reqs)
                self.ready = []

            def ahead(self):
                if self.reqs and len(self.ready) < 2:
                    self.ready.append(wprep(self.reqs.pop(0)))

            def next(self):
                if not self.ready:
                    self.ahead()
                return self.ready.pop(0)

        bigh = BIG[:, 0:8192].rearrange("p (k t) -> p k t", k=8)
        bigl = BIG[:, 8192:16384].rearrange("p (k t) -> p k t", k=8)
        xh = XH[:, :].rearrange("p (t d) -> p t d", t=8)
        xs = XS[:, :].rearrange("p (t d) -> p t d", t=8)
        ev = [Slot(EV[:, 512 * i:512 * i + 512]) for i in range(4)]
        ring_ev = Ring(ev)
        pring = Ring(bank)

        def split_psum(b, t_mm, hi, lo, scale=None, bias=None, waits=[], w=512):
            v = ring_ev.take()
            src = b.ap[:, 0:w]
            tmp = v.ap[:, 0:w]
            if scale is None:
                t = op("dve", lambda e: e.tensor_copy(tmp, src), t_mm, v.free)
            elif bias is None:
                t = op("dve", lambda e: e.tensor_scalar(tmp, src, scale, None, ALU.mult), t_mm, v.free, waits)
            else:
                t = op("dve", lambda e: e.tensor_scalar(tmp, src, scale, bias, ALU.mult, ALU.add), t_mm, v.free, waits)
            b.free = [t]
            t_hi = op("act", lambda e: e.activation(hi, tmp, ACT.Copy), t, waits)
            t_lo = op("pool", lambda e: e.tensor_tensor(lo, tmp, hi.bitcast(F32), ALU.subtract), t_hi, waits)
            v.free = [t_hi, t_lo]
            return t_hi, t_lo

        def log_exp_tables():
            queues["act"].append(([], lambda e: e.preload_act_table_set("natural_log_exp_and_others"), None))

        def rstd_from(n, width, t_ss, src=SS, tables=False, c0=0):
            if tables:
                log_exp_tables()
            v, r, t, = RV[:, c0:c0 + n], RSTD[:, c0:c0 + n], RT[:, c0:c0 + n]
            a = op("dve", lambda e: e.tensor_scalar(v, src[:, c0:c0 + n] if src is SS else src, 1.0 / width, EPS, ALU.mult, ALU.add), t_ss)
            b = op("act", lambda e: e.activation(r, v, ACT.Ln), a)
            b = op("act", lambda e: e.activation(r, r, ACT.Exp, scale=-0.5), b)
            c = op("dve", lambda e: e.tensor_tensor(t, r, r, ALU.mult), b)
            c = op("dve", lambda e: e.tensor_tensor(t, t, v, ALU.mult), c)
            c = op("dve", lambda e: e.tensor_scalar(t, t, -0.5, 1.5, ALU.mult, ALU.add), c)
            return op("dve", lambda e: e.tensor_tensor(r, r, t, ALU.mult), c)

        def all_of(toks):
            best = {}
            for s, v in toks:
                if s[0] not in best or best[s[0]][1] < v:
                    best[s[0]] = (s, v)
            return list(best.values())

        st = {"big": {0: [], 1: []}, "xs": [], "big_r": [], "rstd_r": []}
        late = []
        MIXED = ("act", "dve", "act", "dve")

        def flush():
            while late:
                late.pop(0)()

        def square(src8, t, rdy, junk=None):
            j = xs[:, t, :] if junk is None else junk
            return op("act", lambda e: e.activation(j, src8[:, t, :], ACT.Square, accum_out=SS[:, t:t + 1]),
                      rdy, st["xs"], st["rstd_r"])

        def scaled4(g, t_sq, engines=("dve",) * 4, waits=[]):
            t_r = rstd_from(4, 1024, t_sq, c0=4 * g)
            toks = []
            for t in range(4 * g, 4 * g + 4):
                if engines[t % 4] == "act":
                    toks.append(op("act", lambda e, t=t: e.activation(xs[:, t, :], xh[:, t, :], ACT.Identity, scale=RSTD[:, t:t + 1]),
                                   t_r, t_sq, waits))
                else:
                    toks.append(op("dve", lambda e, t=t: e.tensor_scalar(xs[:, t, :], xh[:, t, :], RSTD[:, t:t + 1], None,
                                                                         ALU.mult), t_r, t_sq, waits))
            st["rstd_r"] = all_of(st["rstd_r"] + toks)
            return toks

        def split_direct(b, t_pe, hi, lo, scale, bias, waits, k):
            if bias is not None:
                v = ring_ev.take()
                t = op("dve", lambda e: e.tensor_scalar(v.ap, b.ap[:, :], scale, bias, ALU.mult, ALU.add), t_pe, v.free, waits)
                b.free = [t]
                t_hi = op("act", lambda e: e.activation(hi, v.ap, ACT.Copy), t, waits)
                t_lo = op("dve" if k % 2 else "pool", lambda e: e.tensor_tensor(lo, v.ap, hi.bitcast(F32), ALU.subtract), t_hi, t, waits)
                v.free = [t_hi, t_lo]
                return [t_hi, t_lo]
            t_hi = op("act", lambda e: e.activation(hi, b.ap[:, :], ACT.Identity, scale=scale), t_pe, waits)
            t_lo = op("dve", lambda e: e.scalar_tensor_tensor(lo, b.ap[:, :], scale, hi.bitcast(F32), ALU.mult, ALU.subtract),
                      t_hi, t_pe, waits)
            b.free = [t_hi, t_lo]
            return [t_hi, t_lo]

        def transpose4(g, t_src, scale_col, bias_col=None, waits=[], by_k={}):
            toks = []
            for k in range(8):
                b = pring.take()
                for t in range(4):
                    t_pe = op("pe", lambda e, b=b, t=t, k=k: e.transpose(
                        b.ap[:, 128 * t:128 * t + 128], xs[:, 4 * g + t, 128 * k:128 * k + 128], ident),
                        by_k.get(k, t_src[t]), b.free, inc=t == 3)
                hi = bigh[:, k, 512 * g:512 * g + 512]
                lo = bigl[:, k, 512 * g:512 * g + 512]
                toks += split_direct(b, t_pe, hi, lo, scale_col(k), bias_col and bias_col(k), waits, k)
            st["big"][g] = all_of(toks)
            return t_pe

        def three(e_list, o, Ah, Al, Bh, Bl, start, stop, waits, last):
            op("pe", lambda e: e.matmul(o, Ah, Bh, start=start, stop=False), waits, inc=False)
            op("pe", lambda e: e.matmul(o, Ah, Bl, start=False, stop=False), inc=False)
            return op("pe", lambda e: e.matmul(o, Al, Bh, start=False, stop=stop), inc=last)

        def gemm_f(slot, f, j, b, waits):
            wh = slot.ap[0].rearrange("p (k n) -> p k n", k=8)
            wl = slot.ap[1].rearrange("p (k n) -> p k n", k=8)
            for k in range(8):
                fs = slice(128 * f, 128 * f + 128)
                ts = slice(512 * j, 512 * j + 512)
                t = three(None, b.ap[:, :], wh[:, k, fs], wl[:, k, fs], bigh[:, k, ts], bigl[:, k, ts],
                          k == 0, k == 7, (waits + b.free) if k == 0 else [], k == 7)
            return t

        def gemm_t(slot, t, b, waits, n=256):
            wh = slot.ap[0].rearrange("p (k n) -> p k n", k=8)
            wl = slot.ap[1].rearrange("p (k n) -> p k n", k=8)
            ts = slice(128 * t, 128 * t + 128)
            for k in range(8):
                r = three(None, b.ap[:, 0:n], bigh[:, k, ts], bigl[:, k, ts], wh[:, k, 0:n], wl[:, k, 0:n],
                          k == 0, k == 7, (waits + b.free) if k == 0 else [], k == 7)
            return r

        QS, KS, VS, US, YS = scr["QS"], scr["KS"], scr["VS"], scr["US"], scr["YS"]
        w_in = I["w_in"][0, :, :]
        x_v = I["x"][0, :, :].rearrange("(t p) d -> p t d", p=128)
        o_v = out[0, :, :].rearrange("(t p) d -> p t d", p=128)
        ys_v = YS.rearrange("(t p) d -> p t d", p=128)

        def blocks_in():
            return [("u", 0, 0)] + [("q", 256 + 256 * i, i) for i in range(2)] + [("k", 768 + 256 * i, i) for i in range(2)] \
                + [("v", 1280 + 256 * i, i) for i in range(2)] + [("q", 1792, 2), ("k", 2048, 2), ("v", 2304, 2)]

        def load_x(H, t, waits):
            return dma("sp", s_x[t // 4], xh[:, t, :], x_v[:, 8 * H + t, :], waits)

        NG = 11
        ffn_order = [("g", 0), ("u", 0)]
        for g in range(1, NG):
            ffn_order += [("g", g), ("d", g - 1), ("u", g)]
        ffn_order.append(("d", NG - 1))
        wi = I["w_in_2"][0, :, :]
        units = []
        for p in range(2):
            a, c = 2 * p, 2 * p + 1
            units.append(("g", p, [cols_of(wi, [(128 * a, 128), (512 + 128 * a, 128)]),
                                   cols_of(wi, [(128 * c, 128), (512 + 128 * c, 128)]),
                                   cols_of(wi, [(1024 + 256 * p, 256)])]))
        for h in range(4):
            o = 1536 + 128 * h
            units.append(("r", h, [cols_of(wi, [(o, 128), (o + 512, 128)]), cols_of(wi, [(o + 1024, 128), (o + 1536, 128)])]))
        units = [units[0], units[2], units[1], units[3], units[4], units[5]]

        def reqs_in():
            return [cols_of(w_in, [(c, 256)]) for _, c, _ in blocks_in()]

        def reqs_after(H):
            wg, wu, wd = I["w_gate"][0, :, :], I["w_up"][0, :, :], I["w_down"][0, :, :]
            r = [cols_of(I["w_out"][0, :, :], [(256 * i, 256)]) for i in range(4)]
            for kind, g in ffn_order:
                r.append(rows_of(wd, 256 * g) if kind == "d" else cols_of(wg if kind == "g" else wu, [(256 * g, 256)]))
            r += [q for u in units for q in u[2]]
            r += [cols_of(I["w_out_2"][0, :, :], [(256 * i, 256)]) for i in range(4)]
            return r + (reqs_in() if H == 0 else [])

        ws = Stream(reqs_in())
        ws.ahead()
        xload = early_x + [load_x(0, t, []) for t in range(4, 8)]
        uhist = {"done": []}
        yst = {"r": []}
        state_tok = {}

        staged = Ring([Slot((AT[:, 1024 * i:1024 * i + 512], AT[:, 1024 * i + 512:1024 * i + 1024])) for i in range(4)])
        s_st = [sem(f"s_st{i}") for i in range(4)]

        def store_parts(n, s, t_hi, t_lo, dh, dl, view=lambda a: a):
            a = dma("sp", s_st[n], dh, view(s.ap[0]).bitcast(F32), t_hi)
            b = dma("sp", s_st[n], dl, view(s.ap[1]).bitcast(F32), t_lo)
            s.free = [b]
            return b

        at_free = {"t": []}

        NU = 1040
        pool_st = {}
        pua = [XS[:, NU * f:NU * f + NU] for f in range(2)]
        pbuf = [XS[:, NU * (2 + f):NU * (3 + f)] for f in range(2)]
        pls = [XS[:, 4 * NU + 1024 * f:4 * NU + 1024 * f + 1024] for f in range(2)]
        pw = XS[:, 8192 - 256:8192]

        def pool_sums(H):
            free = [st["xs_pe"]]
            t_z = op("dve", lambda e: e.memset(pw, 0.0), free)
            for f in range(2):
                for g in range(2):
                    t_pw = dma("sp", s_u, pw[64 * g:64 * g + 64, 128 * f + 64 * g:128 * f + 64 * g + 64],
                               I["pool_w"][0, 2 * f + g, :, :], t_z)
            for f in range(2):
                t_in = dma("sp", s_u, pua[f], US[f, :, HT * H:HT * H + NU], pool_st["u"], uhist["done"], free)
            pool_st["in"] = [t_in]
            pool_st["pl"] = []
            for f in range(2):
                ua, pl = pua[f], pls[f]
                lo_w, hi_w = ((2, 4), (8, 16))[f]
                src, steps, w, t = ua, 0, 1, t_in
                while w < hi_w:
                    dst, w0, s0 = pbuf[steps % 2], w, 2 * w - 1
                    t = op("dve", lambda e, dst=dst, src=src, w0=w0, s0=s0: e.tensor_tensor(
                        dst[:, s0:NU], src[:, s0:NU], src[:, s0 - w0:NU - w0], ALU.add), t, free)
                    w *= 2
                    steps += 1
                    src = dst
                    if w == lo_w:
                        t = op("dve", lambda e, dst=dst, pl=pl: e.tensor_copy(pl[0:64, :], dst[0:64, 16:NU]), t)
                    if w == hi_w:
                        t = op("dve", lambda e, dst=dst, pl=pl: e.tensor_copy(pl[64:128, :], dst[64:128, 16:NU]), t)
                if H == 0:
                    t = op("dve", lambda e, pl=pl, f=f: e.tensor_tensor(pl[:, 0:16], pl[:, 0:16], ICN[:, 16 * f:16 * f + 16], ALU.mult), t, consts)
                    t = op("dve", lambda e, pl=pl, f=f: e.tensor_scalar(pl[:, 16:1024], pl[:, 16:1024], IWC[:, f:f + 1], None, ALU.mult), t)
                else:
                    t = op("dve", lambda e, pl=pl, f=f: e.tensor_scalar(pl, pl, IWC[:, f:f + 1], None, ALU.mult), t)
                t = op("dve", lambda e, pl=pl, ua=ua: e.tensor_tensor(pl, pl, ua[:, 16:NU], ALU.subtract), t)
                pool_st["pl"].append(t)

        def pool_products():
            pool_st["o"] = []
            for f in range(2):
                for j in range(2):
                    b = pring.take()
                    for t in range(4):
                        t_mm = op("pe", lambda e, b=b, t=t, j=j, f=f: e.matmul(
                            b.ap[:, 128 * t:128 * t + 128], pls[f][:, 512 * j + 128 * t:512 * j + 128 * t + 128],
                            pw[:, 128 * f:128 * f + 128], start=True, stop=True, skip_group_check=True),
                            pool_st["pl"][f], pool_st["in"], b.free, inc=t == 3)
                    t = op("dve", lambda e, b=b, j=j, f=f: e.tensor_copy(pua[f][:, 512 * j:512 * j + 512], b.ap[:, :]), t_mm)
                    b.free = [t]
                pool_st["o"].append(t)
            pool_st["mm"] = [t_mm]

        def pool_store(H):
            for f in range(2):
                d = dma("sp", s_us, ys_v[:, 8 * H:8 * H + 8, 128 * f:128 * f + 128],
                        pua[f][:, 0:1024].rearrange("p (t e) -> p t e", t=8), pool_st["o"][f], yst["r"])
            pool_st["out"] = [d]

        zt = op("dve", lambda e: e.memset(EV[:, 0:16], 0.0))
        for f in range(2):
            zd = dma("sp", s_us, US[f, :, 0:16], EV[:, 0:16], zt)
        ev[0].free = [zd]
        uhist["done"] = [zd]

        for H in range(2):
            tok0 = H * HT
            blocks = blocks_in()
            t_pe = None
            for g in range(2):
                rdy = [xload[4 * g + 3]]
                xw = outs_g[g] if H else []
                t_sq = [square(xh, t, rdy + xw) for t in range(4 * g, 4 * g + 4)]
                tk = scaled4(g, t_sq, MIXED, waits=rdy)
                big_r = list(st["big_r"])

                def tr_x(g=g, tk=tk, big_r=big_r):
                    st["xs_pe"] = transpose4(g, tk, lambda k: G1C[:, k:k + 1], waits=big_r + [consts])
                if g == 0:
                    tr_x()
                else:
                    late.append(tr_x)
            for s in staged.slots:
                s.free = list(at_free["t"])
            stores = []
            nblk = 0
            for kind, c0, idx in blocks:
                slot, t_w = ws.next()
                ws.ahead()
                last = []
                if kind in "uqk":
                    for j in range(2):
                        for f in range(2):
                            if j:
                                flush()
                            b = pring.take()
                            t_mm = gemm_f(slot, f, j, b, t_w + st["big"][j])
                            last = [t_mm]
                            sl = slice(tok0 + 512 * j, tok0 + 512 * j + 512)
                            if kind == "u":
                                v = ring_ev.take()
                                n = ev.index(v)
                                t = op("dve", lambda e, v=v, b=b: e.tensor_copy(v.ap, b.ap[:, :]), t_mm, v.free)
                                b.free = [t]
                                v.free = [dma("sp", s_ev[n], US[f, :, 16 + sl.start:16 + sl.stop], v.ap, t)]
                                stores.append(v.free[0])
                                pool_st["u"] = all_of(stores)
                            else:
                                n = staged.n % 4
                                s = staged.take()
                                ft = 2 * idx + f
                                t_hi, t_lo = split_psum(b, t_mm, s.ap[0], s.ap[1], 0.125 if kind == "q" else None,
                                                        waits=list(s.free))
                                Z = QS if kind == "q" else KS
                                stores.append(store_parts(n, s, t_hi, t_lo, Z[0, ft, :, sl], Z[1, ft, :, sl]))
                else:
                    for t2 in range(4):
                        b = pring.take()
                        n = staged.n % 4
                        s = staged.take()
                        for u in range(2):
                            wh = slot.ap[0].rearrange("p (k n) -> p k n", k=8)
                            wl = slot.ap[1].rearrange("p (k n) -> p k n", k=8)
                            ts = slice(128 * (2 * t2 + u), 128 * (2 * t2 + u) + 128)
                            for k in range(8):
                                t_mm = three(None, b.ap[:, 256 * u:256 * u + 256], bigh[:, k, ts], bigl[:, k, ts],
                                             wh[:, k, :], wl[:, k, :], k == 0, k == 7,
                                             (t_w + b.free) if k == 0 and u == 0 else [], k == 7 and u == 1)
                        last = [t_mm]
                        t_hi, t_lo = split_psum(b, t_mm, s.ap[0], s.ap[1], waits=list(s.free))
                        r0 = tok0 + 256 * t2
                        for f in range(2):
                            dst = [VS[p, 2 * idx + f, r0:r0 + 256, :].rearrange("(u p) e -> p u e", p=128) for p in range(2)]
                            view = lambda a, f=f: a.rearrange("p (u n) -> p u n", u=2)[:, :, 128 * f:128 * f + 128]
                            stores.append(store_parts(n, s, t_hi, t_lo, dst[0], dst[1], view))
                slot.free = last
                nblk += 1
                if nblk == 3:
                    pool_sums(H)
                elif nblk == 6:
                    pool_products()
                elif nblk == 8:
                    pool_store(H)
            st["big_r"] = last
            st["xs"] = all_of(pool_st["out"] + pool_st["mm"])
            stores = all_of(stores)
            nk0 = 8 * H
            kvs = [Slot(BIG[:, 8192 * i:8192 * i + 8192]) for i in range(2)]
            for s in kvs:
                s.free = list(st["big_r"])
            qsl = [Slot(AT[:, 1024 * i:1024 * i + 1024]) for i in range(4)]
            for s in qsl:
                s.free = list(stores)
            tr = Ring([Slot(WF[:, 1024 * i:1024 * i + 1024]) for i in range(8)])
            for s in tr.slots:
                s.free = list(st["big_r"])
            ob = [Slot(EV[:, 1024 * i:1024 * i + 1024]) for i in range(2)]
            ob[0].free = ev[0].free + ev[1].free
            ob[1].free = ev[2].free + ev[3].free
            traw = Ring([Slot(RAW[:, 512 * i:512 * i + 512]) for i in range(6)])
            for i, v in enumerate(traw.slots):
                v.free = list(raw[i // 2].free)
            sring = Ring(bank[0:5])
            tring = Ring(bank[5:7])
            oring = Ring(bank[7:8])
            L = tok0 + HT
            ystores = list(pool_st["out"])

            def load_head(j, between=lambda: None):
                kv = kvs[j % 2]
                kk = kv.ap[:, 0:4096].rearrange("p (r t) -> p r t", r=2)
                vv = kv.ap[:, 4096:8192].rearrange("p (t a e) -> p t a e", a=2, e=128)
                for a in range(2):
                    tk = dma("sp", s_kk[j % 2], kk[64 * a:64 * a + 64, :, 0:L].bitcast(F32),
                             KS[a, j, :, 0:L].rearrange("(r d) t -> d r t", r=2), stores, kv.free)
                between()
                for a in range(2):
                    tv = dma("sp", s_kv[j % 2], vv[:, 0:L // 128, a, :].bitcast(F32),
                             VS[a, j, 0:L, :].rearrange("(t p) e -> p t e", p=128), stores, kv.free)
                kv.free = []
                return kk, vv, [tk], kv, [tv]

            queries = {}

            def load_queries(j, h):
                n = (4 * j + h) % 4
                q = qsl[n]
                qq = q.ap.rearrange("p (a r t) -> p a r t", a=2, r=2)
                t0 = tok0 + 256 * h
                for a in range(2):
                    for d in range(2):
                        t = dma("sp", s_q[n], qq[64 * d:64 * d + 64, a, :, :].bitcast(F32),
                                QS[a, j, :, t0:t0 + 256].rearrange("(r d) t -> d r t", r=2), stores, q.free)
                q.free = []
                queries[j, h] = (qq, t, q)

            def qk(g, c, w):
                j, qt = g["j"], g["qt"]
                kk, vv, t_ld, _, _ = heads[j]
                qq, t_q, slot = queries[j, qt // 2]
                res = []
                qs = slice(128 * (qt % 2), 128 * (qt % 2) + 128)
                ks = slice(512 * c, 512 * c + w)
                for r in range(2):
                    b = sring.take()
                    for a in range(2):
                        t = op("pe", lambda e, a=a, r=r, b=b: e.matmul(b.ap[:, 0:w], qq[:, a, r, qs], kk[:, r, ks],
                                                                      start=a == 0, stop=a == 1),
                               t_ld, t_q, b.free, inc=a == 1)
                    res.append((b, t))
                slot.free = [t]
                g["nchunk"] = g.get("nchunk", 0) + 1
                if qt % 2 and g["nchunk"] == len(chunks(nk0 + qt + 1)):
                    h = qt // 2
                    nxt = (j + 1, h) if j < 5 else None
                    if nxt:
                        load_queries(*nxt)
                return res

            def turn(src, w, t_src, hi_engine):
                b, s, v = tring.take(), tr.take(), traw.take()
                for i in range(w // 128):
                    t = op("pe", lambda e, i=i: e.transpose(b.ap[:, 128 * i:128 * i + 128],
                                                            src[:, 128 * i:128 * i + 128], ident),
                           t_src, b.free, inc=i == w // 128 - 1)
                hi, lo, tmp = s.ap[:, 0:w], s.ap[:, 512:512 + w], v.ap[:, 0:w]
                t_c = op("act", lambda e: e.activation(tmp, b.ap[:, 0:w], ACT.Copy), t, v.free)
                b.free = [t_c]
                if hi_engine == "act":
                    t_hi = op("act", lambda e: e.activation(hi, tmp, ACT.Copy), t_c, s.free)
                else:
                    t_hi = op("dve", lambda e: e.tensor_copy(hi, tmp), t_c, s.free)
                t_lo = op("pool", lambda e: e.tensor_tensor(lo, tmp, hi.bitcast(F32), ALU.subtract), t_hi, t_c, s.free)
                v.free = [t_lo]
                s.free = []
                return s, [t_hi, t_lo], t

            def pv(hd, s, t_s, c, w, o, e0, en, first, last, clear=True):
                vv = hd[1]
                for i in range(w // 128):
                    kt = 4 * c + i
                    hi, lo = s.ap[:, 128 * i:128 * i + 128], s.ap[:, 512 + 128 * i:512 + 128 * i + 128]
                    fst, lst = first and i == 0, last and i == w // 128 - 1
                    op("pe", lambda e, hi=hi, kt=kt, fst=fst: e.matmul(o.ap[:, 0:2 * en], hi, vv[:, kt, :, e0:e0 + en],
                                                                      start=fst and clear, stop=False, skip_group_check=True),
                       t_s, hd[4], o.free if fst else [], inc=False)
                    t = op("pe", lambda e, lo=lo, kt=kt, lst=lst: e.matmul(o.ap[:, 0:en], lo, vv[:, kt, 0, e0:e0 + en],
                                                                          start=False, stop=lst, skip_group_check=True),
                           inc=i == w // 128 - 1)
                s.free = [t]
                return t

            def chunks(n):
                return [(c, min(512, 128 * n - 512 * c)) for c in range((n + 3) // 4)]

            heads = {0: load_head(0, lambda: load_queries(0, 0))}
            for h in range(1, 4):
                load_queries(0, h)
            heads[1] = load_head(1)

            def finish_tile(j, O, t_o):
                o = O.ap.rearrange("p (t e) -> p t e", t=8)
                parts = 1 if j < 4 else 2
                n, en = 8 * parts, 128 // parts
                v = O.ap.rearrange("p (n e) -> p n e", n=n)
                q = SCR.rearrange("p (n e) -> p n e", n=n)
                t = op("pool", lambda e: e.tensor_tensor(SCR, O.ap, O.ap, ALU.mult), t_o, scr_free)
                t = op("dve", lambda e: e.reduce_sum(SS[:, 0:n], q, AX), t, st["rstd_r"])
                scr_free[:] = [t]
                t = rstd_from(n, en, [t])
                t = op("pool", lambda e: e.tensor_tensor(v, v, RSTD[:, 0:n].rearrange("p (n a) -> p n a", a=1).broadcast_to([128, n, en]),
                                                         ALU.mult), t, t_o)
                ts = [t]
                st["rstd_r"] = [t]
                c0 = 256 + 128 * j
                d = dma("pool", s_o[j % 2], ys_v[:, 8 * H:8 * H + 8, c0:c0 + 128], o, ts[-1], yst["r"])
                O.free = [d]
                ystores.append(d)

            pch = Ring([Slot(XS[:, 512 * i:512 * i + 512]) for i in range(14)])
            SCR = XS[:, 7168:8192]
            scr_free = list(st["xs"])
            for s in pch.slots:
                s.free = list(st["xs"])
            work = []
            for j in range(4):
                for qt in range(8):
                    g = {"j": j, "qt": qt, "m": (8 * j + qt) % 4, "nc": len(chunks(nk0 + qt + 1)), "t": []}
                    for c, w in chunks(nk0 + qt + 1):
                        work.append({"g": g, "c": c, "w": w, "first": c == 0, "last": c == g["nc"] - 1})
            mfree = {m: [] for m in range(4)}

            def df_a(x):
                g, c, w = x["g"], x["c"], x["w"]
                j, m = g["j"], g["m"]
                x["p"] = []
                for r, (b, t) in enumerate(qk(g, c, w)):
                    if x["last"]:
                        dg = b.ap[:, w - 128:w]
                        t = op("dve", lambda e, dg=dg: e.tensor_tensor(dg, dg, dmask, ALU.min), t)
                    nm = NM[:, 8 * m + 4 * r + c:8 * m + 4 * r + c + 1]
                    sm = SUMS[:, 8 * m + 4 * r + c:8 * m + 4 * r + c + 1]
                    t = op("dve", lambda e, b=b, nm=nm: e.tensor_reduce(nm, b.ap[:, 0:w], AX, ALU.max, negate=True), t, mfree[m])
                    p = pch.take()
                    t = op("act", lambda e, b=b, nm=nm, sm=sm, p=p: e.activation(p.ap[:, 0:w], b.ap[:, 0:w], ACT.Exp, bias=nm,
                                                                              accum_out=sm), t, p.free, mfree[m])
                    b.free = [t]
                    p.free = []
                    x["p"].append(p)
                    g["t"].append(t)

            def df_e(g):
                m, k = g["m"], g["nc"]
                nm = NM[:, 8 * m:8 * m + 8].rearrange("p (r c) -> p r c", r=2)[:, :, 0:k]
                sm = SUMS[:, 8 * m:8 * m + 8].rearrange("p (r c) -> p r c", r=2)[:, :, 0:k]
                f = MX[:, 8 * m:8 * m + 8].rearrange("p (r c) -> p r c", r=2)[:, :, 0:k]
                sc = SC2[:, 4 * m:4 * m + 4]
                a = op("dve", lambda e: e.tensor_reduce(sc[:, 0:2], nm, AX, ALU.min), g["t"])
                a0 = op("act", lambda e: e.activation(f[:, 0, :], nm[:, 0, :], ACT.Exp, scale=-1.0, bias=sc[:, 0:1]), a)
                a1 = op("act", lambda e: e.activation(f[:, 1, :], nm[:, 1, :], ACT.Exp, scale=-1.0, bias=sc[:, 1:2]), a)
                a = op("dve", lambda e: e.tensor_tensor(sm, sm, f, ALU.mult), a0, a1, g["t"])
                a = op("dve", lambda e: e.reduce_sum(sc[:, 2:4], sm, AX), a)
                a = op("dve", lambda e: e.reciprocal(sc[:, 2:4], sc[:, 2:4]), a)
                b0 = op("dve", lambda e: e.tensor_scalar(f[:, 0, :], f[:, 0, :], sc[:, 2:3], None, ALU.mult), a)
                b1 = op("dve", lambda e: e.tensor_scalar(f[:, 1, :], f[:, 1, :], sc[:, 3:4], NLAM, ALU.mult, ALU.mult), a, t_nlam)
                g["e"] = [b0, b1]

            def df_c(x):
                g, c, w, (p1, p2) = x["g"], x["c"], x["w"], x["p"]
                q1 = 8 * g["m"] + c
                a = op("pool", lambda e: e.tensor_scalar(p1.ap[:, 0:w], p1.ap[:, 0:w], MX[:, q1:q1 + 1], 1.0, ALU.mult, ALU.mult), g["e"], g["t"])
                a = op("dve", lambda e: e.scalar_tensor_tensor(p1.ap[:, 0:w], p2.ap[:, 0:w], MX[:, q1 + 4:q1 + 5], p1.ap[:, 0:w],
                                                               ALU.mult, ALU.add), a, g["e"])
                p2.free = [a]
                x["t"] = a
                if x["last"]:
                    mfree[g["m"]] = [a]

            def df_t(x):
                p1 = x["p"][0]
                x["s"], x["ts"], t_pe = turn(p1.ap[:, 0:x["w"]], x["w"], [x["t"]], "act")
                p1.free = [t_pe]

            def pv_stage(x, e0, en):
                g = x["g"]
                if x["first"]:
                    g["o"] = oring.take()
                o = g["o"]
                hd = heads[g["j"]]
                t = pv(hd, x["s"], x["ts"], x["c"], x["w"], o, e0, en, x["first"], x["last"])
                hd[3].free = [t]
                if x["last"]:
                    O = ob[g["j"] % 2]
                    dst = O.ap[:, 128 * g["qt"] + e0:128 * g["qt"] + e0 + en]
                    y = op("dve", lambda e: e.tensor_copy(dst, o.ap[:, 0:en]), t, O.free)
                    y = op("dve", lambda e: e.tensor_tensor(dst, o.ap[:, en:2 * en], dst, ALU.add), y)
                    o.free = [y]
                    return O, y
                return None, None

            def df_d(x):
                O, y = pv_stage(x, 0, 128)
                j = x["g"]["j"]
                if O and x["g"]["qt"] == 7:
                    heads[j + 2] = load_head(j + 2)
                    finish_tile(j, O, y)

            nwork = len(work)
            for i in range(nwork + 9):
                if i < nwork:
                    df_a(work[i])
                if 0 <= i - 1 < nwork and work[i - 1]["last"]:
                    df_e(work[i - 1]["g"])
                if 0 <= i - 5 < nwork:
                    df_c(work[i - 5])
                if 0 <= i - 8 < nwork:
                    df_d(work[i - 8])
                if 0 <= i - 6 < nwork:
                    df_t(work[i - 6])

            aslot = Ring([Slot(XS[:, 512 * i:512 * i + 512]) for i in range(10)])
            cslot = Ring([Slot(XS[:, 5120 + 512 * i:5120 + 512 * i + 512]) for i in range(4)])
            for s, p in zip(aslot.slots + cslot.slots, pch.slots):
                s.free = list(p.free)
            work = []
            for j in (4, 5):
                for qt in range(8):
                    cs = chunks(nk0 + qt + 1)[::-1]
                    g = {"j": j, "qt": qt, "carry": [None, None]}
                    for i, (c, w) in enumerate(cs):
                        work.append({"g": g, "c": c, "w": w, "first": i == 0, "last": i == len(cs) - 1})

            def sb_a(x):
                g, w = x["g"], x["w"]
                x["b"], x["a"], x["t"] = [], [], [None, None]
                for r, (b, t) in enumerate(qk(g, x["c"], w)):
                    s = aslot.take()
                    a = s.ap[:, 0:w]
                    x["t"][r] = op("act", lambda e, a=a, b=b: e.activation(a, b.ap[:, 0:w], ACT.Abs), t, s.free)
                    x["b"].append(b)
                    x["a"].append(s)
                for r in range(2):
                    a = x["a"][r].ap[:, 0:w]
                    x["t"][r] = op("act", lambda e, a=a: e.activation(a, a, ACT.Exp, scale=-1.0), x["t"][r])
                for r in range(2):
                    a = x["a"][r].ap[:, 0:w]
                    x["t"][r] = op("act", lambda e, a=a: e.activation(a, a, ACT.Ln, bias=1.0), x["t"][r])

            def sb_b(x):
                g, w = x["g"], x["w"]
                aa = [x["a"][r].ap[:, 0:w] for r in range(2)]
                t, cc, cs = [None, None], [None, None], [None, None]
                for r in range(2):
                    a, b = aa[r], x["b"][r]
                    t[r] = op("dve", lambda e, a=a, b=b: e.scalar_tensor_tensor(a, b.ap[:, 0:w], 0.0, a, ALU.max, ALU.add), x["t"][r])
                if x["first"]:
                    for r in range(2):
                        d = aa[r][:, w - 128:w]
                        t[r] = op("dve", lambda e, d=d: e.tensor_tensor(d, d, sbmul, ALU.mult), t[r])
                for r in range(2):
                    cs[r] = cslot.take()
                    cc[r] = cs[r].ap[:, 0:w]
                    first = g["carry"][r] is None
                    init, wt = (0.0, []) if first else (g["carry"][r][0], [g["carry"][r][1]])
                    t[r] = op("dve", lambda e, a=aa[r], o=cc[r], init=init: e.tensor_tensor_scan(
                        o[:, ::-1], ONE.broadcast_to([128, w]), a[:, ::-1], init, ALU.mult, ALU.add), t[r], wt, cs[r].free, t_one)
                    g["carry"][r] = (cc[r][:, 0:1], t[r])
                for r in range(2):
                    b = x["b"][r]
                    t[r] = op("dve", lambda e, a=aa[r], b=b, c=cc[r]: e.tensor_tensor(a, b.ap[:, 0:w], c, ALU.subtract), t[r])
                    b.free = [t[r]]
                    cs[r].free = [t[r]]
                if x["first"]:
                    for r in range(2):
                        d = aa[r][:, w - 128:w]
                        t[r] = op("dve", lambda e, d=d: e.tensor_tensor(d, d, sbmin, ALU.min), t[r])
                x["t"] = t

            def sb_c(x):
                for r in range(2):
                    a = x["a"][r].ap[:, 0:x["w"]]
                    x["t"][r] = op("act", lambda e, a=a: e.activation(a, a, ACT.Exp), x["t"][r])

            def sb_t(x):
                x["s"] = []
                for r in range(2):
                    s, ts, t_pe = turn(x["a"][r].ap[:, 0:x["w"]], x["w"], [x["t"][r]], "dve")
                    x["a"][r].free = [t_pe]
                    x["s"].append((s, ts))

            def sb_d(x):
                g = x["g"]
                hd = heads[g["j"]]
                o = bank[7]
                for r in range(2):
                    s, ts = x["s"][r]
                    view = Slot(o.ap[:, 128 * r:128 * r + 128])
                    view.free = o.free
                    t = pv(hd, s, ts, x["c"], x["w"], view, 64 * r, 64, x["first"], x["last"], clear=r == 0)
                hd[3].free = [t]
                if x["last"]:
                    O = ob[g["j"] % 2]
                    dst = O.ap[:, 128 * g["qt"]:128 * g["qt"] + 128].rearrange("p (r e) -> p r e", r=2)
                    ov = o.ap[:, 0:256].rearrange("p (r a e) -> p r a e", r=2, a=2)
                    y = op("dve", lambda e: e.tensor_copy(dst, ov[:, :, 0, :]), t, O.free)
                    y = op("dve", lambda e: e.tensor_tensor(dst, ov[:, :, 1, :], dst, ALU.add), y)
                    o.free = [y]
                    if g["qt"] == 7:
                        finish_tile(g["j"], O, y)

            nwork = len(work)
            for i in range(nwork + 5):
                if 0 <= i - 2 < nwork:
                    sb_c(work[i - 2])
                if i < nwork:
                    sb_a(work[i])
                if 0 <= i - 1 < nwork:
                    sb_b(work[i - 1])
                if 0 <= i - 5 < nwork:
                    sb_d(work[i - 5])
                if 0 <= i - 3 < nwork:
                    sb_t(work[i - 3])

            att_pe = [(esem["pe"], count["done_pe"])]
            st["xs"] = att_pe + all_of([t for s in aslot.slots + cslot.slots for t in s.free] + scr_free)
            xs_free0 = att_pe + all_of([t for s in aslot.slots + cslot.slots for t in s.free])
            st["big_r"] = list(att_pe)
            for s in wslot:
                s.free = list(att_pe)
            for r in raw:
                r.free = all_of([t for v in traw.slots for t in v.free])
            ev_free = ob[0].free + ob[1].free
            for v in ev:
                v.free = list(ev_free)
            pring = Ring(bank)

            ws = Stream(reqs_after(H))
            ws.ahead()
            t_y = []
            for i in range(2):
                rows = slice(8 * H + 4 * i, 8 * H + 4 * i + 4)
                if i == 0:
                    t_ya = dma("sp", s_yf, xs[:, 0:4, 0:896], ys_v[:, rows, 0:896], ystores[:-1], xs_free0)
                    t_y.append(dma("sp", s_y[0], xs[:, 0:4, 896:1024], ys_v[:, rows, 896:1024], ystores, xs_free0))
                else:
                    t_y.append(dma("sp", s_y[1], xs[:, 4:8, :], ys_v[:, rows, :], ystores, st["xs"]))
            yst["r"] = list(t_y) + [t_ya]
            for j in range(2):
                big_r = list(st["big_r"])

                def tr_y(j=j, big_r=big_r):
                    src = {k: [t_ya] for k in range(7)} if j == 0 else {}
                    st["xs_pe"] = transpose4(j, [t_y[j]] * 4, lambda k: PSC[:, k:k + 1] if k < 2 else DGC if k < 6 else SGC,
                                             waits=big_r + [t_dg, consts], by_k=src)
                if j == 0:
                    tr_y()
                else:
                    late.append(tr_y)

            def residual_gemm(nblk, hook):
                for i in range(nblk):
                    slot, t_w = ws.next()
                    ws.ahead()
                    for t in range(8):
                        if t == 4:
                            flush()
                        b = pring.take()
                        t_mm = gemm_t(slot, t, b, t_w + st["big"][t // 4])
                        x = sink(i, t, b, t_mm)
                        if i == nblk - 1:
                            slot.free = [t_mm]
                            hook(t, x, t_mm)
                    slot.free = [t_mm]

            def sink(i, t, b, t_mm):
                dst = xh[:, t, 256 * i:256 * i + 256]
                x = op("dve", lambda e: e.tensor_tensor(dst, b.ap[:, 0:256], dst, ALU.add), t_mm)
                b.free = [x]
                return x

            sq2, mm2 = [], []

            def hook2(t, x, t_mm):
                if t == 0:
                    st["xs"] = [st["xs_pe"]]
                sq2.append(square(xh, t, [x]))
                mm2.append(t_mm)
                if t == 3:
                    sc2.append(scaled4(0, sq2[:4], MIXED))
                if t == 5:
                    st["t0"] = transpose4(0, sc2[0], lambda k: G2C[:, k:k + 1], waits=[mm2[3]])
                if t == 7:
                    sc2.append(scaled4(1, sq2[4:], MIXED))

                    def tr_2():
                        st["xs_pe"] = transpose4(1, sc2[1], lambda k: G2C[:, k:k + 1], waits=[t_mm])
                    late.append(tr_2)
            sc2 = []
            residual_gemm(4, hook2)
            at = AT[:, :].rearrange("p (a f t) -> p a f t", a=2, f=2)
            at_r = all_of(stores + [(esem["pe"], count["done_pe"])])
            sgs = [Slot(XS[:, 512 * i:512 * i + 512]) for i in range(4)]
            for s in sgs:
                s.free = [st["t0"]]
            ACC = XS[:, 2048:5120]
            ada = [Slot(XS[:, 5120:6144]), Slot(XS[:, 6144:7168])]
            t_acc = None
            if H == 0:
                t_sc = op("act", lambda e: e.activation(CC, CC, ACT.Silu), consts)
            acc_t = [None] * 3
            sqa, sqb, scb = {}, {}, {}

            def final_norm4(g):
                t_r = rstd_from(4, 1024, [sqa[t] for t in range(4 * g, 4 * g + 4)], c0=4 * g)
                for t in range(4 * g, 4 * g + 4):
                    x = op("dve", lambda e, t=t: e.scalar_tensor_tensor(xh[:, t, :], xh[:, t, :], RSTD[:, t:t + 1], gf, ALU.mult, ALU.mult),
                           t_r, t_gf, sqa[t])
                    sqb[t] = square(xh, t, [x, sqa[4 * g + 3]] + ([sqb[6]] if t == 7 else []), xs[:, min(t, 6), :])
                st["rstd_r"] = all_of(st["rstd_r"] + [x])
                sqb["x", g] = x

            def pre4(g):
                scb[g] = scaled4(g, [sqb[t] for t in range(4 * g, 4 * g + 4)], MIXED if g else ("act",) * 4, [sqb["x", g]])

            def hook_f(t, x):
                sqa[t] = square(xh, t, [x] + ([sqa[6]] if t == 7 else []), xs[:, min(t, 6), :])
                if t == 3:
                    final_norm4(0)
                if t == 5:
                    pre4(0)
                if t == 6:
                    scb["t0"] = transpose4(0, scb[0], lambda k: GPC[:, k:k + 1], lambda k: SHC[:, k:k + 1], waits=big_u + [t_mod])
                if t == 7:
                    final_norm4(1)
            na = 0
            for kind, g in ffn_order:
                slot, t_w = ws.next()
                ws.ahead()
                if kind in "gu":
                    for j in range(2):
                        for f in range(2):
                            if j and late:
                                flush()
                                st["xs"] = [st["xs_pe"]]
                                ada_free = list(st["xs"])
                                for s in ada:
                                    s.free = list(st["xs"])
                            b = pring.take()
                            t_mm = gemm_f(slot, f, j, b, t_w + st["big"][j])
                            s = sgs[2 * f + j]
                            if kind == "g":
                                s.t = op("act", lambda e, s=s, b=b: e.activation(s.ap, b.ap[:, :], ACT.Silu), t_mm, s.free)
                                b.free = [s.t]
                            else:
                                x = op("dve", lambda e, s=s, b=b: e.tensor_tensor(s.ap, b.ap[:, :], s.ap, ALU.mult), t_mm, s.t)
                                b.free = [x]
                                hi, lo = at[:, 0, f, 512 * j:512 * j + 512], at[:, 1, f, 512 * j:512 * j + 512]
                                t_hi = op("act", lambda e, s=s, hi=hi: e.activation(hi, s.ap, ACT.Copy), x, at_r)
                                t_lo = op("pool", lambda e, s=s, hi=hi, lo=lo: e.tensor_tensor(lo, s.ap, hi.bitcast(F32), ALU.subtract),
                                          t_hi, x, at_r)
                                s.free = [t_hi, t_lo]
                                t_at = [t_hi, t_lo]
                    if H == 0 and kind == "g" and g < 8:
                        for n in range(3):
                            a = ada[na % 2]
                            t_a = dma("sp", s_ada[na % 2], a.ap, I["w_ada_2"][0, 128 * g:128 * g + 128, 1024 * n:1024 * n + 1024], a.free)
                            na += 1
                            acc = ACC[:, 1024 * n:1024 * n + 1024]
                            if g == 0:
                                acc_t[n] = op("dve", lambda e, a=a, acc=acc: e.tensor_scalar(acc, a.ap, CC[:, 0:1], None, ALU.mult),
                                              t_a, t_sc, ada_free)
                            else:
                                acc_t[n] = op("dve", lambda e, a=a, acc=acc, g=g: e.scalar_tensor_tensor(
                                    acc, a.ap, CC[:, g:g + 1], acc, ALU.mult, ALU.add), t_a, acc_t[n])
                            a.free = [acc_t[n]]
                    if H == 0 and kind == "g" and g == 9:
                        b = pring.take()
                        for k in range(16):
                            t_m = op("pe", lambda e, k=k, b=b: e.matmul(b.ap[:, k:k + 1], ACC[:, 128 * k:128 * k + 128], ONE,
                                                                       start=True, stop=True, skip_group_check=True), acc_t, t_one, b.free, inc=k == 15)
                        x = op("dve", lambda e, b=b: e.tensor_copy(MODC, b.ap[:, 0:16]), t_m)
                        b.free = [x]
                        x1 = op("dve", lambda e: e.tensor_tensor(SHC, SHC, MODC[:, 0:8], ALU.add), x, consts)
                        x2 = op("dve", lambda e: e.tensor_tensor(SCC, SCC, MODC[:, 8:16], ALU.add), x)
                        x2 = op("dve", lambda e: e.tensor_scalar_add(SCC, SCC, 1.0), x2)
                        t_mod = op("dve", lambda e: e.tensor_tensor(GPC, GPC, SCC, ALU.mult), x2, x1)
                        rb = XS[:, 5120:6144]
                        rg = XS[:, 6144:7168]
                        t_rb = dma("sp", s_ada[0], rb, I["b_ada_2"][0:1, 2048:3072].broadcast_to([128, 1024]), ada[0].free)
                        t_rg = dma("sp", s_ada[1], rg, I["g_post_2"][0:1, :].broadcast_to([128, 1024]), ada[1].free)
                        ONEM = XS[:, 7168:7296]
                        t_om = op("dve", lambda e: e.memset(ONEM, 1.0), ada_free)
                        for n in range(2):
                            b = pring.take()
                            ns = slice(512 * n, 512 * n + 512)
                            t_m = op("pe", lambda e, n=n, b=b: e.matmul(b.ap[:, :], ONEM, ACC[:, 2048 + 512 * n:2560 + 512 * n],
                                                                       start=True, stop=True), acc_t, t_om, b.free)
                            x = op("dve", lambda e, b=b, ns=ns: e.tensor_tensor(GPROW[:, ns], b.ap[:, :], rb[:, ns], ALU.add), t_m, t_rb)
                            b.free = [x]
                            t_gp = op("dve", lambda e, ns=ns: e.tensor_tensor(GPROW[:, ns], GPROW[:, ns], rg[:, ns], ALU.mult), x, t_rg)
                        st["xs"] = all_of(st["xs"] + [t_gp, t_m])
                else:
                    if g == NG - 1:
                        st["xs"] = all_of(st["xs"] + [t for s in sgs for t in s.free])
                        log_exp_tables()
                        gf = xs[:, 7, :]
                        t_gf = dma("sp", s_m, gf, I["final_norm_g"].rearrange("(a d) -> a d", a=1).broadcast_to([128, 1024]), st["xs"])
                    dh = slot.ap[0].rearrange("p (f n) -> p f n", f=2)
                    dl = slot.ap[1].rearrange("p (f n) -> p f n", f=2)
                    for t in range(8):
                        for n in range(2):
                            b = pring.take()
                            ts, ns = slice(128 * t, 128 * t + 128), slice(512 * n, 512 * n + 512)
                            for f in range(2):
                                t_mm = three(None, b.ap[:, :], at[:, 0, f, ts], at[:, 1, f, ts], dh[:, f, ns], dl[:, f, ns],
                                             f == 0, f == 1, (t_w + t_at + b.free) if f == 0 else [], f == 1)
                            dst = xh[:, t, ns]
                            x = op("dve", lambda e, b=b, dst=dst: e.tensor_tensor(dst, b.ap[:, :], dst, ALU.add), t_mm,
                                   *( [] if g else [st["xs"]]))
                            b.free = [x]
                        if g == NG - 1:
                            hook_f(t, x)
                    at_r = [t_mm]
                slot.free = [t_mm]
                if kind == "u":
                    big_u = [t_mm]
            t0 = scb["t0"]
            pre4(1)

            def tr_3():
                t1 = transpose4(1, scb[1], lambda k: GPC[:, k:k + 1], lambda k: SHC[:, k:k + 1], waits=big_u + [t_mod])
                st["xs_pe"] = t1
                for s in pb.slots[2:]:
                    s.free = [t1]
            late.append(tr_3)

            r2w = all_of(at_r + [(esem["pe"], count["done_pe"])])
            cos = R2[:, 0:512].rearrange("p (t i) -> p t i", t=8)
            sin = R2[:, 512:1024].rearrange("p (t i) -> p t i", t=8)
            rmk = R2[:, 1024:1536]
            qdc = R2[:, 1536:2048]
            tmpa = R2[:, 2048:2560]
            tmpb = R2[:, 2560:3072]
            YB = R2[:, 3072:4096]
            t_r2 = dma("sp", s_r2, rmk, const[:, C_RMASK:C_RMASK + 512], r2w)
            t_r2 = dma("sp", s_r2, qdc, const[:, C_QDEC:C_QDEC + 512], r2w)
            invf = tmpb[:, 0:64]
            t_r2 = dma("sp", s_r2, invf, const[:, C_INVF:C_INVF + 64], r2w)
            posi = tmpb[:, 64:72].bitcast(I32)
            t_r2 = dma("sp", s_r2, posi, I["positions_2"][0, tok0:tok0 + HT].rearrange("(t p) -> p t", p=128), r2w, slow=True)
            rt = {}

            def angles():
                x = op("dve", lambda e: e.tensor_copy(POSF, posi), t_r2)
                for t in range(8):
                    x = op("dve", lambda e, t=t: e.tensor_scalar(cos[:, t, :], invf, POSF[:, t:t + 1], None, ALU.mult), x, r2w)
                cf, sf = R2[:, 0:512], R2[:, 512:1024]
                magic = 12582912.0
                x = op("dve", lambda e: e.tensor_scalar(sf, cf, 1.0 / (2 * math.pi), magic, ALU.mult, ALU.add), x)
                x = op("dve", lambda e: e.tensor_scalar_add(sf, sf, -magic), x)
                for part in two_pi_parts():
                    x = op("dve", lambda e, part=part: e.scalar_tensor_tensor(cf, sf, -part, cf, ALU.mult, ALU.add), x)
                lim = float(np.nextafter(np.float32(math.pi), np.float32(0)))
                x = op("dve", lambda e: e.tensor_scalar(cf, cf, lim, -lim, ALU.min, ALU.max), x)
                rt["x"] = x

            def rotary_tables():
                cf, sf = R2[:, 0:512], R2[:, 512:1024]
                x = rt["x"]
                y = op("act", lambda e: e.activation(sf, cf, ACT.Sin), x)
                y = op("act", lambda e: e.activation(cf, cf, ACT.Sin, scale=0.5), y)
                y = op("dve", lambda e: e.tensor_tensor(cf, cf, cf, ALU.mult), y)
                t_cs = op("dve", lambda e: e.tensor_scalar(cf, cf, -2.0, 1.0, ALU.mult, ALU.add), y)
                t_tmp[:] = [t_cs]

            pb = Ring([Slot(XS[:, 2048 * i:2048 * i + 2048]) for i in range(4)])
            for s in pb.slots:
                s.free = [t0]
            small = Ring([Slot(EV[:, 128 * i:128 * i + 128]) for i in range(16)])
            evf = all_of([t for v in ev for t in v.free])
            for s in small.slots:
                s.free = list(evf)
            pring = Ring(bank[0:4])
            mring = Ring(bank[4:8])
            ylast = {}
            yb = Slot(YB)
            yb.free = list(r2w)
            ystores = []
            grs = [Slot(GROW[:, 128 * i:128 * i + 128]) for i in range(2)]
            t_tmp = []
            nun = 0

            def store_y(c0, t_y):
                d = dma("pool", s_yu[0], ys_v[:, 8 * H:8 * H + 8, c0:c0 + 128], yb.ap.rearrange("p (t e) -> p t e", t=8), t_y, yst["r"])
                yb.free = [d]
                ystores.append(d)

            def layer_norm8(src, t_src, en=128):
                ts = []
                for c in range(8):
                    y = op("dve", lambda e, c=c: e.bn_stats(BN[:, 6 * c:6 * c + 6], src(c)), t_src, st["rstd_r"])
                    ts.append(y)
                for c in range(8):
                    y = op("dve", lambda e, c=c: e.bn_aggr(MV[:, 2 * c:2 * c + 2], BN[:, 6 * c:6 * c + 6]), ts[c], st["rstd_r"])
                mv = MV.rearrange("p (c a) -> p c a", a=2)
                return rstd_from(8, 1.0, [y], src=mv[:, :, 1], tables=True)

            def load_row(src, n):
                g = grs[n % 2]
                t = dma("sp", s_gr[n % 2], g.ap, src.broadcast_to([128, 128]), g.free)
                return g, t

            def gmlp_steps(p, bufs, toks, n0):
                steps = []
                Gb = bufs[2].ap.rearrange("p (t n) -> p t n", t=8)
                for gi in range(2):
                    g = 2 * p + gi
                    B = bufs[gi].ap.rearrange("p (t n) -> p t n", t=8)
                    loc = {}

                    def s_norm(g=g, B=B, loc=loc, n=n0 + gi, gi=gi):
                        wt = small.take()
                        t_w = dma("sp", s_gw[g], wt.ap, I["gmlp_ws_2"][0, g, :, :], wt.free)
                        wt2 = small.take()
                        b = mring.take()
                        t = op("pe", lambda e: e.transpose(b.ap[:, 0:128], wt.ap, ident), t_w, b.free)
                        t = op("dve", lambda e: e.tensor_tensor(wt2.ap, b.ap[:, 0:128], caus, ALU.mult), t, wt2.free)
                        b.free = [t]
                        wt.free = [t]
                        loc["w"], loc["tw"] = wt2, t
                        row, t_row = load_row(I["gmlp_ln_g_2"][0:1, 128 * g:128 * g + 128], n)
                        t_r = layer_norm8(lambda c: B[:, c, 128:256], toks[gi] + toks[2])
                        for c in range(8):
                            t = op("dve", lambda e, c=c: e.tensor_scalar(B[:, c, 128:256], B[:, c, 128:256], MV[:, 2 * c:2 * c + 1],
                                                                          RSTD[:, c:c + 1], ALU.subtract, ALU.mult), t_r)
                            t = op("dve", lambda e, c=c: e.tensor_tensor(B[:, c, 128:256], B[:, c, 128:256], row.ap, ALU.mult), t, t_row)
                        row.free = [t]
                        st["rstd_r"] = [t]
                        loc["v"] = t
                        gs = Gb[:, :, 128 * gi:128 * gi + 128]
                        loc["g"] = op("act", lambda e: e.activation(gs, gs, ACT.Silu), toks[2])

                    def s_mix(q, g=g, B=B, loc=loc, gi=gi):
                        b = mring.take()
                        w = loc["w"]
                        t = op("pe", lambda e: e.matmul(b.ap[:, :].rearrange("p (t n) -> p t n", t=4), w.ap,
                                                        B[:, 4 * q:4 * q + 4, 128:256], start=True, stop=True),
                               loc["tw"], loc["v"], b.free)
                        us = B[:, 4 * q:4 * q + 4, 0:128]
                        t = op("dve", lambda e: e.scalar_tensor_tensor(us, b.ap[:, :].rearrange("p (t n) -> p t n", t=4),
                                                                       BSC[:, g:g + 1], us, ALU.add, ALU.mult), t)
                        b.free = [t]
                        dst = yb.ap.rearrange("p (t e) -> p t e", t=8)[:, 4 * q:4 * q + 4, :]
                        loc["y"] = op("dve", lambda e: e.tensor_tensor(dst, us, Gb[:, 4 * q:4 * q + 4, 128 * gi:128 * gi + 128],
                                                                       ALU.mult), t, loc["g"], yb.free)
                        if q == 1:
                            loc["w"].free = [loc["y"]]
                            store_y(128 * g, loc["y"])
                            bufs[gi].free = [loc["y"]]
                            if gi == 1:
                                bufs[2].free = [loc["y"]]
                    steps += [s_norm, lambda f=s_mix: f(0), lambda f=s_mix: f(1)]
                return steps

            def ret_steps(h, bufs, toks, n0):
                A = bufs[0].ap.rearrange("p (t n) -> p t n", t=8)
                B = bufs[1].ap.rearrange("p (t n) -> p t n", t=8)
                ta = tmpa.rearrange("p (t i) -> p t i", t=8)
                tb = tmpb.rearrange("p (t i) -> p t i", t=8)
                loc = {}
                cd = (1.0 - 2.0 ** (-5.0 - h)) ** 128
                S_ = ST[:, 128 * h:128 * h + 128]
                ctx_ = [dict() for _ in range(8)]

                def rot():
                    for half in range(2):
                        x1 = A[:, :, 128 * half:128 * half + 64]
                        x2 = A[:, :, 128 * half + 64:128 * half + 128]
                        t1 = op("dve", lambda e, x1=x1: e.tensor_tensor(ta, x1, sin, ALU.mult), toks[0] + t_tmp)
                        t2 = op("dve", lambda e, x2=x2: e.tensor_tensor(tb, x2, sin, ALU.mult), t_tmp)
                        t3 = op("dve", lambda e, x1=x1: e.tensor_tensor(x1, x1, cos, ALU.mult), t1)
                        t4 = op("dve", lambda e, x2=x2: e.tensor_tensor(x2, x2, cos, ALU.mult), t2)
                        t5 = op("dve", lambda e, x1=x1: e.tensor_tensor(x1, x1, tb, ALU.subtract), t3)
                        t6 = op("dve", lambda e, x2=x2: e.tensor_tensor(x2, x2, ta, ALU.add), t4)
                        t_tmp[:] = [t6]
                        loc[half] = [t5, t6]
                    loc["rot"] = [t6]
                    if H == 0:
                        state_tok[h] = [op("dve", lambda e: e.memset(S_, 0.0))]
                    loc["g"] = op("act", lambda e: e.activation(B[:, :, 128:256], B[:, :, 128:256], ACT.Silu), toks[1])

                def s_a(c):
                    x = ctx_[c]
                    b = mring.take()
                    op("pe", lambda e: e.transpose(b.ap[:, 0:128], A[:, c, 0:128], ident), loc["rot"], b.free, inc=False)
                    t = op("pe", lambda e: e.transpose(b.ap[:, 128:256], A[:, c, 128:256], ident))
                    x["qT"], x["kT"], x["qd"], x["kd"] = [small.take() for _ in range(4)]
                    t1 = op("act", lambda e: e.activation(x["qT"].ap, b.ap[:, 0:128], ACT.Copy), t, x["qT"].free)
                    t2 = op("act", lambda e: e.activation(x["kT"].ap, b.ap[:, 128:256], ACT.Copy), t1, x["kT"].free)
                    t3 = op("pool", lambda e: e.tensor_tensor(x["qd"].ap, x["qT"].ap, qdc[:, 128 * h:128 * h + 128], ALU.mult),
                            t1, x["qd"].free, t_r2)
                    t4 = op("pool", lambda e: e.tensor_scalar(x["kd"].ap, A[:, c, 128:256], KDC[:, h:h + 1], None, ALU.mult),
                            loc["rot"], x["kd"].free, consts)
                    b.free = [t2]
                    x["ta"] = [t2, t4]

                def s_b(c):
                    x = ctx_[c]
                    b = mring.take()
                    op("pe", lambda e: e.matmul(b.ap[:, 0:128], x["kT"].ap, x["qT"].ap, start=True, stop=True), x["ta"], b.free, inc=False)
                    t = op("pe", lambda e: e.matmul(b.ap[:, 128:256], x["kd"].ap, B[:, c, 0:128], start=True, stop=True), toks[1])
                    x["kT"].free = [t]
                    x["kd"].free = [t]
                    x["sm"] = small.take()
                    x["tb"] = op("dve", lambda e: e.tensor_tensor(x["sm"].ap, b.ap[:, 0:128], rmk[:, 128 * h:128 * h + 128], ALU.mult),
                                 t, x["sm"].free, t_r2)
                    x["bank"] = b

                def s_c(c):
                    x = ctx_[c]
                    b = mring.take()
                    op("pe", lambda e: e.matmul(b.ap[:, 0:128], x["sm"].ap, B[:, c, 0:128], start=True, stop=False), x["tb"], b.free, inc=False)
                    t = op("pe", lambda e: e.matmul(b.ap[:, 0:128], x["qd"].ap, S_, start=False, stop=True), state_tok[h])
                    x["sm"].free = [t]
                    x["qd"].free = [t]
                    x["qT"].free = [t]
                    kvb = x["bank"]
                    t2 = op("dve", lambda e: e.scalar_tensor_tensor(S_, S_, cd, kvb.ap[:, 128:256], ALU.mult, ALU.add), t, x["tb"])
                    kvb.free = [t2]
                    state_tok[h] = [t2]
                    t3 = op("dve", lambda e: e.tensor_copy(A[:, c, 0:128], b.ap[:, 0:128]), t)
                    b.free = [t3]
                    loc["o"] = t3

                def fin():
                    row, t_row = load_row(I["ret_gn_g_2"][0:1, 128 * h:128 * h + 128], n0)
                    t_r = layer_norm8(lambda c: A[:, c, 0:128], [loc["o"]])
                    y8 = yb.ap.rearrange("p (t e) -> p t e", t=8)
                    for c in range(8):
                        t = op("dve", lambda e, c=c: e.tensor_scalar(A[:, c, 0:128], A[:, c, 0:128], MV[:, 2 * c:2 * c + 1],
                                                                      RSTD[:, c:c + 1], ALU.subtract, ALU.mult), t_r)
                        t = op("dve", lambda e, c=c: e.tensor_tensor(A[:, c, 0:128], A[:, c, 0:128], row.ap, ALU.mult), t, t_row)
                    row.free = [t]
                    st["rstd_r"] = [t]
                    t = op("dve", lambda e: e.tensor_tensor(y8, A[:, :, 0:128], B[:, :, 128:256], ALU.mult), t, loc["g"], yb.free)
                    if h == 3:
                        ylast["t"] = t
                    else:
                        store_y(512 + 128 * h, t)
                    bufs[0].free = [t]
                    bufs[1].free = [t]

                steps = [rot]
                for i in range(10):
                    def one(i=i):
                        if i < 8:
                            s_a(i)
                        if 0 <= i - 1 < 8:
                            s_b(i - 1)
                        if 0 <= i - 2 < 8:
                            s_c(i - 2)
                    steps.append(one)
                return steps + [fin]

            pending = []
            for kind, idx, req in units:
                bufs, toks = [], []
                total = 8 * len(req)
                done = 0
                nsteps = len(pending)
                for _ in req:
                    slot, t_w = ws.next()
                    ws.ahead()
                    buf = None
                    for t in range(8):
                        if t == 4:
                            flush()
                        b = pring.take()
                        t_mm = gemm_t(slot, t, b, t_w + st["big"][t // 4])
                        if buf is None:
                            buf = pb.take()
                            while not isinstance(buf.free, list):
                                pending.pop(0)()
                        dst = buf.ap.rearrange("p (t n) -> p t n", t=8)[:, t, :]
                        x = op("act", lambda e, b=b, dst=dst: e.activation(dst, b.ap[:, 0:256], ACT.Copy), t_mm, buf.free)
                        b.free = [x]
                        done += 1
                        want = nsteps * done // total
                        while nsteps - len(pending) < want:
                            pending.pop(0)()
                        if not nun and done == 5:
                            angles()
                        if not nun and done == 16:
                            rotary_tables()
                    slot.free = [t_mm]
                    buf.free = None
                    bufs.append(buf)
                    toks.append([x])
                while pending:
                    pending.pop(0)()
                pending = gmlp_steps(idx, bufs, toks, nun) if kind == "g" else ret_steps(idx, bufs, toks, nun)
                nun += 2 if kind == "g" else 1
            st["big_r"] = [t_mm]
            yfr = all_of(pb.slots[2].free + pb.slots[3].free)

            def load_y(i, w):
                return dma("sp", s_y[i], xs[:, 4:8, 0:896], ys_v[:, 8 * H + 4 * i:8 * H + 4 * i + 4, 0:896], ystores, w)

            def transposed_y(i, k, src, w):
                b = pring.take()
                for t in range(4):
                    t_pe = op("pe", lambda e, t=t: e.transpose(b.ap[:, 128 * t:128 * t + 128], src(t), ident), w, b.free, inc=t == 3)
                hi, lo = bigh[:, k, 512 * i:512 * i + 512], bigl[:, k, 512 * i:512 * i + 512]
                t_hi = op("act", lambda e: e.activation(hi, b.ap[:, :], ACT.Copy), t_pe, st["big_r"])
                t_lo = op("dve", lambda e: e.tensor_tensor(lo, b.ap[:, :], hi.bitcast(F32), ALU.subtract), t_hi, t_pe, st["big_r"])
                b.free = [t_hi, t_lo]
                st["big"][i] = [t_hi, t_lo]
                return t_pe

            yl = [load_y(0, yfr)]
            npend = len(pending)
            todo = [(i, k) for i in range(2) for k in range(7)]
            while pending:
                pending.pop(0)()
                step = npend - len(pending)
                for _ in range(2 if step >= 3 else 0):
                    if todo and (todo[0][0] == 0 or step >= 8):
                        i, k = todo.pop(0)
                        t_pe = transposed_y(i, k, lambda t, k=k: xs[:, 4 + t, 128 * k:128 * k + 128], yl[i])
                        if (i, k) == (0, 6):
                            yl.append(load_y(1, [t_pe]))
            while todo:
                i, k = todo.pop(0)
                t_pe = transposed_y(i, k, lambda t, k=k: xs[:, 4 + t, 128 * k:128 * k + 128], yl[i])
            yst["r"] = list(yl)
            y8 = yb.ap.rearrange("p (t e) -> p t e", t=8)
            for i in range(2):
                yb.free = [transposed_y(i, 7, lambda t, i=i: y8[:, 4 * i + t, :], [ylast["t"]])]
            t_xsw = [t_pe, ylast["t"]]
            for v in ev:
                v.free = all_of([t for s in small.slots for t in s.free])
            pring = Ring(bank)
            log_exp_tables()
            sq4, outs_g, xload = {}, {}, []

            def sink(i, t, b, t_mm):
                dst = xs[:, t, 256 * i:256 * i + 256]
                x = op("act", lambda e: e.activation(dst, b.ap[:, 0:256], ACT.Copy), t_mm, t_xsw)
                b.free = [x]
                return x
            junk = R2[:, 2048:3072]
            last_sq = []

            def finish4(g):
                t_r = rstd_from(4, 1024, [sq4[t] for t in range(4 * g, 4 * g + 4)], c0=4 * g)
                for t in range(4 * g, 4 * g + 4):
                    x = op("dve", lambda e, t=t: e.scalar_tensor_tensor(xs[:, t, :], xs[:, t, :], RSTD[:, t:t + 1], GPROW[:, :],
                                                                        ALU.mult, ALU.mult), t_r, t_gp, sq4[t])
                    y = op("pool", lambda e, t=t: e.tensor_tensor(xs[:, t, :], xs[:, t, :], xh[:, t, :], ALU.add), x)
                    outs_g[g] = [dma("sp", s_out[g], o_v[:, 8 * H + t, :], xs[:, t, :], y)]
                    if H == 0:
                        xload.append(load_x(1, t, [y]))
                st["rstd_r"] = all_of(st["rstd_r"] + [x])

            def hook4(t, x, t_mm):
                sq4[t] = op("act", lambda e: e.activation(junk, xs[:, t, :], ACT.Square, accum_out=SS[:, t:t + 1]),
                            x, st["rstd_r"], t_tmp, last_sq)
                last_sq[:] = [sq4[t]]
                st["big_r"] = [t_mm]
                if t == 4:
                    finish4(0)
                if t == 7:
                    finish4(1)
            residual_gemm(4, hook4)
            st["xs"] = []
            t_ss = last_sq
            at_free["t"] = all_of([yb.free[0], t_ss[-1], (esem["pe"], count["done_pe"]), (esem["dve"], count["done_dve"]),
                                   (esem["pool"], count["done_pool"]), (esem["act"], count["done_act"])])

        ends = [(s, count[s[0]]) for s in s_st + s_ev + s_o + s_yu + [s_us] + s_out if count[s[0]]]

        block = ctx.enter_context(nc.Block())

        def play(e, name):
            seen = {}
            for waits, f, inc in queues[name]:
                for w in waits:
                    if w is None:
                        continue
                    s, v = w
                    if seen.get(s[0], 0) < v:
                        e.wait_ge(s[1], v)
                        seen[s[0]] = v
                r = f(e)
                if inc:
                    r.then_inc(*inc)

        @block.tensor
        def _(e):
            play(e, "pe")

        @block.scalar
        def _(e):
            play(e, "act")

        @block.vector
        def _(e):
            play(e, "dve")

        @block.gpsimd
        def _(e):
            play(e, "pool")

        @block.sync
        def _(e):
            play(e, "sp")
            for s, v in ends:
                e.wait_ge(s[1], v)


_INS = ["x", "norm1_g", "w_in", "pool_w", "pool_scale", "lam_q1", "lam_k1", "lam_q2", "lam_k2", "diff_norm_g",
        "sb_norm_g", "w_out", "norm2_g", "w_gate", "w_up", "w_down", "final_norm_g", "c_2", "positions_2", "w_ada_2",
        "b_ada_2", "g_pre_2", "w_in_2", "gmlp_ln_g_2", "gmlp_ws_2", "gmlp_bs_2", "ret_gn_g_2", "w_out_2", "g_post_2"]


def kernel(**inputs):
    import concourse.bacc as bacc
    from concourse.bass_utils import run_bass_kernel_spmd

    nc = bacc.Bacc("TRN2", target_bir_lowering=False, num_devices=1)
    arrays, aps = {}, {}
    for name in _INS:
        a = np.ascontiguousarray(inputs[name])
        arrays[f"in_{name}"] = a
        aps[name] = nc.dram_tensor(f"in_{name}", a.shape, mybir.dt.from_np(a.dtype), kind="ExternalInput").ap()
    arrays["shape_constants"] = shape_constants()
    const = nc.dram_tensor("shape_constants", [128, C_END], F32, kind="ExternalInput").ap()
    out = nc.dram_tensor("out_0", [1, S, D], F32, kind="ExternalOutput").ap()
    scr = {}
    for name, shape in (("QS", [2, 6, 128, S]), ("KS", [2, 6, 128, S]), ("VS", [2, 6, S, 128]),
                        ("US", [2, 128, S + 16]), ("YS", [S, D])):
        scr[name] = nc.dram_tensor("scratch_" + name, shape, F32, kind="Internal").ap()
    build(nc, aps, const, out, scr)
    r = run_bass_kernel_spmd(nc, [arrays], core_ids=[0])
    return r.results[0]["out_0"]
```
